# Optimizing a Trainium2 kernel written in Bass

```python
import math, functools
import jax, jax.numpy as jnp
from jax import lax
import numpy as np

D_MODEL = 1024
BATCH = 1
SEQ = 1024
DEPTH = 1
DEC_BATCH = 8
DEC_SEQ = 4
PAST_LEN = 4096
PAGE_SIZE = 128

A_HEADS = 8
A_KDIM = 128
A_VDIM = D_MODEL // A_HEADS
A_KW = A_HEADS * A_KDIM
A_VW = A_HEADS * A_VDIM
A_CHUNK = 64
B_QHEADS = 16
B_KVHEADS = 2
B_HDIM = 64
B_GROUP = B_QHEADS // B_KVHEADS
B_QW = B_QHEADS * B_HDIM
B_KVW = B_KVHEADS * B_HDIM
WINDOW = 128
EPS = 1e-6
NEG = -1e30
SPLITS = (A_KW, A_KW, A_VW, A_VW, B_QW, B_KVW, B_KVW, B_QW, D_MODEL, D_MODEL)
IN_COLS = A_KW + A_KW + A_VW + A_VW + B_QW + B_KVW + B_KVW + B_QW + D_MODEL + D_MODEL

kernel_name = "hgrn2_swa_sink_gated_hybrid_step"

def rmsnorm(x, g):
    xf = x.astype(jnp.float32)
    y = xf * lax.rsqrt(jnp.mean(xf * xf, axis=-1, keepdims=True) + EPS)
    return (y * g.astype(jnp.float32)).astype(x.dtype)

def alibi_slopes(n):
    return 2.0 ** (-8.0 * jnp.arange(1, n + 1, dtype=jnp.float32) / n)

def in_projection(xn, w_in):
    h = jnp.einsum('btd,dc->btc', xn, w_in)
    offs = [int(o) for o in np.cumsum(SPLITS)[:-1]]
    return jnp.split(h, offs, axis=-1)

def hgrn2_features(qa, fa, ia, lb):
    B, T, _ = qa.shape
    q = jax.nn.silu(qa.astype(jnp.float32))
    sig = jax.nn.sigmoid(fa.astype(jnp.float32))
    lbf = lb.astype(jnp.float32)
    f = lbf + (1.0 - lbf) * sig
    k = (1.0 - lbf) * (1.0 - sig)
    logf = jnp.log(f)
    shp = (B, T, A_HEADS, A_KDIM)
    v = ia.astype(jnp.float32).reshape(B, T, A_HEADS, A_VDIM)
    return q.reshape(shp), k.reshape(shp), v, logf.reshape(shp)

def hgrn2_chunk(S, q, k, v, logf):
    C = q.shape[1]
    b = jnp.cumsum(logf, axis=1)
    causal = jnp.tril(jnp.ones((C, C), dtype=bool))[None, :, :, None, None]
    diff = b[:, :, None] - b[:, None, :]
    decay = jnp.where(causal, jnp.exp(jnp.where(causal, diff, 0.0)), 0.0)
    att = jnp.einsum('bthk,bshk,btshk->bhts', q, k, decay)
    o = jnp.einsum('bhts,bshv->bthv', att, v) + jnp.einsum('bthk,bhkv->bthv', q * jnp.exp(b), S)
    b_last = b[:, -1]
    k_dec = k * jnp.exp(b_last[:, None] - b)
    S_new = jnp.exp(b_last)[..., None] * S + jnp.einsum('bshk,bshv->bhkv', k_dec, v)
    return S_new, o

def hgrn2_prompt(q, k, v, logf):
    B, T = q.shape[:2]
    n_chunks = T // A_CHUNK

    def to_chunks(a):
        return a.reshape((B, n_chunks, A_CHUNK) + a.shape[2:]).swapaxes(0, 1)

    S0 = jnp.zeros((B, A_HEADS, A_KDIM, A_VDIM), jnp.float32)
    S_fin, o = lax.scan(lambda S, inp: hgrn2_chunk(S, *inp), S0,
                        (to_chunks(q), to_chunks(k), to_chunks(v), to_chunks(logf)))
    o = o.swapaxes(0, 1).reshape(B, T, A_HEADS, A_VDIM)
    return o, S_fin

def hgrn2_sample(q, k, v, logf, S):
    S_new, o = hgrn2_chunk(S.astype(jnp.float32), q, k, v, logf)
    return o, S_new

def sink_softmax(s, sinks):
    sk = jnp.broadcast_to(sinks.astype(jnp.float32).reshape(B_KVHEADS, B_GROUP, 1, 1), s.shape[:-1] + (1,))
    return jax.nn.softmax(jnp.concatenate([s, sk], axis=-1), axis=-1)[..., :-1]

def swa_prompt(q, k, v, sinks):
    B, T, _ = q.shape
    nb = T // WINDOW
    scale = 1.0 / math.sqrt(B_HDIM)
    qb = q.reshape(B, nb, WINDOW, B_KVHEADS, B_GROUP, B_HDIM)
    kb = k.reshape(B, nb, WINDOW, B_KVHEADS, B_HDIM)
    vb = v.reshape(B, nb, WINDOW, B_KVHEADS, B_HDIM)

    def prev(a):
        return jnp.concatenate([jnp.zeros_like(a[:, :1]), a[:, :-1]], axis=1)

    kk = jnp.concatenate([prev(kb), kb], axis=2)
    vv = jnp.concatenate([prev(vb), vb], axis=2)
    qi = jnp.arange(WINDOW)[:, None]
    kj = jnp.arange(2 * WINDOW)[None, :] - WINDOW
    dist = (qi - kj).astype(jnp.float32)
    band = ((qi - kj) >= 0) & ((qi - kj) < WINDOW)
    valid = band[None] & ((jnp.arange(nb)[:, None, None] > 0) | (kj >= 0)[None])
    s = jnp.einsum('bnqhgd,bnshd->bnhgqs', qb, kk).astype(jnp.float32) * scale
    s = s - alibi_slopes(B_QHEADS).reshape(B_KVHEADS, B_GROUP, 1, 1) * dist
    s = jnp.where(valid[None, :, None, None], s, NEG)
    p = sink_softmax(s, sinks)
    o = jnp.einsum('bnhgqs,bnshd->bnqhgd', p, vv.astype(jnp.float32)).reshape(B, T, B_QW)
    L = min(WINDOW, T)
    ck = k[:, T - L:].reshape(B, L, B_KVHEADS, B_HDIM)
    cv = v[:, T - L:].reshape(B, L, B_KVHEADS, B_HDIM)
    return o, ck, cv

def swa_sample(q, k, v, sinks, ck, cv):
    DB, T, _ = q.shape
    L = ck.shape[1]
    scale = 1.0 / math.sqrt(B_HDIM)
    qr = q.reshape(DB, T, B_KVHEADS, B_GROUP, B_HDIM)
    kk = jnp.concatenate([ck.astype(k.dtype), k.reshape(DB, T, B_KVHEADS, B_HDIM)], axis=1)
    vv = jnp.concatenate([cv.astype(v.dtype), v.reshape(DB, T, B_KVHEADS, B_HDIM)], axis=1)
    qpos = jnp.arange(T)[:, None]
    kpos = jnp.concatenate([jnp.arange(L) - L, jnp.arange(T)])[None, :]
    d = qpos - kpos
    valid = (d >= 0) & (d < WINDOW)
    s = jnp.einsum('bqhgd,bshd->bhgqs', qr, kk).astype(jnp.float32) * scale
    s = s - alibi_slopes(B_QHEADS).reshape(B_KVHEADS, B_GROUP, 1, 1) * d.astype(jnp.float32)
    s = jnp.where(valid, s, NEG)
    p = sink_softmax(s, sinks)
    o = jnp.einsum('bhgqs,bshd->bqhgd', p, vv.astype(jnp.float32)).reshape(DB, T, B_QW)
    return o, kk[:, -L:], vv[:, -L:]

def decoder_layer(x, hgrn_fn, swa_fn, norm_in, w_in, lb, a_gnorm, b_sinks, w_pa, w_pb, w_out):
    xn = rmsnorm(x, norm_in)
    qa, fa, ia, za, qb, kb, vb, zb, ga, gb = in_projection(xn, w_in)
    q, k, v, logf = hgrn2_features(qa, fa, ia, lb)
    oa, S_new = hgrn_fn(q, k, v, logf)
    oa = oa * lax.rsqrt(jnp.mean(oa * oa, axis=-1, keepdims=True) + EPS) * a_gnorm.astype(jnp.float32)
    B, T = x.shape[:2]
    ha = oa.reshape(B, T, A_VW) * jax.nn.silu(za.astype(jnp.float32))
    ob, ck, cv = swa_fn(qb, kb, vb, b_sinks)
    hb = ob * jax.nn.silu(zb.astype(jnp.float32))
    pa = jnp.einsum('btc,cd->btd', ha.astype(x.dtype), w_pa)
    pb = jnp.einsum('btc,cd->btd', hb.astype(x.dtype), w_pb)
    merged = jax.nn.sigmoid(ga.astype(jnp.float32)) * pa + jax.nn.sigmoid(gb.astype(jnp.float32)) * pb
    y = x + jnp.einsum('btd,de->bte', merged.astype(x.dtype), w_out)
    return y.astype(x.dtype), S_new, ck, cv

def setup_inputs(seed: int = 0) -> dict:
    key = jax.random.key(seed)
    ks = jax.random.split(key, 16)
    L = min(WINDOW, PAST_LEN)
    f32 = jnp.float32
    return {
        "x_prompt": jax.random.normal(ks[0], (BATCH, SEQ, D_MODEL), f32),
        "x_sample": jax.random.normal(ks[1], (DEC_BATCH, DEC_SEQ, D_MODEL), f32),
        "state_hgrn": 0.5 * jax.random.normal(ks[2], (DEPTH, DEC_BATCH, A_HEADS, A_KDIM, A_VDIM), f32),
        "cache_k": jax.random.normal(ks[3], (DEPTH, DEC_BATCH, L, B_KVHEADS, B_HDIM), f32),
        "cache_v": jax.random.normal(ks[4], (DEPTH, DEC_BATCH, L, B_KVHEADS, B_HDIM), f32),
        "norm_in": 1.0 + 0.02 * jax.random.normal(ks[5], (DEPTH, D_MODEL), f32),
        "w_in": jax.random.normal(ks[6], (DEPTH, D_MODEL, IN_COLS), f32) * D_MODEL ** -0.5,
        "lb_logits": 0.5 * jax.random.normal(ks[7], (DEPTH + 1, A_KW), f32),
        "a_gnorm": 1.0 + 0.02 * jax.random.normal(ks[8], (DEPTH, A_VDIM), f32),
        "b_sinks": 0.5 * jax.random.normal(ks[9], (DEPTH, B_QHEADS), f32),
        "w_pa": jax.random.normal(ks[10], (DEPTH, A_VW, D_MODEL), f32) * A_VW ** -0.5,
        "w_pb": jax.random.normal(ks[11], (DEPTH, B_QW, D_MODEL), f32) * B_QW ** -0.5,
        "w_out": jax.random.normal(ks[12], (DEPTH, D_MODEL, D_MODEL), f32) * D_MODEL ** -0.5,
        "norm_final": 1.0 + 0.02 * jax.random.normal(ks[13], (D_MODEL,), f32),
    }

def reference(x_prompt, x_sample, state_hgrn, cache_k, cache_v, norm_in, w_in, lb_logits, a_gnorm,
              b_sinks, w_pa, w_pb, w_out, norm_final):
    lbs = jnp.cumsum(jax.nn.softmax(lb_logits.astype(jnp.float32), axis=0), axis=0)
    hp, hs = x_prompt, x_sample
    sp, kp, vp, ss, ksm, vsm = [], [], [], [], [], []
    for l in range(DEPTH):
        w = (norm_in[l], w_in[l], lbs[l], a_gnorm[l], b_sinks[l], w_pa[l], w_pb[l], w_out[l])
        hp, s_p, k_p, v_p = decoder_layer(hp, hgrn2_prompt, swa_prompt, *w)
        hs, s_s, k_s, v_s = decoder_layer(
            hs, functools.partial(hgrn2_sample, S=state_hgrn[l]),
            functools.partial(swa_sample, ck=cache_k[l], cv=cache_v[l]), *w)
        sp.append(s_p.astype(state_hgrn.dtype)); kp.append(k_p.astype(cache_k.dtype)); vp.append(v_p.astype(cache_v.dtype))
        ss.append(s_s.astype(state_hgrn.dtype)); ksm.append(k_s.astype(cache_k.dtype)); vsm.append(v_s.astype(cache_v.dtype))
    y_prompt = rmsnorm(hp, norm_final)
    y_sample = rmsnorm(hs, norm_final)
    state_hgrn_prompt = jnp.stack(sp)
    cache_k_prompt = jnp.stack(kp)
    cache_v_prompt = jnp.stack(vp)
    state_hgrn_sample = jnp.stack(ss)
    cache_k_sample = jnp.stack(ksm)
    cache_v_sample = jnp.stack(vsm)
    return (y_prompt, y_sample, state_hgrn_prompt, cache_k_prompt, cache_v_prompt,
            state_hgrn_sample, cache_k_sample, cache_v_sample)


_drawn_inputs = setup_inputs


def setup_inputs(seed=0):
    import zlib

    import numpy as np

    out = dict(_drawn_inputs(seed))
    spreads = {}
    factors = {'a_gnorm': 22.662, 'b_sinks': 200.0, 'norm_final': 20.54, 'w_pb': 4.859}
    for name, (base, spread) in spreads.items():
        noise = np.random.default_rng([zlib.crc32(name.encode()), seed]).standard_normal(out[name].shape)
        drawn = base * np.exp(spread * noise) if base else spread * noise
        out[name] = __import__('jax').numpy.asarray(drawn.astype(out[name].dtype))
    for name, factor in factors.items():
        out[name] = (out[name] * factor).astype(out[name].dtype)
    return out
```

```python
from contextlib import ExitStack

import concourse.bass as bass
from concourse import mybir

F32 = mybir.dt.float32
F32R = mybir.dt.float32r
I32 = mybir.dt.int32
ALU = mybir.AluOpType
ACT = mybir.ActivationFunctionType

P = 128
D = 1024
KT = D // P
SEQ = 1024
NB, DEC = 8, 4
NS = NB * DEC
T = SEQ + NS
NC = SEQ // P
SLOTS = 3
W = T // SLOTS
HEADS = 8
QH, HD = 16, 64
EPS = 1e-6
QU = 4
OFFSET = -1e33
CLAMP = 85.0
OFF = dict(q=0, f=1024, i=2048, z=3072, qb=4096, kb=5120, vb=5248, zb=5376, ga=6400, gb=7424)


class Steps:

    def __init__(self, order):
        self.base, self.names, self.now, total = {}, {}, {}, 0
        for phase, names, rounds, skip in order:
            assert len(set(names)) == len(names), phase
            self.base[phase], self.names[phase], self.now[phase] = total - skip, names, skip
            total += len(names) * rounds - skip

    def at(self, where, step):
        phase, i = where
        return i * len(self.names[phase]) + (self.base[phase] + self.names[phase].index(step) + 1)

    def tick(self, where, step):
        phase = where[0]
        want = self.names[phase][self.now[phase] % len(self.names[phase])]
        assert want == step, f"{phase}: {step} stands where {want} is due"
        self.now[phase] += 1
        return 1


class Blocks:

    def __init__(self, first, per, i):
        self.first, self.per, self.i = first, per, i

    def __call__(self, k):
        return (self.i * self.per + (self.first + k), (self.first + k) % 2,
                self.i * (self.per // 2) + (self.first + k) // 2)


def hybrid_step(nc, x_prompt, x_sample, state_hgrn, cache_k, cache_v, norm_in, w_in, lb_logits, a_gnorm,
                b_sinks, w_pa, w_pb, w_out, norm_final, c_ident, c_causal, c_causal_s, c_batch,
                c_dist, c_slopes, c_bias_s,
                y_prompt, y_sample, st_prompt, ck_prompt, cv_prompt, st_sample, ck_sample, cv_sample):
    per_tile = [f"{s}{t}" for t in range(NC + 1) for s in ("ss", "ln", "rstd", "hi_a", "hi_b")]
    next_head = lambda s: [s + "0", s + "1", s + "2"]
    turn_order = ["t0", "t1", "t2"] + [x for n in range(8) for x in ([f"o{n}"] + ([f"t{n + 3}"] if n < 5 else []))]
    tiles8 = lambda s: [f"{s}{n}" for n in range(8)]
    units = lambda s, k, n=QU: [f"{s}{u}" for u in range(n * k, n * (k + 1))]
    quarters = range(2 * NC // QU)
    exps = [x for k in quarters for x in [f"es0_{k}", f"es1_{k}"] + units("p", k)]
    softmax = (["b0", "b1", "sk", "qs"] + [x for k in quarters for x in units("t", k) + [f"nm0_{k}", f"nm1_{k}"]] + ["zs"]
               + [x for k in quarters for x in [f"dn{k}", f"rd{k}"] + units("n", k)])
    act = Steps([
        ("pro", ["lb0", "lb1"] + per_tile + next_head("sf") + next_head("sigq") + next_head("sigz"), 1, 0),
        ("head", ["rl0", "rl1", "rls", "rx", "lnf", "v0", "ebl", "ebs", "xkD", "v1", "x64", "x32", "v2",
                  "xdq", "xdk", "xqI", "vt0", "vt1", "vts"] + next_head("sf")
         + ["sigq0", "sq0", "sq1", "sqs", "sigq1", "sigq2"] + next_head("sigz"), HEADS - 1, 4),
        ("last", ["rl0", "rl1", "rls", "rx", "lnf", "v0", "ebl", "ebs", "xkD", "v1", "x64", "x32", "v2",
                  "xdq", "xdk", "xqI", "vt0", "vt1", "vts", "sq0", "sq1", "sqs",
                  "fl0", "fl1", "fls", "fx"], 1, 0),
        ("split_a", tiles8("h"), 1, 0),
        ("pa", next_head("sg"), HEADS, 0),
        ("kv", next_head("k") + next_head("v") + ["vt0", "vts", "kt", "ks"] + next_head("q") + next_head("sigz"), 1, 0),
        ("swa", exps + next_head("q") + [f"pt{n}" for n in range(0, NC, 2)] + next_head("sigz"), HEADS - 1, 0),
        ("swa_l", exps + [f"pt{n}" for n in range(0, NC, 2)], 1, 0),
        ("swa_s", ["ct0", "es0_0", "es1_0"] + [f"p{u}" for u in range(4)] + ["pt"], 1, 0),
        ("gb", [f"g{n}" for n in range(6)], HEADS // 2, 0),
        ("split_b", tiles8("h"), 1, 0),
        ("split_m", tiles8("h"), 1, 0),
        ("out", [f"{s}{t}" for t in range(NC + 1) for s in ("ss", "ln", "rs")], 1, 0),
    ])
    prep = ["kf", "scan", "kDa", "kDs", "a64q", "a64k", "a32q", "a32k", "cs", "css", "xa", "xas", "xc",
            "kD", "m64q", "m64k", "m32q", "m32k", "dqm", "dkm", "qIm", "kt0", "kt1", "kts"]
    chain = [f"s{c}" for c in range(1, NC + 1)]
    dve = Steps([
        ("pro", ["par", "lbm", "lbd0", "lbd1", "lbs", "lbr", "lb", "oml", "noml", "ones"]
         + [f"{s}{t}" for t in range(NC + 1) for s in ("xn", "lo_a", "lo_b")] + ["att0", "atts0", "reset", "reset_p", "reset_s"] + next_head("q") + next_head("z"), 1, 0),
        ("head", ["ha"] + prep + chain + ["att0", "att1", "atts", "q0", "gate0", "gate1", "gates", "q1",
                  "so0", "so1", "q2", "z0", "z1", "z2"], HEADS - 1, 1),
        ("last", ["ha"] + prep + chain + ["att0", "att1", "atts", "gate0", "gate1", "gates", "so0", "so1", "hal"], 1, 0),
        ("split_a", tiles8("l"), 1, 0),
        ("pa", next_head("m"), HEADS, 0),
        ("kv", ["sel0", "sel1", "vt1"] + next_head("z"), 1, 0),
        ("swa", softmax
         + [f"pt{n}" for n in range(1, NC, 2)] + ["h0", "h1"] + next_head("z"), HEADS - 1, 0),
        ("swa_l", softmax
         + [f"pt{n}" for n in range(1, NC, 2)] + ["h0", "h1"], 1, 0),
        ("swa_s", ["ct1"] + [f"t{u}" for u in range(4)] + ["nm0_0", "nm1_0", "dn0", "rd0"] + [f"n{u}" for u in range(4)] + ["pn", "h"], 1, 0),
        ("split_b", tiles8("l"), 1, 0),
        ("pb", [f"{s}{n}" for n in range(6) for s in "gm"], HEADS // 2, 0),
        ("split_m", tiles8("l"), 1, 0),
        ("out", [f"{s}{t}" for t in range(NC + 1) for s in ("ya", "yb", "yn")], 1, 0),
    ])
    pe = Steps([
        ("pro", ["par"] + [f"{s}{t}" for t in range(NC + 1) for s in ("xa", "xb")], 1, 0),
        ("head", ["vt0", "vt1", "vts", "kt0", "kt1", "kts", "u0", "u1", "p0", "p1", "ps",
                  "o0", "o1", "os", "us0", "us1", "ms0", "ms1", "mss"], HEADS - 1, 0),
        ("last", ["vt0", "vt1", "vts", "kt0", "kt1", "kts", "u0", "u1", "p0", "p1", "ps",
                  "o0", "o1", "os", "us0", "us1", "ms0", "ms1", "mss"], 1, 0),
        ("kv", ["vt0", "vt1", "vts", "kt"], 1, 0),
        ("swa", tiles8("s") + turn_order, HEADS - 1, 0),
        ("swa_l", tiles8("s") + turn_order, 1, 0),
        ("swa_s", ["ct0", "ct1", "s0", "s1", "s2", "s3", "pt", "pn", "o"], 1, 0),
        ("out", [f"{s}{t}" for t in range(NC + 1) for s in "ab"], 1, 0),
    ])
    pool = Steps([
        ("pro", ["z"], 1, 0),
        ("head", ["vexp", "s0e"], HEADS - 1, 0),
        ("last", ["vexp", "s0e"], 1, 0),
    ])

    ctx = ExitStack()
    with ctx:
        def sb(name, shape, dt=F32, where=ctx):
            return where.enter_context(nc.sbuf_tensor(name, shape, dt))

        def sem(name):
            return ctx.enter_context(nc.semaphore(name))

        pj = [ctx.enter_context(nc.psum_tensor(f"pj{g}", [P, 512], F32)) for g in range(SLOTS)]
        ps_a, ps_b, ps_c, ps_d, ps_e = [ctx.enter_context(nc.psum_tensor(f"ps_{n}", [P, 512], F32)) for n in "abcde"]

        xn_h = sb("xn_h", [P, KT, T], F32R)
        xn_l = sb("xn_l", [P, KT, T], F32R)
        w_raw = [sb(f"w_raw{p}", [P, KT, P]) for p in range(2)]
        w_h = [sb(f"w_h{p}", [P, KT, P], F32R) for p in range(2)]
        w_l = [sb(f"w_l{p}", [P, KT, P], F32R) for p in range(2)]
        ident = sb("ident", [P, P])
        mean_m = sb("mean_m", [P, P])
        par = sb("par", [P, 32])
        lb = sb("lb", [P, HEADS])
        oml = sb("oml", [P, HEADS])
        noml = sb("noml", [P, HEADS])
        lbt = sb("lbt", [P, 3, HEADS])
        rstd = sb("rstd", [P, 2, NC + 1])
        eps = sb("eps", [P, 1])
        mg_area = ExitStack()
        ha = sb("ha", [P, HEADS, T], where=mg_area)
        mg_area.close()
        mg = sb("mg", [P, HEADS, T], where=mg_area)
        mg_area.close()
        x_o = [sb(f"x_o{n}", [P, D], where=mg_area) for n in range(3)]
        y_o = [sb(f"y_o{n}", [P, D], where=mg_area) for n in range(3)]
        y_sq = sb("y_sq", [P, D], where=mg_area)
        g_fin = sb("g_fin", [P, D], where=mg_area)
        sb("mg_pad", [P, HEADS * (T - D)], where=mg_area)
        ctx.enter_context(mg_area)

        area = ExitStack()
        q = sb("q", [P, T], where=area)
        k = sb("k", [P, T], where=area)
        b = sb("b", [P, T], where=area)
        vT = sb("vT", [P, T], where=area)
        zs = sb("zs", [P, T], where=area)
        d64 = sb("d64", [P, NC, 2, 64], where=area)
        d32 = sb("d32", [P, 2 * NC, 2, 32], where=area)
        dq = sb("dq", [P, T], where=area)
        dk = sb("dk", [P, T], where=area)
        qI = sb("qI", [P, T], where=area)
        kD = sb("kD", [P, T], where=area)
        v_tok = sb("v_tok", [P, NC + 1, P], where=area)
        k_tok = sb("k_tok", [P, NC + 1, P], where=area)
        att = sb("att", [P, NC, P], where=area)
        att_s = sb("att_s", [NS, NS], where=area)
        S = sb("S", [P, NC, P], where=area)
        s0 = sb("s0", [P, NB, P], where=area)
        v_exp = sb("v_exp", [NS, NB, P], where=area)
        rs = sb("rs", [P, T], where=area)
        E = sb("E", [P, NC + NB], where=area)
        cs = sb("cs", [P, 32 + NB], where=area)
        reset = sb("reset", [P, T], mybir.dt.bfloat16, where=area)
        causal = sb("causal", [P, P], I32, where=area)
        causal_s = sb("causal_s", [NS, NS], I32, where=area)
        batch_m = sb("batch_m", [NS, NB], where=area)
        area.close()

        area = ExitStack()
        sg = sb("sg", [P, T], where=area)
        hl_h = sb("hl_h", [P, KT, T], F32R, where=area)
        hl_l = sb("hl_l", [P, KT, T], F32R, where=area)
        area.close()

        area = ExitStack()
        hb = sb("hb", [P, HEADS, T], where=area)
        swa = ExitStack()
        kT = sb("kT", [P, T], where=swa)
        v_tk = sb("v_tk", [P, NC + 1, P], where=swa)
        qT = sb("qT", [P, T], where=swa)
        zb = sb("zb", [P, T], where=swa)
        PT = sb("PT", [P, 3, 4, P], where=swa)
        k_out = sb("k_out", [P, 2, P], where=swa)
        dist = sb("dist", [P, 2 * P], where=swa)
        bias = sb("bias", [P, 2, 2 * P], where=swa)
        q_s = sb("q_s", [P, NB, HEADS, DEC], where=swa)
        z_s = sb("z_s", [P, HEADS, NS], where=swa)
        stat = sb("stat", [P, 5, 2 * NC], where=swa)
        sinks = sb("sinks", [P, QH], where=swa)
        pick = sb("pick", [P, HEADS], where=swa)
        sink_m = sb("sink_m", [P, 2], where=swa)
        sinks_s = sb("sinks_s", [P, 2], where=swa)
        slopes = sb("slopes", [P, QH], where=swa)
        stat_s = sb("stat_s", [P, 5, 4], where=swa)
        sc = ExitStack()
        scores = sb("scores", [P, 2 * NC, 2 * P], where=sc)
        sc.close()
        ck = sb("ck", [P, NB, P], where=sc)
        cv = sb("cv", [P, NB, P], where=sc)
        ckT = sb("ckT", [P, NB, P], where=sc)
        sc_s = sb("sc_s", [P, 4, P + NS], where=sc)
        sc.close()
        swa.close()
        sgb = sb("sgb", [P, HEADS, T], where=area)
        wo_raw = sb("wo_raw", [P, KT, P], where=area)
        area.close()
        bias_s = qT[:, 0:4 * (P + NS)].rearrange("p (u k) -> p u k", u=4)
        PT_s = PT[:, 0, :, :]
        PT_n = PT[0:NS, 1, :, :]

        area = ExitStack()
        wo_h = [sb("wo_h0", [P, KT, 512], F32R, where=area)]
        wo_l = [sb("wo_l0", [P, KT, 512], F32R, where=area)]
        sb("wo_pad", [P, HEADS * T - 2 * KT * 512], where=area)
        wo_h += [sb("wo_h1", [P, KT, 512], F32R, where=area)]
        wo_l += [sb("wo_l1", [P, KT, 512], F32R, where=area)]
        area.close()

        area = ExitStack()
        x_t = [sb(f"x_t{n}", [P, D], where=area) for n in range(3)]
        x_sq = sb("x_sq", [P, D], where=area)
        x_n = [sb(f"x_n{n}", [P, D], where=area) for n in range(2)]
        g_row = sb("g_row", [P, D], where=area)
        rows = sb("rows", [32, P], where=area)
        area.close()

        act_done, dve_done, pe_done, pool_done = sem("act_done"), sem("dve_done"), sem("pe_done"), sem("pool_done")
        w_loaded = [sem("w_loaded0"), sem("w_loaded1")]
        w_hi_ready, w_lo_ready, slot_done = sem("w_hi_ready"), sem("w_lo_ready"), sem("slot_done")
        x_loaded = [sem(f"x_loaded{n}") for n in range(3)]
        consts_loaded, g_loaded, masks_loaded = sem("consts_loaded"), sem("g_loaded"), sem("masks_loaded")
        s0_loaded, s0_stored, sp_stored = sem("s0_loaded"), sem("s0_stored"), sem("sp_stored")

        slopes_loaded, caches_loaded, bias_s_loaded = sem("slopes_loaded"), sem("caches_loaded"), sem("bias_s_loaded")
        caches_stored, wo_loaded, wo_hi_ready, wo_lo_ready = sem("caches_stored"), sem("wo_loaded"), sem("wo_hi_ready"), sem("wo_lo_ready")
        g_fin_loaded = sem("g_fin_loaded")
        xo_loaded = [sem(f"xo_loaded{n}") for n in range(3)]
        y_stored = [sem(f"y_stored{n}") for n in range(3)]

        w_pa_v = w_pa[0].rearrange("(k p) c -> p k c", p=P)
        w_pb_v = w_pb[0].rearrange("(s k d) c -> s d k c", s=2, d=HD)
        w_out_v = w_out[0].rearrange("(k p) c -> p k c", p=P)
        GA, KV, QZ, GB, PB, END = 32, 48, 50, 66, 74, 82
        bank_of = lambda t, n: (pj + [ps_a, ps_b, ps_c, ps_d, ps_e])[(2 * t + n) % 8]
        score_bank = lambda n, h: ((ps_a, ps_b, ps_c, ps_d)[n // 2 % 2 * 2 + h], n % 2 * 2 * P)
        pair_of = lambda m: ("swa_l", 0) if is_last(m) else ("swa", m)
        w_in_v = w_in[0].rearrange("(k p) c -> p k c", p=P)
        st_in = state_hgrn[0].rearrange("b h k v -> k b h v")
        st_out = st_sample[0].rearrange("b h k v -> k b h v")
        sp_out = st_prompt[0, 0].rearrange("h k v -> k h v")
        span = lambda g: slice(g * W, (g + 1) * W)
        chunks = lambda a: a.rearrange("p (c t) -> p c t", c=NC)
        half = lambda g: slice(g * 512, (g + 1) * 512)
        by_head = lambda a, k: a.rearrange("p (k n h) -> p k h n", h=2, n=QU // 2)[:, k, :, :]
        now_of = lambda i: ("last", 0) if is_last(i) else ("head", i)
        prev_of = lambda i: ("pro", 0) if is_first(i) else ("head", i - 1)
        is_first = lambda i: isinstance(i, int) and i == 0
        is_last = lambda i: isinstance(i, int) and i == HEADS - 1
        head_blocks = lambda i: Blocks(3, 4, i)

        block = ctx.enter_context(nc.Block())

        @block.sync
        def _(sp):
            def load(B, src, col):
                n, p, _ = B
                if not (isinstance(n, int) and n < 2):
                    sp.wait_ge(w_lo_ready, n - 1)
                for r in range(2):
                    sp.dma_start(w_raw[p][:, 4 * r:4 * r + 4, :], src[:, 4 * r:4 * r + 4, bass.ds(col, P)]).then_inc(w_loaded[p], 16)

            sp.dma_start(ident[:], c_ident).then_inc(consts_loaded, 16)
            sp.dma_start(rows[0:16, :], lb_logits.rearrange("l (h p) -> (l h) p", p=P)).then_inc(consts_loaded, 16)
            sp.dma_start(rows[16:17, :], a_gnorm).then_inc(consts_loaded, 16)
            sp.dma_start(g_row[:], norm_in.to_broadcast([P, D])).then_inc(g_loaded, 16)
            for t in range(3):
                sp.dma_start(x_t[t][:], x_prompt[0, t * P:(t + 1) * P, :]).then_inc(x_loaded[t], 16)
            pro = Blocks(0, 1, 0)
            load(pro(0), w_in_v, OFF["f"])
            load(pro(1), w_in_v, OFF["q"])
            for t in range(3, NC + 1):
                sp.wait_ge(dve_done, dve.at(("pro", 0), f"xn{t - 3}"))
                if t < NC:
                    sp.dma_start(x_t[t % 3][:], x_prompt[0, t * P:(t + 1) * P, :]).then_inc(x_loaded[t % 3], 16)
                else:
                    sp.dma_start(x_t[t % 3][0:NS, :], x_sample.rearrange("b t d -> (b t) d")).then_inc(x_loaded[t % 3], 16)
            load(pro(2), w_in_v, OFF["z"])
            sp.wait_ge(pe_done, pe.at(("pro", 0), f"xb{NC}"))
            sp.dma_start(causal[:], c_causal).then_inc(masks_loaded, 16)
            sp.dma_start(causal_s[:], c_causal_s).then_inc(masks_loaded, 16)
            sp.dma_start(batch_m[:], c_batch).then_inc(masks_loaded, 16)

            def head(i):
                B = head_blocks(i)
                now = now_of(i)
                if is_first(i):
                    sp.dma_start(s0[:], st_in[:, :, 0, :]).then_inc(s0_loaded, 16)
                load(B(0), w_in_v, i * P + OFF["i"])
                if is_last(i):
                    load(B(1), w_in_v, OFF["ga"])
                    load(B(2), w_pa_v, 0)
                else:
                    load(B(1), w_in_v, i * P + (OFF["f"] + P))
                    load(B(2), w_in_v, i * P + (OFF["q"] + P))
                    load(B(3), w_in_v, i * P + (OFF["z"] + P))
                sp.wait_ge(dve_done, dve.at(now, "s8"))
                sp.dma_start(sp_out[:, bass.ds(i, 1), :], S[:, NC - 1:NC, :]).then_inc(sp_stored, 16)
                sp.wait_ge(dve_done, dve.at(now, "so1"))
                sp.dma_start(st_out[:, :, bass.ds(i, 1), :], s0[:].rearrange("p b (o v) -> p b o v", o=1)).then_inc(s0_stored, 16)
                if not is_last(i):
                    sp.wait_ge(s0_stored, i * 16 + 16)
                    sp.dma_start(s0[:].rearrange("p b (o v) -> p b o v", o=1), st_in[:, :, bass.ds(i + 1, 1), :]).then_inc(s0_loaded, 16)

            head(0)
            with nc.sync.Fori(1, HEADS - 1) as i:
                head(i)
            head(HEADS - 1)

            with nc.sync.Fori(0, HEADS - 1) as j:
                B = Blocks(GA, 2, j)
                load(B(2), w_in_v, j * P + (OFF["ga"] + P))
                load(B(3), w_pa_v, j * P + P)
            kv = Blocks(KV, 2, 0)
            load(kv(0), w_in_v, OFF["kb"])
            load(kv(1), w_in_v, OFF["vb"])
            sp.wait_ge(slot_done, SLOTS * KV)
            sp.dma_start(dist[:], c_dist).then_inc(slopes_loaded, 16)
            sp.dma_start(slopes[:], c_slopes[:, 0:QH]).then_inc(slopes_loaded, 16)
            sp.dma_start(pick[:], c_slopes[:, QH:QH + 8]).then_inc(slopes_loaded, 16)
            sp.dma_start(sinks[:], b_sinks.to_broadcast([P, QH])).then_inc(slopes_loaded, 16)

            def load_pair(B, off, m):
                n, p, _ = B
                sp.wait_ge(w_lo_ready, n - 1)
                for r in range(2):
                    sp.dma_start(w_raw[p][:, :, r * HD:(r + 1) * HD],
                                 w_in_v[:, :, bass.ds(m * HD + (off + r * QH // 2 * HD), HD)]).then_inc(w_loaded[p], 16)

            qz = Blocks(QZ, 2, 0)
            load_pair(qz(0), OFF["qb"], 0)
            load_pair(qz(1), OFF["zb"], 0)
            for new, old in ((ck_sample, cache_k), (cv_sample, cache_v)):
                sp.dma_start(new[0, :, 0:P - DEC].rearrange("b t h d -> b (t h d)"),
                             old[0, :, DEC:P].rearrange("b t h d -> b (t h d)")).then_inc(caches_stored, 16)
            sp.wait_ge(act_done, act.at(("kv", 0), "ks"))
            sp.wait_ge(dve_done, dve.at(("kv", 0), "vt1"))
            sp.dma_start(ck_prompt[0, 0].rearrange("t h d -> t (h d)"), k_out[:, 0, :]).then_inc(caches_stored, 16)
            sp.dma_start(cv_prompt[0, 0].rearrange("t h d -> t (h d)"), v_tk[:, NC - 1, :]).then_inc(caches_stored, 16)
            for m in range(NB):
                rows_m = slice(DEC * m, DEC * (m + 1))
                sp.dma_start(ck_sample[0, m, P - DEC:P].rearrange("t h d -> t (h d)"), k_out[rows_m, 1, :]).then_inc(caches_stored, 16)
                sp.dma_start(cv_sample[0, m, P - DEC:P].rearrange("t h d -> t (h d)"), v_tk[rows_m, NC, :]).then_inc(caches_stored, 16)
            with nc.sync.Fori(0, HEADS - 1) as m:
                B = Blocks(QZ, 2, m)
                load_pair(B(2), OFF["qb"], m + 1)
                load_pair(B(3), OFF["zb"], m + 1)
            gb = Blocks(GB, 2, 0)
            load(gb(0), w_in_v, OFF["gb"])
            load(gb(1), w_in_v, OFF["gb"] + P)
            sp.wait_ge(pe_done, pe.at(("swa_l", 0), "t7"))
            sp.wait_ge(dve_done, dve.at(("swa_l", 0), "n15"))
            sp.dma_start(ck[:], cache_k[0].rearrange("b t h d -> t b (h d)")).then_inc(caches_loaded, 16)
            sp.dma_start(cv[:], cache_v[0].rearrange("b t h d -> t b (h d)")).then_inc(caches_loaded, 16)
            sp.dma_start(bias_s, c_bias_s).then_inc(bias_s_loaded, 16)

            def load_pb(B, col):
                n, p, _ = B
                sp.wait_ge(w_lo_ready, n - 1)
                for r in range(2):
                    sp.dma_start(w_raw[p][r * HD:(r + 1) * HD, :, :], w_pb_v[r, :, :, bass.ds(col, P)]).then_inc(w_loaded[p], 16)

            with nc.sync.Fori(0, 3) as j:
                B = Blocks(GB, 2, j)
                load(B(2), w_in_v, j * (2 * P) + (OFF["gb"] + 2 * P))
                load(B(3), w_in_v, j * (2 * P) + (OFF["gb"] + 3 * P))
            pb = Blocks(PB, 2, 0)
            load_pb(pb(0), 0)
            load_pb(pb(1), P)

            def load_wo(c):
                if isinstance(c, int) and c == 0:
                    sp.wait_ge(dve_done, dve.at(("swa_s", 0), "h"))
                else:
                    sp.wait_ge(wo_lo_ready, c)
                sp.dma_start(wo_raw[:], w_out_v[:, :, bass.ds(c * P, P)]).then_inc(wo_loaded, 16)

            load_wo(0)
            with nc.sync.Fori(0, 3) as j:
                B = Blocks(PB, 2, j)
                load_pb(B(2), j * (2 * P) + 2 * P)
                load_pb(B(3), j * (2 * P) + 3 * P)
                load_wo(j + 1)
            for c in range(4, 8):
                load_wo(c)

            sp.wait_ge(dve_done, dve.at(("split_m", 0), "l7"))
            sp.dma_start(g_fin[:], norm_final.rearrange("(o d) -> o d", o=1).to_broadcast([P, D])).then_inc(g_fin_loaded, 16)

            def token_rows(prompt, sample, t):
                return prompt[0, t * P:(t + 1) * P, :] if t < NC else sample.rearrange("b t d -> (b t) d")

            def load_x(t):
                r = P if t < NC else NS
                sp.dma_start(x_o[t % 3][0:r, :], token_rows(x_prompt, x_sample, t)).then_inc(xo_loaded[t % 3], 16)

            for t in range(3):
                load_x(t)
            for t in range(NC + 1):
                r = P if t < NC else NS
                sp.wait_ge(dve_done, dve.at(("out", 0), f"yn{t}"))
                sp.dma_start(token_rows(y_prompt, y_sample, t), y_o[t % 3][0:r, :]).then_inc(y_stored[t % 3], 16)
                if t + 3 < NC + 1:
                    load_x(t + 3)
            for n in range(3):
                sp.wait_ge(y_stored[n], 16 * 3)
            sp.wait_ge(sp_stored, 16 * HEADS)
            sp.wait_ge(s0_stored, 16 * HEADS)
            sp.wait_ge(caches_stored, 16 * (4 + 2 * NB))

        @block.gpsimd
        def _(g):
            def split_lo(B):
                n, p, _ = B
                g.wait_ge(w_hi_ready, n + 1)
                g.tensor_tensor(w_l[p][:], w_raw[p][:], w_h[p][:].bitcast(F32), ALU.subtract).then_inc(w_lo_ready, 1)

            pro = Blocks(0, 1, 0)
            g.memset(eps[:], EPS).then_inc(pool_done, pool.tick(("pro", 0), "z"))
            for n in range(3):
                split_lo(pro(n))

            def head(i):
                B, now = head_blocks(i), now_of(i)
                split_lo(B(0))
                if is_first(i):
                    g.wait_ge(masks_loaded, 48)
                g.wait_ge(act_done, act.at(now, "vts"))
                g.tensor_tensor(v_exp[:], v_tok[0:NS, NC:NC + 1, :].to_broadcast([NS, NB, P]),
                                batch_m[:].rearrange("p (b o) -> p b o", o=1).to_broadcast([NS, NB, P]),
                                ALU.mult).then_inc(pool_done, pool.tick(now, "vexp"))
                if not is_last(i):
                    split_lo(B(1))
                    split_lo(B(2))
                g.wait_ge(pe_done, pe.at(now, "os"))
                g.tensor_tensor(s0[:], s0[:], E[:, NC:NC + NB].rearrange("p (b o) -> p b o", o=1).to_broadcast([P, NB, P]),
                                ALU.mult).then_inc(pool_done, pool.tick(now, "s0e"))
                split_lo(B(1) if is_last(i) else B(3))

            head(0)
            with nc.gpsimd.Fori(1, HEADS - 1) as i:
                head(i)
            head(HEADS - 1)
            with nc.gpsimd.Fori(0, HEADS) as j:
                B = Blocks(GA, 2, j)
                split_lo(B(1))
                split_lo(B(2))
            for n in range(1, 4):
                split_lo(Blocks(KV, 2, 0)(n))
            split_lo(Blocks(QZ, 2, 0)(2))
            split_lo(Blocks(QZ, 2, 0)(3))
            with nc.gpsimd.Fori(0, HEADS - 1) as m:
                B = Blocks(QZ, 2, m)
                split_lo(B(4))
                split_lo(B(5))
            with nc.gpsimd.Fori(0, 4) as j:
                B = Blocks(GB, 2, j)
                split_lo(B(2))
                split_lo(B(3))

            def wo_split_lo(c, half_, at):
                g.wait_ge(wo_hi_ready, c + 1)
                g.tensor_tensor(wo_l[half_][:, :, at], wo_raw[:], wo_h[half_][:, :, at].bitcast(F32), ALU.subtract).then_inc(wo_lo_ready, 1)

            for j in range(4):
                if j < 3:
                    split_lo(Blocks(PB, 2, j)(2))
                    split_lo(Blocks(PB, 2, j)(3))
                wo_split_lo(j, 0, slice(j * P, (j + 1) * P))
            for c in range(4, 8):
                wo_split_lo(c, 1, slice((c - 4) * P, (c - 3) * P))

        @block.scalar
        def _(a):
            pr = ("pro", 0)
            nc.scalar.preload_act_table_set("natural_log_exp_and_others")

            def split_hi(B):
                n, p, h = B
                a.wait_ge(w_loaded[p], h * 32 + 32)
                if not (isinstance(n, int) and n < 2):
                    a.wait_ge(slot_done, n * 3 - 3)
                a.activation(w_h[p][:], w_raw[p][:], ACT.Copy).then_inc(w_hi_ready, 1)

            a.wait_ge(dve_done, dve.at(pr, "lbd1"))
            a.activation(lbt[:, 0, :], lbt[:, 0, :], ACT.Exp).then_inc(act_done, act.tick(pr, "lb0"))
            a.activation(lbt[:, 1, :], lbt[:, 1, :], ACT.Exp).then_inc(act_done, act.tick(pr, "lb1"))
            a.wait_ge(pool_done, pool.at(pr, "z"))
            pro = Blocks(0, 1, 0)
            split_hi(pro(0))
            split_hi(pro(1))
            for t in range(NC + 1):
                r = P if t < NC else NS
                a.wait_ge(x_loaded[t % 3], 16 * (t // 3 + 1))
                if t:
                    a.wait_ge(act_done, act.at(pr, f"ss{t - 1}"))
                a.activation(x_sq[0:r], x_t[t % 3][0:r, :], ACT.Square, accum_out=rstd[0:r, 0, t:t + 1]).then_inc(act_done, act.tick(pr, f"ss{t}"))
                a.wait_ge(act_done, act.at(pr, f"ss{t}"))
                a.activation(rstd[0:r, 0, t:t + 1], rstd[0:r, 0, t:t + 1], ACT.Ln, scale=1.0 / D, bias=eps[0:r]).then_inc(act_done, act.tick(pr, f"ln{t}"))
                a.wait_ge(act_done, act.at(pr, f"ln{t}"))
                a.activation(rstd[0:r, 1, t:t + 1], rstd[0:r, 0, t:t + 1], ACT.Exp, scale=-0.5).then_inc(act_done, act.tick(pr, f"rstd{t}"))
                for n, (bank, s) in enumerate((((ps_a, ps_c)[t % 2], "a"), ((ps_b, ps_d)[t % 2], "b"))):
                    a.wait_ge(pe_done, pe.at(pr, f"x{s}{t}"))
                    a.activation(xn_h[:, 4 * n:4 * n + 4, t * P:t * P + r], bank[:].rearrange("p (k t) -> p k t", k=4)[:, :, 0:r],
                                 ACT.Copy).then_inc(act_done, act.tick(pr, f"hi_{s}{t}"))

            def sig(where, name, n_slot, g, out):
                a.wait_ge(slot_done, n_slot)
                a.activation(out[:, span(g)], pj[g][:, 0:W], ACT.Sigmoid).then_inc(act_done, act.tick(where, f"{name}{g}"))

            for n, (name, out) in enumerate((("sf", k), ("sigq", q), ("sigz", zs))):
                for g in range(SLOTS):
                    sig(pr, name, 3 * n + g + 1, g, out)
                if n + 2 < 4:
                    split_hi(pro(n + 2) if n == 0 else head_blocks(0)(0))

            def head(i):
                B, now = head_blocks(i), now_of(i)
                prev = prev_of(i)
                last = is_last(i)
                if not is_first(i):
                    nc.scalar.preload_act_table_set("natural_log_exp_and_others")
                    a.wait_ge(pe_done, pe.at(prev, "mss"))
                    a.activation(rs[:, half(0)], ps_a[:], ACT.Ln, bias=eps[:]).then_inc(act_done, act.tick(now, "rl0"))
                    a.activation(rs[:, half(1)], ps_b[:], ACT.Ln, bias=eps[:]).then_inc(act_done, act.tick(now, "rl1"))
                    a.activation(rs[:, SEQ:T], ps_d[:, 64:64 + NS], ACT.Ln, bias=eps[:]).then_inc(act_done, act.tick(now, "rls"))
                    a.wait_ge(act_done, act.at(now, "rls"))
                    a.activation(rs[:], rs[:], ACT.Exp, scale=-0.5).then_inc(act_done, act.tick(now, "rx"))
                a.wait_ge(act_done, act.at(prev, "sf2"))
                if is_first(i):
                    nc.scalar.preload_act_table_set("natural_log_exp_and_others")
                a.activation(b[:], k[:], ACT.Ln, scale=oml[:, bass.ds(i, 1)], bias=lb[:, bass.ds(i, 1)]).then_inc(act_done, act.tick(now, "lnf"))
                if not last:
                    split_hi(B(1))

                def v_copy(g):
                    a.wait_ge(slot_done, B(0)[0] * 3 + (g + 1))
                    a.activation(vT[:, span(g)], pj[g][:, 0:W], ACT.Copy).then_inc(act_done, act.tick(now, f"v{g}"))

                def exp(name, need, out, src, scale=1.0):
                    a.wait_ge(dve_done, dve.at(now, need))
                    a.activation(out, src, ACT.Exp, scale=scale).then_inc(act_done, act.tick(now, name))

                v_copy(0)
                if not is_first(i):
                    a.wait_ge(pool_done, pool.at(prev, "s0e"))
                exp("ebl", "scan", E[:, 0:NC], chunks(b[:, 0:SEQ])[:, :, P - 1])
                exp("ebs", "scan", E[:, NC:NC + NB], b[:, SEQ:T].rearrange("p (b t) -> p b t", b=NB)[:, :, DEC - 1])
                exp("xkD", "kDs", kD[:], kD[:])
                v_copy(1)
                exp("x64", "a64k", d64[:], d64[:])
                exp("x32", "a32k", d32[:], d32[:])
                v_copy(2)
                split_hi(B(1) if last else B(2))
                exp("xdq", "xc", dq[:], dk[:], -1.0)
                exp("xdk", "xc", dk[:], dk[:])
                exp("xqI", "scan", qI[:], b[:])
                for n, (bank, cols) in enumerate(((ps_a, slice(0, 4)), (ps_b, slice(4, 8)))):
                    a.wait_ge(pe_done, pe.at(now, f"vt{n}"))
                    a.activation(v_tok[:, cols, :], bank[:].rearrange("p (c v) -> p c v", c=4), ACT.Copy).then_inc(act_done, act.tick(now, f"vt{n}"))
                a.wait_ge(pe_done, pe.at(now, "vts"))
                a.activation(v_tok[0:NS, NC, :], ps_e[0:NS, 0:P], ACT.Copy).then_inc(act_done, act.tick(now, "vts"))

                def squares():
                    a.wait_ge(pe_done, pe.at(now, "o0"))
                    a.activation(dq[:, half(0)], ps_e[:], ACT.Square).then_inc(act_done, act.tick(now, "sq0"))
                    a.wait_ge(pe_done, pe.at(now, "o1"))
                    a.activation(dq[:, half(1)], ps_c[:], ACT.Square).then_inc(act_done, act.tick(now, "sq1"))
                    a.wait_ge(pe_done, pe.at(now, "os"))
                    a.activation(dq[:, SEQ:T], ps_d[:, 0:NS], ACT.Square).then_inc(act_done, act.tick(now, "sqs"))

                if last:
                    squares()
                    a.wait_ge(pe_done, pe.at(now, "mss"))
                    a.activation(rs[:, half(0)], ps_a[:], ACT.Ln, bias=eps[:]).then_inc(act_done, act.tick(now, "fl0"))
                    a.activation(rs[:, half(1)], ps_b[:], ACT.Ln, bias=eps[:]).then_inc(act_done, act.tick(now, "fl1"))
                    a.activation(rs[:, SEQ:T], ps_d[:, 64:64 + NS], ACT.Ln, bias=eps[:]).then_inc(act_done, act.tick(now, "fls"))
                    a.wait_ge(act_done, act.at(now, "fls"))
                    a.activation(rs[:], rs[:], ACT.Exp, scale=-0.5).then_inc(act_done, act.tick(now, "fx"))
                    return
                nc.scalar.preload_act_table(ACT.Sigmoid)
                a.wait_ge(dve_done, dve.at(now, "qIm"))
                for g in range(SLOTS):
                    sig(now, "sf", B(1)[0] * 3 + (g + 1), g, k)
                split_hi(B(3))
                sig(now, "sigq", B(2)[0] * 3 + 1, 0, q)
                squares()
                for g in (1, 2):
                    sig(now, "sigq", B(2)[0] * 3 + (g + 1), g, q)
                split_hi(B(4))
                a.wait_ge(dve_done, dve.at(now, "gates"))
                for g in range(SLOTS):
                    sig(now, "sigz", B(3)[0] * 3 + (g + 1), g, zs)

            head(0)
            with nc.scalar.Fori(1, HEADS - 1) as i:
                head(i)
            head(HEADS - 1)

            def split_rows(phase, src, hi):
                for n in range(KT):
                    a.activation(hi[:, n, :], src[:, n, :], ACT.Copy).then_inc(act_done, act.tick((phase, 0), f"h{n}"))

            nc.scalar.preload_act_table(ACT.Sigmoid)
            a.wait_ge(dve_done, dve.at(("last", 0), "hal"))
            a.wait_ge(sp_stored, 16 * HEADS)
            a.wait_ge(s0_stored, 16 * HEADS)
            split_rows("split_a", ha, hl_h)
            with nc.scalar.Fori(0, HEADS) as j:
                B = Blocks(GA, 2, j)
                split_hi(B(1))
                for g in range(SLOTS):
                    a.wait_ge(dve_done, dve.at(("pa", j - 1), f"m{g}"))
                    sig(("pa", j), "sg", B(0)[0] * 3 + (g + 1), g, sg)
                split_hi(B(2))

            def copy(where, name, n_slot, g, out, scale=1.0):
                a.wait_ge(slot_done, n_slot)
                a.activation(out[:, span(g)], pj[g][:, 0:W], ACT.Copy, scale=scale).then_inc(act_done, act.tick(where, f"{name}{g}"))

            kv, here = Blocks(KV, 2, 0), ("kv", 0)
            split_hi(kv(1))
            a.wait_ge(dve_done, dve.at(("pa", HEADS - 1), "m2"))
            for g in range(SLOTS):
                copy(here, "k", 3 * KV + g + 1, g, kT)
            split_hi(kv(2))
            for g in range(SLOTS):
                copy(here, "v", 3 * (KV + 1) + g + 1, g, zb)
            split_hi(kv(3))
            a.wait_ge(pe_done, pe.at(here, "vt0"))
            a.activation(v_tk[:, 0:4, :], ps_a[:].rearrange("p (c v) -> p c v", c=4), ACT.Copy).then_inc(act_done, act.tick(here, "vt0"))
            a.wait_ge(pe_done, pe.at(here, "vts"))
            a.activation(v_tk[0:NS, NC, :], ps_c[0:NS, 0:P], ACT.Copy).then_inc(act_done, act.tick(here, "vts"))
            a.wait_ge(pe_done, pe.at(here, "kt"))
            a.activation(k_out[:, 0, :], ps_d[:, 0:P], ACT.Copy).then_inc(act_done, act.tick(here, "kt"))
            a.activation(k_out[0:NS, 1, :], ps_d[0:NS, P:2 * P], ACT.Copy).then_inc(act_done, act.tick(here, "ks"))
            for g in range(SLOTS):
                copy(here, "q", 3 * QZ + g + 1, g, qT, HD ** -0.5)
            split_hi(Blocks(QZ, 2, 0)(2))
            for g in range(SLOTS):
                sig(here, "sigz", 3 * (QZ + 1) + g + 1, g, zb)
            split_hi(Blocks(QZ, 2, 0)(3))

            def pair(m):
                B, now = Blocks(QZ, 2, m), pair_of(m)
                last = is_last(m)
                nc.scalar.preload_act_table_set("natural_log_exp_and_others")
                for k in quarters:
                    for h in range(2):
                        a.wait_ge(dve_done, dve.at(now, f"nm{h}_{k}"))
                        a.activation(by_head(stat[:, 2, :], k)[:, h, :], by_head(stat[:, 1, :], k)[:, h, :], ACT.Exp,
                                     bias=sink_m[:, h:h + 1]).then_inc(act_done, act.tick(now, f"es{h}_{k}"))
                    for u in range(QU * k, QU * (k + 1)):
                        keys = slice(P if u < 2 else 0, 2 * P)
                        a.activation(scores[:, u, keys], scores[:, u, keys], ACT.Exp, bias=stat[:, 1, u:u + 1],
                                     accum_out=stat[:, 3, u:u + 1]).then_inc(act_done, act.tick(now, f"p{u}"))
                if not last:
                    a.wait_ge(pe_done, pe.at(now, "s7"))
                    a.wait_ge(dve_done, dve.at(now, "qs"))
                    for g in range(SLOTS):
                        copy(now, "q", B(2)[0] * 3 + (g + 1), g, qT, HD ** -0.5)
                    split_hi(B(4))
                for n in range(0, NC, 2):
                    a.wait_ge(pe_done, pe.at(now, f"t{n}"))
                    if n >= 3:
                        a.wait_ge(pe_done, pe.at(now, f"o{n - 3}"))
                    fill = slice(P if n == 0 else 0, 4 * P)
                    src = (ps_a, ps_b, ps_c)[n % 3]
                    a.activation(PT[:, n % 3, :, :].rearrange("p a q -> p (a q)")[:, fill], src[:, fill], ACT.Copy).then_inc(act_done, act.tick(now, f"pt{n}"))
                if not last:
                    nc.scalar.preload_act_table(ACT.Sigmoid)
                    a.wait_ge(dve_done, dve.at(now, "h1"))
                    for g in range(SLOTS):
                        sig(now, "sigz", B(3)[0] * 3 + (g + 1), g, zb)
                    split_hi(B(5))

            with nc.scalar.Fori(0, HEADS - 1) as m:
                pair(m)
            pair(HEADS - 1)

            here = ("swa_s", 0)
            a.wait_ge(pe_done, pe.at(here, "ct0"))
            a.activation(ckT[:, 0:4, :], ps_a[:].rearrange("p (c v) -> p c v", c=4), ACT.Copy).then_inc(act_done, act.tick(here, "ct0"))
            for h in range(2):
                a.wait_ge(dve_done, dve.at(here, f"nm{h}_0"))
                a.activation(stat_s[:, 2, 2 * h:2 * h + 2], stat_s[:, 1, 2 * h:2 * h + 2], ACT.Exp, bias=sinks_s[:, h:h + 1]).then_inc(act_done, act.tick(here, f"es{h}_0"))
            for u in range(4):
                a.activation(sc_s[:, u, :], sc_s[:, u, :], ACT.Exp, bias=stat_s[:, 1, u:u + 1], accum_out=stat_s[:, 3, u:u + 1]).then_inc(act_done, act.tick(here, f"p{u}"))
            a.wait_ge(pe_done, pe.at(here, "pt"))
            a.activation(PT_s.rearrange("p a q -> p (a q)"), ps_a[:], ACT.Copy).then_inc(act_done, act.tick(here, "pt"))

            nc.scalar.preload_act_table(ACT.Sigmoid)
            a.wait_ge(dve_done, dve.at(here, "h"))
            with nc.scalar.Fori(0, 4) as j:
                B = Blocks(GB, 2, j)
                for m in range(2):
                    for g in range(SLOTS):
                        a.wait_ge(slot_done, B(m)[0] * 3 + (g + 1))
                        a.activation(sgb[:, bass.ds(j * 2 + m, 1), span(g)], pj[g][:, 0:W].rearrange("p (o t) -> p o t", o=1), ACT.Sigmoid)\
                         .then_inc(act_done, act.tick(("gb", j), f"g{3 * m + g}"))
                    split_hi(B(2 + m))
            a.wait_ge(slot_done, 3 * PB)
            split_rows("split_b", hb, xn_h)

            def wo_split_hi(c, half_, at):
                a.wait_ge(wo_loaded, 16 * (c + 1))
                a.activation(wo_h[half_][:, :, at], wo_raw[:], ACT.Copy).then_inc(wo_hi_ready, 1)

            a.wait_ge(dve_done, dve.at(("split_b", 0), "l7"))
            for j in range(4):
                if j < 3:
                    split_hi(Blocks(PB, 2, j)(2))
                    split_hi(Blocks(PB, 2, j)(3))
                wo_split_hi(j, 0, slice(j * P, (j + 1) * P))
            a.wait_ge(dve_done, dve.at(("pb", 3), "m5"))
            split_rows("split_m", mg, xn_h)
            for c in range(4, 8):
                wo_split_hi(c, 1, slice((c - 4) * P, (c - 3) * P))
            nc.scalar.preload_act_table_set("natural_log_exp_and_others")
            here = ("out", 0)
            for t in range(NC + 1):
                r = P if t < NC else NS
                a.wait_ge(dve_done, dve.at(here, f"yb{t}"))
                if t:
                    a.wait_ge(act_done, act.at(here, f"rs{t - 1}"))
                else:
                    a.wait_ge(dve_done, dve.at(("split_m", 0), "l7"))
                a.activation(y_sq[0:r], y_o[t % 3][0:r, :], ACT.Square, accum_out=rstd[0:r, 0, t:t + 1]).then_inc(act_done, act.tick(here, f"ss{t}"))
                a.wait_ge(act_done, act.at(here, f"ss{t}"))
                a.activation(rstd[0:r, 0, t:t + 1], rstd[0:r, 0, t:t + 1], ACT.Ln, scale=1.0 / D, bias=eps[0:r]).then_inc(act_done, act.tick(here, f"ln{t}"))
                a.wait_ge(act_done, act.at(here, f"ln{t}"))
                a.activation(rstd[0:r, 1, t:t + 1], rstd[0:r, 0, t:t + 1], ACT.Exp, scale=-0.5).then_inc(act_done, act.tick(here, f"rs{t}"))

        @block.tensor
        def _(t):
            pr = ("pro", 0)

            def slot(B, g, xh=xn_h, xl=xn_l):
                n, p, _ = B
                if g == 0:
                    t.wait_ge(w_hi_ready, n + 1)
                    t.wait_ge(w_lo_ready, n + 1)
                passes = ((w_h[p], xh), (w_h[p], xl), (w_l[p], xh))
                for kt in range(KT):
                    for m, (w, x) in enumerate(passes):
                        mm = nc.tensor.matmul(pj[g][:, 0:W], w[:, kt, :], x[:, kt, span(g)],
                                              start=(kt == 0 and m == 0), stop=(kt == KT - 1 and m == 2))
                mm.then_inc(slot_done, 1)

            t.wait_ge(consts_loaded, 48)
            nc.tensor.transpose(ps_e[:, 0:17], rows[0:17, :], ident[0:17, 0:17]).then_inc(pe_done, pe.tick(pr, "par"))
            for n in range(NC + 1):
                r = P if n < NC else NS
                t.wait_ge(dve_done, dve.at(pr, f"xn{n}"))
                for m, (bank, s) in enumerate((((ps_a, ps_c)[n % 2], "a"), ((ps_b, ps_d)[n % 2], "b"))):
                    if n >= 2:
                        t.wait_ge(act_done, act.at(pr, f"hi_{s}{n - 2}"))
                        t.wait_ge(dve_done, dve.at(pr, f"lo_{s}{n - 2}"))
                    for j in range(4):
                        kt = 4 * m + j
                        mm = nc.tensor.transpose(bank[:, j * P:j * P + r], x_n[n % 2][0:r, kt * P:(kt + 1) * P], ident[0:r, 0:r])
                    mm.then_inc(pe_done, pe.tick(pr, f"x{s}{n}"))
            t.wait_ge(act_done, act.at(pr, f"hi_b{NC}"))
            t.wait_ge(dve_done, dve.at(pr, f"lo_b{NC}"))
            pro = Blocks(0, 1, 0)
            for g in range(SLOTS):
                slot(pro(0), g)
            for g in range(SLOTS):
                t.wait_ge(act_done, act.at(pr, f"sf{g}"))
                slot(pro(1), g)
            for g in range(SLOTS):
                t.wait_ge(dve_done, dve.at(pr, f"q{g}"))
                slot(pro(2), g)

            def head(i):
                B, now = head_blocks(i), now_of(i)
                prev = prev_of(i)
                last = is_last(i)

                def turn(bank, at, src, cols, name):
                    for j, c in enumerate(cols):
                        r = P if c < NC else NS
                        mm = nc.tensor.transpose(bank[0:r, at + j * P:at + (j + 1) * P], src[:, c * P:c * P + r], ident[:, :])
                    mm.then_inc(pe_done, pe.tick(now, name))

                for g in range(SLOTS):
                    t.wait_ge(dve_done, dve.at(prev, f"z{g}"))
                    slot(B(0), g)
                t.wait_ge(act_done, act.at(now, "v2"))
                turn(ps_a, 0, vT, range(0, 4), "vt0")
                turn(ps_b, 0, vT, range(4, 8), "vt1")
                turn(ps_e, 0, vT, [NC], "vts")

                def gate_slot(k_block, name, by, g):
                    if not last:
                        t.wait_ge(by[0], by[1].at(now, f"{name}{g}"))
                        slot(B(k_block), g)

                gate_slot(1, "v", (act_done, act), 0)
                t.wait_ge(dve_done, dve.at(now, "kD"))
                turn(ps_c, 0, kD, range(0, 4), "kt0")
                turn(ps_d, 0, kD, range(4, 8), "kt1")
                t.wait_ge(act_done, act.at(now, "vts"))
                turn(ps_e, P, kD, [NC], "kts")
                gate_slot(1, "v", (act_done, act), 1)
                t.wait_ge(act_done, act.at(now, "vts"))
                t.wait_ge(dve_done, dve.at(now, "kts"))
                for n, bank in enumerate((ps_c, ps_d)):
                    for j in range(4):
                        c = 4 * n + j
                        mm = nc.tensor.matmul(bank[:, j * P:(j + 1) * P], k_tok[:, c, :], v_tok[:, c, :], start=True, stop=True)
                    mm.then_inc(pe_done, pe.tick(now, f"u{n}"))
                gate_slot(1, "v", (act_done, act), 2)
                t.wait_ge(dve_done, dve.at(now, "dkm"))
                for n, bank in enumerate((ps_a, ps_b)):
                    for j in range(4):
                        c, o = 4 * n + j, j * P
                        nc.tensor.matmul(bank[0:64, o + 64:o + 128], d64[:, c, 0, :], d64[:, c, 1, :], start=True, stop=True)
                        for m in range(2):
                            nc.tensor.matmul(bank[64 * m:64 * m + 32, o + 64 * m + 32:o + 64 * m + 64],
                                             d32[:, 2 * c + m, 0, :], d32[:, 2 * c + m, 1, :], start=True, stop=True)
                        for m in range(4):
                            e = c * P + 32 * m
                            mm = nc.tensor.matmul(bank[32 * m:32 * m + 32, o + 32 * m:o + 32 * m + 32],
                                                  dk[:, e:e + 32], dq[:, e:e + 32], start=True, stop=True)
                    mm.then_inc(pe_done, pe.tick(now, f"p{n}"))
                nc.tensor.matmul(ps_e[0:NS, 256:256 + NS], dk[:, SEQ:T], dq[:, SEQ:T], start=True, stop=True).then_inc(pe_done, pe.tick(now, "ps"))
                gate_slot(2, "sf", (act_done, act), 0)
                t.wait_ge(dve_done, dve.at(now, "atts"))
                t.wait_ge(dve_done, dve.at(now, "qIm"))
                for n, bank in enumerate((ps_e, ps_c)):
                    for j in range(4):
                        c = 4 * n + j
                        mm = nc.tensor.matmul(bank[:, j * P:(j + 1) * P], v_tok[:, c, :], att[:, c, :], start=True, stop=(c == 0))
                        if c:
                            mm = nc.tensor.matmul(bank[:, j * P:(j + 1) * P], S[:, c - 1, :], qI[:, c * P:(c + 1) * P], start=False, stop=True)
                    mm.then_inc(pe_done, pe.tick(now, f"o{n}"))
                t.wait_ge(s0_loaded, i * 16 + 16)
                nc.tensor.matmul(ps_d[:, 0:NS], v_tok[0:NS, NC, :], att_s[:, :], start=True, stop=True)
                for m in range(NB):
                    e = SEQ + DEC * m
                    mm = nc.tensor.matmul(ps_d[:, DEC * m:DEC * (m + 1)], s0[:, m, :], qI[:, e:e + DEC], start=False, stop=True, skip_group_check=True)
                mm.then_inc(pe_done, pe.tick(now, "os"))
                gate_slot(2, "sf", (act_done, act), 1)
                t.wait_ge(pool_done, pool.at(now, "vexp"))
                for n, bank in enumerate((ps_a, ps_b)):
                    nc.tensor.matmul(bank[:, :], k_tok[0:NS, NC, :], v_exp[:, 4 * n:4 * n + 4, :].rearrange("p b v -> p (b v)"),
                                     start=True, stop=True).then_inc(pe_done, pe.tick(now, f"us{n}"))
                gate_slot(2, "sf", (act_done, act), 2)
                gate_slot(3, "q", (dve_done, dve), 0)
                t.wait_ge(act_done, act.at(now, "sqs"))
                t.wait_ge(dve_done, dve.at(now, "so1"))
                t.wait_ge(dve_done, dve.at(now, "gates"))
                nc.tensor.matmul(ps_a[:, :], mean_m[:, :], dq[:, half(0)], start=True, stop=True).then_inc(pe_done, pe.tick(now, "ms0"))
                nc.tensor.matmul(ps_b[:, :], mean_m[:, :], dq[:, half(1)], start=True, stop=True).then_inc(pe_done, pe.tick(now, "ms1"))
                nc.tensor.matmul(ps_d[:, 64:64 + NS], mean_m[:, :], dq[:, SEQ:T], start=True, stop=True).then_inc(pe_done, pe.tick(now, "mss"))
                gate_slot(3, "q", (dve_done, dve), 1)
                gate_slot(3, "q", (dve_done, dve), 2)

            head(0)
            with nc.tensor.Fori(1, HEADS - 1) as i:
                head(i)
            head(HEADS - 1)

            with nc.tensor.Fori(0, HEADS) as j:
                B = Blocks(GA, 2, j)
                for g in range(SLOTS):
                    t.wait_ge(dve_done, dve.at(("pa", j - 1), f"m{g}"))
                    slot(B(0), g)
                for g in range(SLOTS):
                    t.wait_ge(act_done, act.at(("pa", j), f"sg{g}"))
                    if g == 0:
                        t.wait_ge(dve_done, dve.at(("split_a", 0), "l7"))
                    slot(B(1), g, hl_h, hl_l)

            kv, here = Blocks(KV, 2, 0), ("kv", 0)
            for g in range(SLOTS):
                t.wait_ge(dve_done, dve.at(("pa", HEADS - 1), f"m{g}"))
                slot(kv(0), g)
            for g in range(SLOTS):
                t.wait_ge(act_done, act.at(here, f"k{g}"))
                slot(kv(1), g)
            t.wait_ge(act_done, act.at(here, "v2"))
            for n, bank in enumerate((ps_a, ps_b)):
                for j in range(4):
                    c = 4 * n + j
                    mm = nc.tensor.transpose(bank[:, j * P:(j + 1) * P], zb[:, c * P:(c + 1) * P], ident[:, :])
                mm.then_inc(pe_done, pe.tick(here, f"vt{n}"))
            nc.tensor.transpose(ps_c[0:NS, 0:P], zb[:, SEQ:T], ident[:, :]).then_inc(pe_done, pe.tick(here, "vts"))
            nc.tensor.transpose(ps_d[:, 0:P], kT[:, SEQ - P:SEQ], ident[:, :])
            nc.tensor.transpose(ps_d[0:NS, P:2 * P], kT[:, SEQ:T], ident[:, :]).then_inc(pe_done, pe.tick(here, "kt"))
            for g in range(SLOTS):
                slot(kv(2), g)
            for g in range(SLOTS):
                t.wait_ge(act_done, act.at(here, f"q{g}"))
                slot(kv(3), g)

            def pair(m):
                B, now = Blocks(QZ, 2, m), pair_of(m)
                prev = ("swa", m - 1)
                last = is_last(m)
                z_prev = lambda g: dve.at(("kv", 0), f"z{g}") if isinstance(m, int) and m == 0 else dve.at(prev, f"z{g}")
                t.wait_ge(dve_done, z_prev(2))
                for n in range(NC):
                    if n >= 4 and n % 2 == 0:
                        t.wait_ge(dve_done, dve.at(now, f"t{2 * (n - 4) + 3}"))
                    for h in range(2):
                        bank, o = score_bank(n, h)
                        rows_h = slice(h * HD, (h + 1) * HD)
                        lo = P if n == 0 else 0
                        mm = nc.tensor.matmul(bank[:, o + lo:o + 2 * P], qT[rows_h, n * P:(n + 1) * P],
                                              kT[rows_h, (n - 1) * P + lo:(n + 1) * P], start=True, stop=True)
                    mm.then_inc(pe_done, pe.tick(now, f"s{n}"))
                if not last:
                    for g in range(SLOTS):
                        slot(B(2), g)

                def turn(n):
                    bank = (ps_a, ps_b, ps_c)[n % 3]
                    t.wait_ge(dve_done, dve.at(now, f"n{2 * n + 1}"))
                    if n >= 3:
                        if n % 2:
                            t.wait_ge(act_done, act.at(now, f"pt{n - 3}"))
                        else:
                            t.wait_ge(dve_done, dve.at(now, f"pt{n - 3}"))
                    for h in range(2):
                        for w in range(1 if n == 0 else 0, 2):
                            o = (2 * h + w) * P
                            mm = nc.tensor.transpose(bank[:, o:o + P], scores[:, 2 * n + h, w * P:(w + 1) * P], ident[:, :])
                    mm.then_inc(pe_done, pe.tick(now, f"t{n}"))

                def out(n):
                    bank, o = (ps_d, ps_e)[n // 4], (n % 4) * P
                    if n % 2:
                        t.wait_ge(dve_done, dve.at(now, f"pt{n}"))
                    else:
                        t.wait_ge(act_done, act.at(now, f"pt{n}"))
                    for h in range(2):
                        rows_h = slice(h * HD, (h + 1) * HD)
                        for w in range(1 if n == 0 else 0, 2):
                            mm = nc.tensor.matmul(bank[rows_h, o:o + P], v_tk[:, n - 1 + w, rows_h], PT[:, n % 3, 2 * h + w, :],
                                                  start=(w == 0 or n == 0), stop=(w == 1))
                    mm.then_inc(pe_done, pe.tick(now, f"o{n}"))

                for n in range(3):
                    turn(n)
                for n in range(NC):
                    out(n)
                    if n + 3 < NC:
                        turn(n + 3)
                if not last:
                    for g in range(SLOTS):
                        t.wait_ge(act_done, act.at(now, f"q{g}"))
                        slot(B(3), g)

            with nc.tensor.Fori(0, HEADS - 1) as m:
                pair(m)
            pair(HEADS - 1)

            here = ("swa_s", 0)
            t.wait_ge(caches_loaded, 32)
            t.wait_ge(dve_done, dve.at(("swa_l", 0), "h1"))
            for n, bank in enumerate((ps_a, ps_b)):
                for j in range(4):
                    mm = nc.tensor.transpose(bank[:, j * P:(j + 1) * P], ck[:, 4 * n + j, :], ident[:, :])
                mm.then_inc(pe_done, pe.tick(here, f"ct{n}"))
            t.wait_ge(act_done, act.at(here, "ct0"))
            t.wait_ge(dve_done, dve.at(here, "ct1"))
            for u in range(4):
                h, grp = u // 2, u % 2
                rows_h = slice(h * HD, (h + 1) * HD)
                bank, o = (ps_c, ps_d)[h], grp * 2 * P
                for j in range(4):
                    m = 4 * grp + j
                    q_m = q_s[rows_h, m, :, :].rearrange("p g t -> p (g t)")
                    nc.tensor.matmul(bank[32 * j:32 * j + 32, o:o + P], q_m, ckT[rows_h, m, :], start=True, stop=True)
                    mm = nc.tensor.matmul(bank[32 * j:32 * j + 32, o + P:o + P + NS], q_m, kT[rows_h, SEQ:T], start=True, stop=True)
                mm.then_inc(pe_done, pe.tick(here, f"s{u}"))
            t.wait_ge(dve_done, dve.at(here, "n3"))
            for u in range(4):
                mm = nc.tensor.transpose(ps_a[:, u * P:(u + 1) * P], sc_s[:, u, 0:P], ident[:, :])
            mm.then_inc(pe_done, pe.tick(here, "pt"))
            for u in range(4):
                mm = nc.tensor.transpose(ps_b[0:NS, u * P:(u + 1) * P], sc_s[:, u, P:P + NS], ident[:, :])
            mm.then_inc(pe_done, pe.tick(here, "pn"))
            t.wait_ge(act_done, act.at(here, "pt"))
            t.wait_ge(dve_done, dve.at(here, "pn"))
            for u in range(4):
                h, grp = u // 2, u % 2
                rows_h = slice(h * HD, (h + 1) * HD)
                nc.tensor.matmul(ps_e[rows_h, grp * P:(grp + 1) * P], v_tk[0:NS, NC, rows_h], PT_n[:, u, :], start=True, stop=True)
                for j in range(4):
                    o = grp * P + 32 * j
                    mm = nc.tensor.matmul(ps_e[rows_h, o:o + 32], cv[:, 4 * grp + j, rows_h], PT_s[:, u, 32 * j:32 * j + 32],
                                          start=False, stop=True, skip_group_check=True)
            mm.then_inc(pe_done, pe.tick(here, "o"))

            with nc.tensor.Fori(0, 4) as j:
                B = Blocks(GB, 2, j)
                for m in range(2):
                    for g in range(SLOTS):
                        t.wait_ge(act_done, act.at(("gb", j), f"g{3 * m + g}") - SLOTS)
                        slot(B(m), g)
            t.wait_ge(dve_done, dve.at(("split_b", 0), "l7"))
            with nc.tensor.Fori(0, 4) as j:
                B = Blocks(PB, 2, j)
                for m in range(2):
                    for g in range(SLOTS):
                        t.wait_ge(dve_done, dve.at(("pb", j), f"g{3 * m + g}") - 2 * SLOTS)
                        if m == 0:
                            t.wait_ge(act_done, act.at(("gb", 3), f"g{3 + g}"))
                        slot(B(m), g)
            here = ("out", 0)
            t.wait_ge(dve_done, dve.at(("split_m", 0), "l7"))
            for n in range(NC + 1):
                r = P if n < NC else NS
                cols = slice(n * P, n * P + r)
                for m in range(2):
                    if n == 0:
                        t.wait_ge(wo_lo_ready, 4 * (m + 1))
                    if n >= 4:
                        t.wait_ge(dve_done, dve.at(here, f"y{'ab'[m]}{n - 4}"))
                    bank = bank_of(n, m)
                    passes = ((xn_h, wo_h[m]), (xn_h, wo_l[m]), (xn_l, wo_h[m]))
                    for kt in range(KT):
                        for i, (x, w) in enumerate(passes):
                            mm = nc.tensor.matmul(bank[0:r, :], x[:, kt, cols], w[:, kt, :],
                                                  start=(kt == 0 and i == 0), stop=(kt == KT - 1 and i == 2))
                    mm.then_inc(pe_done, pe.tick(here, f"{'ab'[m]}{n}"))

        @block.vector
        def _(v):
            pr = ("pro", 0)
            tt = nc.vector.tensor_tensor
            v.wait_ge(pe_done, pe.at(pr, "par"))
            v.tensor_copy(par[:, 0:17], ps_e[:, 0:17]).then_inc(dve_done, dve.tick(pr, "par"))
            v.wait_ge(dve_done, dve.at(pr, "par"))
            tt(lbt[:, 2, :], par[:, 0:8], par[:, 8:16], ALU.max).then_inc(dve_done, dve.tick(pr, "lbm"))
            v.wait_ge(dve_done, dve.at(pr, "lbm"))
            tt(lbt[:, 0, :], par[:, 0:8], lbt[:, 2, :], ALU.subtract).then_inc(dve_done, dve.tick(pr, "lbd0"))
            tt(lbt[:, 1, :], par[:, 8:16], lbt[:, 2, :], ALU.subtract).then_inc(dve_done, dve.tick(pr, "lbd1"))
            v.wait_ge(act_done, act.at(pr, "lb1"))
            tt(lbt[:, 2, :], lbt[:, 0, :], lbt[:, 1, :], ALU.add).then_inc(dve_done, dve.tick(pr, "lbs"))
            v.wait_ge(dve_done, dve.at(pr, "lbs"))
            v.reciprocal(lbt[:, 2, :], lbt[:, 2, :]).then_inc(dve_done, dve.tick(pr, "lbr"))
            v.wait_ge(dve_done, dve.at(pr, "lbr"))
            tt(lb[:], lbt[:, 0, :], lbt[:, 2, :], ALU.mult).then_inc(dve_done, dve.tick(pr, "lb"))
            v.wait_ge(dve_done, dve.at(pr, "lb"))
            v.tensor_scalar(oml[:], lb[:], -1.0, 1.0, ALU.mult, ALU.add).then_inc(dve_done, dve.tick(pr, "oml"))
            v.tensor_scalar(noml[:], lb[:], 1.0, -1.0, ALU.mult, ALU.add).then_inc(dve_done, dve.tick(pr, "noml"))
            v.memset(mean_m[:], 1.0 / P).then_inc(dve_done, dve.tick(pr, "ones"))
            for t in range(NC + 1):
                r = P if t < NC else NS
                if t == 0:
                    v.wait_ge(g_loaded, 16)
                v.wait_ge(act_done, act.at(pr, f"rstd{t}"))
                if t >= 2:
                    v.wait_ge(pe_done, pe.at(pr, f"xb{t - 2}"))
                v.scalar_tensor_tensor(out=x_n[t % 2][0:r, :], in0=x_t[t % 3][0:r, :], scalar=rstd[0:r, 1, t:t + 1], in1=g_row[0:r, :],
                                       op0=ALU.mult, op1=ALU.mult).then_inc(dve_done, dve.tick(pr, f"xn{t}"))
                for n, (bank, s) in enumerate((((ps_a, ps_c)[t % 2], "a"), ((ps_b, ps_d)[t % 2], "b"))):
                    v.wait_ge(act_done, act.at(pr, f"hi_{s}{t}"))
                    tt(xn_l[:, 4 * n:4 * n + 4, t * P:t * P + r], bank[:].rearrange("p (k t) -> p k t", k=4)[:, :, 0:r],
                       xn_h[:, 4 * n:4 * n + 4, t * P:t * P + r].bitcast(F32), ALU.subtract).then_inc(dve_done, dve.tick(pr, f"lo_{s}{t}"))
            v.wait_ge(pe_done, pe.at(pr, f"xb{NC}"))
            v.memset(att[:], 0.0).then_inc(dve_done, dve.tick(pr, "att0"))
            v.memset(att_s[:], 0.0).then_inc(dve_done, dve.tick(pr, "atts0"))
            v.memset(reset[:], 1.0).then_inc(dve_done, dve.tick(pr, "reset"))
            v.wait_ge(dve_done, dve.at(pr, "reset"))
            v.memset(reset[:, 0:SEQ:P], 0.0).then_inc(dve_done, dve.tick(pr, "reset_p"))
            v.memset(reset[:, SEQ:T:DEC], 0.0).then_inc(dve_done, dve.tick(pr, "reset_s"))

            def gated(where, name, g, out):
                v.wait_ge(act_done, act.at(where, f"{'sigq' if name == 'q' else 'sigz'}{g}"))
                tt(out[:, span(g)], out[:, span(g)], pj[g][:, 0:W], ALU.mult).then_inc(dve_done, dve.tick(where, f"{name}{g}"))

            for g in range(SLOTS):
                gated(pr, "q", g, q)
            for g in range(SLOTS):
                gated(pr, "z", g, zs)

            def head(i):
                now = now_of(i)
                prev = prev_of(i)
                last = is_last(i)

                def need(steps, sem_, name):
                    v.wait_ge(sem_, steps.at(now, name))

                def done(name):
                    return dve.tick(now, name)

                if not is_first(i):
                    need(act, act_done, "rx")
                    tt(ha[:, bass.ds(i - 1, 1), :], ha[:, bass.ds(i - 1, 1), :], rs[:].rearrange("p (o t) -> p o t", o=1), ALU.mult).then_inc(dve_done, done("ha"))
                need(act, act_done, "lnf")
                v.tensor_scalar(k[:], k[:], noml[:, bass.ds(i, 1)], oml[:, bass.ds(i, 1)], ALU.mult, ALU.add).then_inc(dve_done, done("kf"))
                if is_first(i):
                    v.wait_ge(dve_done, dve.at(pr, "reset_s"))
                v.tensor_tensor_scan(b[:], reset[:], b[:], 0.0, ALU.mult, ALU.add).then_inc(dve_done, done("scan"))
                need(dve, dve_done, "scan")
                bc = chunks(b[:, 0:SEQ])
                bs = b[:, SEQ:T].rearrange("p (b t) -> p b t", b=NB)
                tt(chunks(kD[:, 0:SEQ]), bc[:, :, P - 1:P].to_broadcast([P, NC, P]), bc, ALU.subtract).then_inc(dve_done, done("kDa"))
                tt(kD[:, SEQ:T].rearrange("p (b t) -> p b t", b=NB), bs[:, :, DEC - 1:DEC].to_broadcast([P, NB, DEC]), bs, ALU.subtract).then_inc(dve_done, done("kDs"))
                for h, d in ((64, d64), (32, d32)):
                    n = SEQ // (2 * h)
                    bh = b[:, 0:SEQ].rearrange("p (c s t) -> p c s t", s=2, t=h)
                    mid = bh[:, :, 0, h - 1:h].to_broadcast([P, n, h])
                    tt(d[:, :, 1, :], bh[:, :, 1, :], mid, ALU.subtract).then_inc(dve_done, done(f"a{h}q"))
                    tt(d[:, :, 0, :], mid, bh[:, :, 0, :], ALU.subtract).then_inc(dve_done, done(f"a{h}k"))
                bd = b[:, 0:SEQ].rearrange("p (c t) -> p c t", t=32)
                tt(cs[:, 0:32].rearrange("p (c o) -> p c o", o=1), bd[:, :, 0:1], bd[:, :, 31:32], ALU.add).then_inc(dve_done, done("cs"))
                tt(cs[:, 32:40].rearrange("p (c o) -> p c o", o=1), bs[:, :, 0:1], bs[:, :, DEC - 1:DEC], ALU.add).then_inc(dve_done, done("css"))
                need(dve, dve_done, "css")
                v.scalar_tensor_tensor(out=dk[:, 0:SEQ].rearrange("p (c t) -> p c t", t=32), in0=cs[:, 0:32].rearrange("p (c o) -> p c o", o=1).to_broadcast([P, 32, 32]),
                                       scalar=0.5, in1=bd, op0=ALU.mult, op1=ALU.subtract).then_inc(dve_done, done("xa"))
                v.scalar_tensor_tensor(out=dk[:, SEQ:T].rearrange("p (c t) -> p c t", t=DEC), in0=cs[:, 32:40].rearrange("p (c o) -> p c o", o=1).to_broadcast([P, NB, DEC]),
                                       scalar=0.5, in1=bs, op0=ALU.mult, op1=ALU.subtract).then_inc(dve_done, done("xas"))
                need(dve, dve_done, "xas")
                v.tensor_scalar(dk[:], dk[:], CLAMP, -CLAMP, ALU.min, ALU.max).then_inc(dve_done, done("xc"))
                need(act, act_done, "xkD")
                tt(kD[:], kD[:], k[:], ALU.mult).then_inc(dve_done, done("kD"))
                for h, d in ((64, d64), (32, d32)):
                    need(act, act_done, f"x{h}")
                    tt(d[:, :, 1, :], d[:, :, 1, :], q[:, 0:SEQ].rearrange("p (c s t) -> p c s t", s=2, t=h)[:, :, 1, :], ALU.mult).then_inc(dve_done, done(f"m{h}q"))
                    tt(d[:, :, 0, :], d[:, :, 0, :], k[:, 0:SEQ].rearrange("p (c s t) -> p c s t", s=2, t=h)[:, :, 0, :], ALU.mult).then_inc(dve_done, done(f"m{h}k"))
                need(act, act_done, "xdk")
                tt(dq[:], dq[:], q[:], ALU.mult).then_inc(dve_done, done("dqm"))
                tt(dk[:], dk[:], k[:], ALU.mult).then_inc(dve_done, done("dkm"))
                need(act, act_done, "xqI")
                tt(qI[:], qI[:], q[:], ALU.mult).then_inc(dve_done, done("qIm"))
                for n, bank in enumerate((ps_c, ps_d)):
                    need(pe, pe_done, f"kt{n}")
                    v.tensor_copy(k_tok[:, 4 * n:4 * n + 4, :], bank[:].rearrange("p (c v) -> p c v", c=4)).then_inc(dve_done, done(f"kt{n}"))
                need(pe, pe_done, "kts")
                v.tensor_copy(k_tok[0:NS, NC, :], ps_e[0:NS, P:2 * P]).then_inc(dve_done, done("kts"))
                for c in range(NC):
                    u = (ps_c, ps_d)[c // 4][:, (c % 4) * P:(c % 4 + 1) * P]
                    if c % 4 == 0:
                        need(pe, pe_done, f"u{c // 4}")
                    if c == 0:
                        v.tensor_copy(S[:, 0, :], u).then_inc(dve_done, done("s1"))
                        continue
                    need(dve, dve_done, f"s{c}")
                    if c == NC - 1:
                        need(pe, pe_done, "ps")
                    if c == NC - 1 and not is_first(i):
                        v.wait_ge(sp_stored, i * 16)
                    v.scalar_tensor_tensor(out=S[:, c, :], in0=S[:, c - 1, :], scalar=E[:, c:c + 1], in1=u,
                                           op0=ALU.mult, op1=ALU.add).then_inc(dve_done, done(f"s{c + 1}"))
                if is_first(i):
                    v.wait_ge(masks_loaded, 48)
                for n, bank in enumerate((ps_a, ps_b)):
                    v.copy_predicated(att[:, 4 * n:4 * n + 4, :], causal[:].rearrange("p (o t) -> p o t", o=1).to_broadcast([P, 4, P]),
                                      bank[:].rearrange("p (c t) -> p c t", c=4)).then_inc(dve_done, done(f"att{n}"))
                v.copy_predicated(att_s[:], causal_s[:], ps_e[0:NS, 256:256 + NS]).then_inc(dve_done, done("atts"))

                def gate(name, squared, bank, cols, src):
                    need(act, act_done, squared)
                    v.scalar_tensor_tensor(out=ha[:, bass.ds(i, 1), cols], in0=bank[:, src].rearrange("p (o t) -> p o t", o=1), scalar=par[:, 16:17],
                                           in1=zs[:, cols].rearrange("p (o t) -> p o t", o=1), op0=ALU.mult, op1=ALU.mult).then_inc(dve_done, done(name))

                if not last:
                    gated(now, "q", 0, q)
                gate("gate0", "sq0", ps_e, half(0), slice(0, 512))
                gate("gate1", "sq1", ps_c, half(1), slice(0, 512))
                gate("gates", "sqs", ps_d, slice(SEQ, T), slice(0, NS))
                if not last:
                    gated(now, "q", 1, q)
                need(pool, pool_done, "s0e")
                for n, bank in enumerate((ps_a, ps_b)):
                    need(pe, pe_done, f"us{n}")
                    tt(s0[:, 4 * n:4 * n + 4, :], s0[:, 4 * n:4 * n + 4, :], bank[:].rearrange("p (b v) -> p b v", b=4), ALU.add).then_inc(dve_done, done(f"so{n}"))
                if last:
                    need(act, act_done, "fx")
                    tt(ha[:, i, :], ha[:, i, :], rs[:], ALU.mult).then_inc(dve_done, done("hal"))
                    return
                gated(now, "q", 2, q)
                for g in range(SLOTS):
                    gated(now, "z", g, zs)

            head(0)
            with nc.vector.Fori(1, HEADS - 1) as i:
                head(i)
            head(HEADS - 1)

            def split_rows(phase, src, hi, lo):
                for n in range(KT):
                    v.wait_ge(act_done, act.at((phase, 0), f"h{n}"))
                    tt(lo[:, n, :], src[:, n, :], hi[:, n, :].bitcast(F32), ALU.subtract).then_inc(dve_done, dve.tick((phase, 0), f"l{n}"))

            split_rows("split_a", ha, hl_h, hl_l)
            one = lambda a: a.rearrange("p (o t) -> p o t", o=1)
            with nc.vector.Fori(0, HEADS) as j:
                B = Blocks(GA, 2, j)
                for g in range(SLOTS):
                    v.wait_ge(act_done, act.at(("pa", j), f"sg{g}"))
                    v.wait_ge(slot_done, B(1)[0] * 3 + (g + 1))
                    tt(mg[:, bass.ds(j, 1), span(g)], one(sg[:, span(g)]), one(pj[g][:, 0:W]), ALU.mult).then_inc(dve_done, dve.tick(("pa", j), f"m{g}"))

            here = ("kv", 0)
            v.wait_ge(slopes_loaded, 64)
            for h in range(2):
                v.tensor_tensor_reduce(out=bias[:, h, 0:8], in0=sinks[:, 8 * h:8 * h + 8], in1=pick[:], scale=1.0, scalar=0.0,
                                       op0=ALU.mult, op1=ALU.add, accum_out=sinks_s[:, h:h + 1]).then_inc(dve_done, dve.tick(here, f"sel{h}"))
            v.wait_ge(pe_done, pe.at(here, "vt1"))
            v.tensor_copy(v_tk[:, 4:8, :], ps_b[:].rearrange("p (c v) -> p c v", c=4)).then_inc(dve_done, dve.tick(here, "vt1"))
            for g in range(SLOTS):
                gated(here, "z", g, zb)

            def negate(now, k, new, old, sink, scores_next=len(quarters)):
                v.tensor_scalar(new(0), old(0), sink(0), -1.0, ALU.max, ALU.mult).then_inc(dve_done, dve.tick(now, f"nm0_{k}"))
                if scores_next < len(quarters):
                    v.wait_ge(pe_done, pe.at(now, f"s{2 * scores_next + 1}"))
                v.tensor_scalar(new(1), old(1), sink(1), -1.0, ALU.max, ALU.mult).then_inc(dve_done, dve.tick(now, f"nm1_{k}"))

            def normalise(now, k, st, first, last, target, keys):
                v.wait_ge(act_done, act.at(now, f"p{last - 1}"))
                tt(st[:, 3, first:last], st[:, 3, first:last], st[:, 2, first:last], ALU.add).then_inc(dve_done, dve.tick(now, f"dn{k}"))
                v.wait_ge(dve_done, dve.at(now, f"dn{k}"))
                v.reciprocal(st[:, 4, first:last], st[:, 3, first:last]).then_inc(dve_done, dve.tick(now, f"rd{k}"))
                v.wait_ge(dve_done, dve.at(now, f"rd{k}"))
                for u in range(first, last):
                    v.tensor_scalar(target[:, u, keys(u)], target[:, u, keys(u)], st[:, 4, u:u + 1], None, ALU.mult).then_inc(dve_done, dve.tick(now, f"n{u}"))

            def pair(m):
                now = pair_of(m)
                last = is_last(m)
                keys = lambda u: slice(P if u < 2 else 0, 2 * P)
                v.wait_ge(pe_done, pe.at(now, "s1"))
                for h in range(2):
                    v.tensor_scalar(bias[:, h, :], dist[:], slopes[:, bass.ds(m + 8 * h, 1)], None, ALU.mult).then_inc(dve_done, dve.tick(now, f"b{h}"))
                def biased(u):
                    n, h = u // 2, u % 2
                    (bank, o), lo = score_bank(n, h), P if n == 0 else 0
                    v.tensor_tensor_reduce(out=scores[:, u, lo:2 * P], in0=bank[:, o + lo:o + 2 * P], in1=bias[:, h, lo:2 * P],
                                           scale=1.0, scalar=-3e38, op0=ALU.add, op1=ALU.max,
                                           accum_out=stat[:, 0, u:u + 1]).then_inc(dve_done, dve.tick(now, f"t{u}"))

                v.tensor_copy(sink_m[:].rearrange("p (h m) -> p h m", h=2), sinks[:].rearrange("p (h m) -> p h m", h=2)[:, :, bass.ds(m, 1)])\
                 .then_inc(dve_done, dve.tick(now, "sk"))
                v.wait_ge(dve_done, dve.at(now, "b1"))
                v.tensor_copy(q_s[:, :, bass.ds(m, 1), :], qT[:, SEQ:T].rearrange("p (b o t) -> p b o t", b=NB, o=1)).then_inc(dve_done, dve.tick(now, "qs"))
                for k in quarters:
                    for u in range(QU * k, QU * (k + 1)):
                        biased(u)
                    v.wait_ge(dve_done, dve.at(now, f"t{QU * k + QU - 1}"))
                    negate(now, k, lambda h: by_head(stat[:, 1, :], k)[:, h, :], lambda h: by_head(stat[:, 0, :], k)[:, h, :],
                           lambda h: sink_m[:, h:h + 1], scores_next=k + 1)
                v.tensor_copy(z_s[:, bass.ds(m, 1), :], one(zb[:, SEQ:T])).then_inc(dve_done, dve.tick(now, "zs"))
                for k in quarters:
                    normalise(now, k, stat, QU * k, QU * (k + 1), scores, keys)
                for n in range(1, NC, 2):
                    v.wait_ge(pe_done, pe.at(now, f"t{n}"))
                    if n >= 3:
                        v.wait_ge(pe_done, pe.at(now, f"o{n - 3}"))
                    src = (ps_a, ps_b, ps_c)[n % 3]
                    v.tensor_copy(PT[:, n % 3, :, :].rearrange("p a q -> p (a q)"), src[:]).then_inc(dve_done, dve.tick(now, f"pt{n}"))
                for n, bank in enumerate((ps_d, ps_e)):
                    v.wait_ge(pe_done, pe.at(now, f"o{4 * n + 3}"))
                    tt(hb[:, bass.ds(m, 1), half(n)], one(bank[:]), one(zb[:, half(n)]), ALU.mult).then_inc(dve_done, dve.tick(now, f"h{n}"))
                if not last:
                    for g in range(SLOTS):
                        gated(now, "z", g, zb)

            with nc.vector.Fori(0, HEADS - 1) as m:
                pair(m)
            pair(HEADS - 1)

            here = ("swa_s", 0)
            v.wait_ge(pe_done, pe.at(here, "ct1"))
            v.tensor_copy(ckT[:, 4:8, :], ps_b[:].rearrange("p (c v) -> p c v", c=4)).then_inc(dve_done, dve.tick(here, "ct1"))
            v.wait_ge(bias_s_loaded, 16)
            for u in range(4):
                bank, o = (ps_c, ps_d)[u // 2], (u % 2) * 2 * P
                v.wait_ge(pe_done, pe.at(here, f"s{u | 1}"))
                v.tensor_tensor_reduce(out=sc_s[:, u, :], in0=bank[:, o:o + P + NS], in1=bias_s[:, u, :], scale=1.0, scalar=-3e38,
                                       op0=ALU.add, op1=ALU.max, accum_out=stat_s[:, 0, u:u + 1]).then_inc(dve_done, dve.tick(here, f"t{u}"))
            v.wait_ge(dve_done, dve.at(here, "t3"))
            negate(here, 0, lambda h: stat_s[:, 1, 2 * h:2 * h + 2], lambda h: stat_s[:, 0, 2 * h:2 * h + 2], lambda h: sinks_s[:, h:h + 1])
            normalise(here, 0, stat_s, 0, 4, sc_s, lambda u: slice(0, P + NS))
            v.wait_ge(pe_done, pe.at(here, "pn"))
            v.tensor_copy(PT_n.rearrange("p a q -> p (a q)"), ps_b[0:NS, :]).then_inc(dve_done, dve.tick(here, "pn"))
            v.wait_ge(pe_done, pe.at(here, "o"))
            for_g = lambda a: a.rearrange("p g (b t) -> p g b t", t=DEC)
            tt(for_g(hb[:, :, SEQ:T]), ps_e[:, 0:2 * P].rearrange("p (b g t) -> p g b t", b=NB, g=HEADS), for_g(z_s[:]), ALU.mult).then_inc(dve_done, dve.tick(here, "h"))

            split_rows("split_b", hb, xn_h, xn_l)
            with nc.vector.Fori(0, 4) as j:
                B, now = Blocks(PB, 2, j), ("pb", j)
                for m in range(2):
                    for g in range(SLOTS):
                        s_, at = 3 * m + g, bass.ds(j * 2 + m, 1)
                        v.wait_ge(slot_done, B(m)[0] * 3 + (g + 1))
                        tt(sgb[:, at, span(g)], sgb[:, at, span(g)], one(pj[g][:, 0:W]), ALU.mult).then_inc(dve_done, dve.tick(now, f"g{s_}"))
                        v.wait_ge(dve_done, dve.at(now, f"g{s_}"))
                        tt(mg[:, at, span(g)], mg[:, at, span(g)], sgb[:, at, span(g)], ALU.add).then_inc(dve_done, dve.tick(now, f"m{s_}"))
            split_rows("split_m", mg, xn_h, xn_l)
            here = ("out", 0)
            v.wait_ge(g_fin_loaded, 16)
            for t in range(NC + 1):
                r = P if t < NC else NS
                v.wait_ge(xo_loaded[t % 3], 16 * (t // 3 + 1))
                if t >= 3:
                    v.wait_ge(y_stored[t % 3], 16 * (t // 3))
                for m in range(2):
                    v.wait_ge(pe_done, pe.at(here, f"{'ab'[m]}{t}"))
                    tt(y_o[t % 3][0:r, half(m)], bank_of(t, m)[0:r, :], x_o[t % 3][0:r, half(m)], ALU.add).then_inc(dve_done, dve.tick(here, f"y{'ab'[m]}{t}"))
                v.wait_ge(act_done, act.at(here, f"rs{t}"))
                v.scalar_tensor_tensor(out=y_o[t % 3][0:r, :], in0=y_o[t % 3][0:r, :], scalar=rstd[0:r, 1, t:t + 1], in1=g_fin[0:r, :],
                                       op0=ALU.mult, op1=ALU.mult).then_inc(dve_done, dve.tick(here, f"yn{t}"))


_INS = ["x_prompt", "x_sample", "state_hgrn", "cache_k", "cache_v", "norm_in", "w_in", "lb_logits", "a_gnorm",
        "b_sinks", "w_pa", "w_pb", "w_out", "norm_final"]
_CONSTS = ["c_ident", "c_causal", "c_causal_s", "c_batch", "c_dist", "c_slopes", "c_bias_s"]
_OUTS = [(1, 1024, 1024), (8, 4, 1024), (1, 1, 8, 128, 128), (1, 1, 128, 2, 64), (1, 1, 128, 2, 64),
         (1, 8, 8, 128, 128), (1, 8, 128, 2, 64), (1, 8, 128, 2, 64)]


def shape_constants():
    import numpy as np

    s, t = np.arange(P)[:, None], np.arange(P)[None, :]
    ss, st = np.arange(NS)[:, None], np.arange(NS)[None, :]
    dist = np.arange(P)[:, None] - (np.arange(2 * P)[None, :] - P)
    slopes = np.float32(2.0) ** (np.float32(-8.0) * np.arange(1, QH + 1, dtype=np.float32) / np.float32(QH))
    row = np.arange(P)
    bias_s = np.zeros((P, 4, P + NS), np.float32)
    for u in range(4):
        slope = slopes[8 * (u // 2) + row // DEC % 8][:, None]
        batch, query = (4 * (u % 2) + row // 32)[:, None], (row % DEC)[:, None]
        old, new = query + P - np.arange(P)[None, :], query - np.arange(NS)[None, :] % DEC
        bias_s[:, u, 0:P] = np.where(old < P, -slope * old, -1e30)
        bias_s[:, u, P:] = np.where((new >= 0) & (np.arange(NS)[None, :] // DEC == batch), -slope * new, -1e30)
    return {
        "c_ident": np.eye(P, dtype=np.float32),
        "c_causal": (s <= t).astype(np.int32),
        "c_causal_s": ((ss <= st) & (ss // DEC == st // DEC)).astype(np.int32),
        "c_dist": np.where((dist >= 0) & (dist < P), -dist, OFFSET).astype(np.float32),
        "c_slopes": np.concatenate([np.broadcast_to(slopes, (P, QH)), (row // DEC % 8)[:, None] == np.arange(8)], 1).astype(np.float32),
        "c_bias_s": bias_s,
        "c_batch": (ss // DEC == np.arange(NB)[None, :]).astype(np.float32),
    }


def kernel(**inputs):
    import numpy as _np
    import concourse.bacc as _bacc
    from concourse import mybir as _mybir
    from concourse.bass_utils import run_bass_kernel_spmd as _run

    nc = _bacc.Bacc("TRN2", target_bir_lowering=False, num_devices=1)
    constants = shape_constants()
    arrays, args = {}, []
    for name, a in [(n, inputs[n]) for n in _INS] + [(n, constants[n]) for n in _CONSTS]:
        a = _np.ascontiguousarray(a)
        arrays[f"in_{name}_dram"] = a
        args.append(nc.dram_tensor(f"in_{name}_dram", a.shape, _mybir.dt.from_np(a.dtype), kind="ExternalInput").ap())
    for i, shape in enumerate(_OUTS):
        args.append(nc.dram_tensor(f"out_{i}_dram", shape, _mybir.dt.float32, kind="ExternalOutput").ap())
    hybrid_step(nc, *args)
    r = _run(nc, [arrays], core_ids=[0])
    return tuple(r.results[0][f"out_{i}_dram"] for i in range(len(_OUTS)))
```

```python
from contextlib import ExitStack

import concourse.bass as bass
from concourse import mybir

F32 = mybir.dt.float32
F32R = mybir.dt.float32r
I32 = mybir.dt.int32
ALU = mybir.AluOpType
ACT = mybir.ActivationFunctionType

P = 128
D = 1024
KT = D // P
SEQ = 1024
NB, DEC = 8, 4
NS = NB * DEC
T = SEQ + NS
NC = SEQ // P
SLOTS = 3
W = T // SLOTS
HEADS = 8
QH, HD = 16, 64
EPS = 1e-6
QU = 4
OFFSET = -1e33
CLAMP = 85.0
OFF = dict(q=0, f=1024, i=2048, z=3072, qb=4096, kb=5120, vb=5248, zb=5376, ga=6400, gb=7424)


class Steps:

    def __init__(self, order):
        self.base, self.names, self.now, total = {}, {}, {}, 0
        for phase, names, rounds, skip in order:
            assert len(set(names)) == len(names), phase
            self.base[phase], self.names[phase], self.now[phase] = total - skip, names, skip
            total += len(names) * rounds - skip

    def at(self, where, step):
        phase, i = where
        return i * len(self.names[phase]) + (self.base[phase] + self.names[phase].index(step) + 1)

    def tick(self, where, step):
        phase = where[0]
        want = self.names[phase][self.now[phase] % len(self.names[phase])]
        assert want == step, f"{phase}: {step} stands where {want} is due"
        self.now[phase] += 1
        return 1


class Blocks:

    def __init__(self, first, per, i):
        self.first, self.per, self.i = first, per, i

    def __call__(self, k):
        return (self.i * self.per + (self.first + k), (self.first + k) % 2,
                self.i * (self.per // 2) + (self.first + k) // 2)


def hybrid_step(nc, x_prompt, x_sample, state_hgrn, cache_k, cache_v, norm_in, w_in, lb_logits, a_gnorm,
                b_sinks, w_pa, w_pb, w_out, norm_final, c_ident, c_causal, c_causal_s, c_batch,
                c_dist, c_slopes, c_bias_s,
                y_prompt, y_sample, st_prompt, ck_prompt, cv_prompt, st_sample, ck_sample, cv_sample):
    per_tile = lambda first, second: [f"{s}{t - d}" for t in range(NC + 2) for d, names in ((0, first), (1, second))
                                      for s in names if 0 <= t - d <= NC]
    next_head = lambda s: [s + "0", s + "1", s + "2"]
    turn_order = ["t0", "t1", "t2"] + [x for n in range(8) for x in ([f"o{n}"] + ([f"t{n + 3}"] if n < 5 else []))]
    tiles8 = lambda s: [f"{s}{n}" for n in range(8)]
    units = lambda s, k, n=QU: [f"{s}{u}" for u in range(n * k, n * (k + 1))]
    quarters = range(2 * NC // QU)
    exps = [x for k in quarters for x in [f"es0_{k}", f"es1_{k}"] + units("p", k)]
    softmax = (["b0", "b1", "sk", "qs"] + [x for k in quarters for x in units("t", k) + [f"nm0_{k}", f"nm1_{k}"]] + ["zs"]
               + [x for k in quarters for x in [f"dn{k}", f"rd{k}"] + units("n", k)])
    out_order = [f"{s}{t}" for s in "ab" for t in range(4)] + [f"{s}{t}" for t in range(4, NC + 1) for s in "ab"]
    norms = ["rl0", "rl1", "rls", "rx"]
    exponentials = ["v0", "ebl", "ebs", "xkD", "v1", "x64", "x32", "v2", "xdq", "xdk", "xqI"]
    turned = ["vt0", "vt1", "vts"]
    act = Steps([
        ("pro", ["lb0", "lb1"] + per_tile(["ss", "ln", "rstd"], ["hi_a", "hi_b"]) + next_head("sf") + ["lnf"] + next_head("sigq") + next_head("sigz"), 1, 0),
        ("head", norms + exponentials + turned + next_head("sf")
         + ["lnf", "sigq0", "sq0", "sq1", "sqs", "sigq1", "sigq2"] + next_head("sigz"), HEADS - 1, len(norms)),
        ("last", norms + exponentials + turned + [f"k{g}{h}" for g in range(SLOTS) for h in "ab"] + ["sq0", "sq1", "sqs", "fl0", "fl1", "fls", "fx"] + next_head("sg"), 1, 0),
        ("split_a", tiles8("h"), 1, 0),
        ("pa", next_head("sg"), HEADS - 1, 0),
        ("kv", next_head("v") + next_head("q") + ["vt0", "vts", "kt", "ks"] + next_head("sigz"), 1, 0),
        ("swa", exps + ["q0", "q1", "pt0", "q2", "pt2", "pt4", "pt6"] + next_head("sigz"), HEADS - 1, 0),
        ("swa_l", exps + [f"pt{n}" for n in range(0, NC, 2)], 1, 0),
        ("swa_s", ["g0", "g1", "g2", "ct0", "es0_0", "es1_0"] + [f"p{u}" for u in range(4)] + ["pt", "g3", "g4", "g5"], 1, 0),
        ("gb", [f"g{n}" for n in range(6)], HEADS // 2 - 1, 0),
        ("split_b", tiles8("h"), 1, 0),
        ("split_m", tiles8("h"), 1, 0),
        ("out", [f"{s}{t}" for t in range(NC + 1) for s in ("ss", "ln", "rs")], 1, 0),
    ])
    exponents = ["kf", "scan", "kDa", "kDs", "a64q", "a64k", "a32q", "a32k", "cs", "css", "xa", "xas", "xc"]
    products = ["kD", "m64q", "m64k", "m32q", "m32k", "dqm", "dkm", "qIm", "kt0", "kt1", "kts"]
    chain = [f"s{c}" for c in range(1, NC + 1)]
    dve = Steps([
        ("pro", ["par", "lbm", "lbd0", "lbd1", "lbs", "lbr", "lb", "oml", "noml", "ones"]
         + per_tile(["xn"], ["lo_a", "lo_b"]) + ["att0", "atts0", "zkT0", "zkT1", "zk_a", "zk_b", "zv_a", "zv_b", "reset", "reset_p", "reset_s"] + exponents + next_head("q") + next_head("z"), 1, 0),
        ("head", ["ha"] + products + chain + ["att0", "att1", "atts"] + exponents + ["q0", "gate0", "gate1", "gates", "q1",
                  "so0", "so1", "q2", "z0", "z1", "z2"], HEADS - 1, 1),
        ("last", ["ha"] + products + chain + ["att0", "att1", "atts", "gate0", "gate1", "gates", "so0", "so1", "hal"], 1, 0),
        ("split_a", tiles8("l"), 1, 0),
        ("pa", next_head("m"), HEADS, 0),
        ("kv", ["sel0", "sel1", "vt1"] + next_head("z"), 1, 0),
        ("swa", softmax
         + [f"pt{n}" for n in range(1, NC, 2)] + ["h0", "h1"] + next_head("z"), HEADS - 1, 0),
        ("swa_l", softmax
         + [f"pt{n}" for n in range(1, NC, 2)] + ["h0", "h1"], 1, 0),
        ("swa_s", ["ct1"] + [f"t{u}" for u in range(4)] + ["nm0_0", "nm1_0", "dn0", "rd0"] + [f"n{u}" for u in range(4)] + ["pn", "h"], 1, 0),
        ("split_b", tiles8("l"), 1, 0),
        ("pb", [f"{s}{n}" for n in range(6) for s in "gm"], HEADS // 2, 0),
        ("split_m", tiles8("l"), 1, 0),
        ("out", [f"{s}{t}" for t in range(NC + 1) for s in ("ya", "yb", "yn")], 1, 0),
    ])
    pe = Steps([
        ("pro", ["par"] + [f"{s}{t}" for t in range(NC + 1) for s in ("xa", "xb")], 1, 0),
        ("head", ["vt0", "vt1", "vts", "kt0", "kt1", "kts", "p0", "p1", "ps", "u0", "u1",
                  "o0", "o1", "os", "us0", "us1", "ms0", "ms1", "mss"], HEADS - 1, 0),
        ("last", ["vt0", "vt1", "vts", "kt0", "kt1", "kts", "p0", "p1", "ps", "u0", "u1",
                  "o0", "o1", "os", "us0", "us1", "ms0", "ms1", "mss"], 1, 0),
        ("kv", ["vt0", "vt1", "vts", "kt"], 1, 0),
        ("swa", tiles8("s") + turn_order, HEADS - 1, 0),
        ("swa_l", tiles8("s") + turn_order, 1, 0),
        ("swa_s", ["ct0", "ct1", "s0", "s1", "s2", "s3", "pt", "pn", "o"], 1, 0),
        ("out", out_order, 1, 0),
    ])
    pool = Steps([
        ("pro", ["eps"], 1, 0),
        ("head", ["vexp", "s0e"], HEADS - 1, 0),
        ("last", ["vexp", "s0e"], 1, 0),
    ])

    ctx = ExitStack()
    with ctx:
        def sb(name, shape, dt=F32, where=ctx):
            return where.enter_context(nc.sbuf_tensor(name, shape, dt))

        def sem(name):
            return ctx.enter_context(nc.semaphore(name))

        pj = [ctx.enter_context(nc.psum_tensor(f"pj{g}", [P, 512], F32)) for g in range(SLOTS)]
        ps_a, ps_b, ps_c, ps_d, ps_e = [ctx.enter_context(nc.psum_tensor(f"ps_{n}", [P, 512], F32)) for n in "abcde"]

        xn_h = sb("xn_h", [P, KT, T], F32R)
        xn_l = sb("xn_l", [P, KT, T], F32R)
        w_raw = [sb(f"w_raw{p}", [P, KT, P]) for p in range(2)]
        w_h = [sb(f"w_h{p}", [P, KT, P], F32R) for p in range(2)]
        w_l = [sb(f"w_l{p}", [P, KT, P], F32R) for p in range(2)]
        kT = sb("kT", [P, 2, T])
        ident = sb("ident", [P, P])
        mean_m = sb("mean_m", [P, P])
        par = sb("par", [P, 32])
        lb = sb("lb", [P, HEADS])
        oml = sb("oml", [P, HEADS])
        noml = sb("noml", [P, HEADS])
        lbt = sb("lbt", [P, 3, HEADS])
        rstd = sb("rstd", [P, 2, NC + 1])
        eps = sb("eps", [P, 1])
        mg_area = ExitStack()
        ha = sb("ha", [P, HEADS, T], where=mg_area)
        mg_area.close()
        mg = sb("mg", [P, HEADS, T], where=mg_area)
        mg_area.close()
        x_o = [sb(f"x_o{n}", [P, D], where=mg_area) for n in range(3)]
        y_o = [sb(f"y_o{n}", [P, D], where=mg_area) for n in range(3)]
        y_sq = sb("y_sq", [P, D], where=mg_area)
        g_fin = sb("g_fin", [P, D], where=mg_area)
        sb("mg_pad", [P, HEADS * (T - D)], where=mg_area)
        ctx.enter_context(mg_area)

        area = ExitStack()
        q = sb("q", [P, T], where=area)
        k = sb("k", [P, T], where=area)
        b = sb("b", [P, T], where=area)
        vT = sb("vT", [P, T], where=area)
        zs = sb("zs", [P, T], where=area)
        d64 = sb("d64", [P, NC, 2, 64], where=area)
        d32 = sb("d32", [P, 2 * NC, 2, 32], where=area)
        dq = sb("dq", [P, T], where=area)
        dk = sb("dk", [P, T], where=area)
        qI = sb("qI", [P, T], where=area)
        rs = qI
        kD = sb("kD", [P, T], where=area)
        v_tok = sb("v_tok", [P, NC + 1, P], where=area)
        k_tok = sb("k_tok", [P, NC + 1, P], where=area)
        att = sb("att", [P, NC, P], where=area)
        att_s = sb("att_s", [NS, NS], where=area)
        S = sb("S", [P, NC, P], where=area)
        s0 = sb("s0", [P, NB, P], where=area)
        v_exp = sb("v_exp", [P, NB, P], where=area)
        E = sb("E", [P, NC + NB], where=area)
        cs = sb("cs", [P, 32 + NB], where=area)
        reset = sb("reset", [P, T], mybir.dt.bfloat16, where=area)
        causal = sb("causal", [P, P], I32, where=area)
        causal_s = sb("causal_s", [NS, NS], I32, where=area)
        batch_m = sb("batch_m", [NS, NB], where=area)
        area.close()

        area = ExitStack()
        sg = sb("sg", [P, T], where=area)
        hl_h = sb("hl_h", [P, KT, T], F32R, where=area)
        hl_l = sb("hl_l", [P, KT, T], F32R, where=area)
        area.close()

        area = ExitStack()
        hb = sb("hb", [P, HEADS, T], where=area)
        swa = ExitStack()
        zb = sb("zb", [P, T], where=swa)
        k_out = sb("k_out", [P, 2, P], where=swa)
        dist = sb("dist", [P, 2 * P], where=swa)
        bias = sb("bias", [P, 2, 2 * P], where=swa)
        sb("gate_pad", [P, T - 8 * P], where=swa)
        v_tk = sb("v_tk", [P, NC + 1, P], where=swa)
        qT = sb("qT", [P, T], where=swa)
        PT = sb("PT", [P, 3, 4, P], where=swa)
        q_s = sb("q_s", [P, NB, HEADS, DEC], where=swa)
        z_s = sb("z_s", [P, HEADS, NS], where=swa)
        stat = sb("stat", [P, 5, 2 * NC], where=swa)
        sinks = sb("sinks", [P, QH], where=swa)
        pick = sb("pick", [P, HEADS], where=swa)
        sink_m = sb("sink_m", [P, 2], where=swa)
        sinks_s = sb("sinks_s", [P, 2], where=swa)
        slopes = sb("slopes", [P, QH], where=swa)
        stat_s = sb("stat_s", [P, 5, 4], where=swa)
        sc = ExitStack()
        scores = sb("scores", [P, 2 * NC, 2 * P], where=sc)
        sc.close()
        ck = sb("ck", [P, NB, P], where=sc)
        cv = sb("cv", [P, NB, P], where=sc)
        ckT = sb("ckT", [P, NB, P], where=sc)
        sc_s = sb("sc_s", [P, 4, P + NS], where=sc)
        sc.close()
        swa.close()
        sgb = sb("sgb", [P, HEADS, T], where=area)
        wo_raw = sb("wo_raw", [P, KT, P], where=area)
        area.close()
        bias_s = qT[:, 0:4 * (P + NS)].rearrange("p (u k) -> p u k", u=4)
        PT_s = PT[:, 0, :, :]
        PT_n = PT[0:NS, 1, :, :]

        area = ExitStack()
        wo_h0 = sb("wo_h0", [P, KT, 512], F32R, where=area)
        wo_l0 = sb("wo_l0", [P, KT, 512], F32R, where=area)
        sb("wo_pad", [P, HEADS * T - 2 * KT * 512], where=area)
        wo_1 = sb("wo_1", [P, HEADS, T], F32R, where=area)
        area.close()
        wo_at = lambda c, lo: ((wo_h0, wo_l0)[lo][:, :, c * P:(c + 1) * P] if c < 4 else
                               wo_1[:, 2 * (c - 4) + lo, 0:D].rearrange("p (k c) -> p k c", k=KT))
        wo_rhs = lambda m, lo, kt: (wo_h0, wo_l0)[lo][:, kt, :] if m == 0 else wo_1[:, lo:HEADS:2, kt * P:(kt + 1) * P]

        area = ExitStack()
        x_t = [sb(f"x_t{n}", [P, D], where=area) for n in range(NC + 1)]
        x_sq = sb("x_sq", [P, D], where=area)
        x_n = [sb(f"x_n{n}", [P, D], where=area) for n in range(2)]
        g_row = sb("g_row", [P, D], where=area)
        rows = sb("rows", [32, P], where=area)
        area.close()

        act_done, dve_done, pe_done, pool_done = sem("act_done"), sem("dve_done"), sem("pe_done"), sem("pool_done")
        w_loaded = [sem("w_loaded0"), sem("w_loaded1")]
        w_hi_ready, w_lo_ready, slot_done = sem("w_hi_ready"), sem("w_lo_ready"), sem("slot_done")
        x_loaded = [sem(f"x_loaded{t}") for t in range(NC + 1)]
        consts_loaded, g_loaded, masks_loaded = sem("consts_loaded"), sem("g_loaded"), sem("masks_loaded")
        s0_loaded, s0_stored, sp_stored = sem("s0_loaded"), sem("s0_stored"), sem("sp_stored")

        slopes_loaded, caches_loaded, bias_s_loaded = sem("slopes_loaded"), sem("caches_loaded"), sem("bias_s_loaded")
        caches_stored, wo_loaded, wo_hi_ready, wo_lo_ready = sem("caches_stored"), sem("wo_loaded"), sem("wo_hi_ready"), sem("wo_lo_ready")
        g_fin_loaded = sem("g_fin_loaded")
        xo_loaded = [sem(f"xo_loaded{n}") for n in range(3)]
        y_stored = [sem(f"y_stored{n}") for n in range(3)]

        w_pa_v = w_pa[0].rearrange("(k p) c -> p k c", p=P)
        w_pb_v = w_pb[0].rearrange("(s k d) c -> s d k c", s=2, d=HD)
        w_out_v = w_out[0].rearrange("(k p) c -> p k c", p=P)
        GA, KV, QZ, GB, PB = 33, 49, 50, 66, 74
        bank_of = lambda t, n: (pj + [ps_a, ps_b, ps_c, ps_d, ps_e])[(2 * t + n) % 8]
        score_bank = lambda n, h: ((ps_a, ps_b, ps_c, ps_d)[n % 4], h * 2 * P)
        pair_of = lambda m: ("swa_l", 0) if is_last(m) else ("swa", m)
        w_in_v = w_in[0].rearrange("(k p) c -> p k c", p=P)
        st_in = state_hgrn[0].rearrange("b h k v -> k b h v")
        st_out = st_sample[0].rearrange("b h k v -> k b h v")
        sp_out = st_prompt[0, 0].rearrange("h k v -> k h v")
        span = lambda g: slice(g * W, (g + 1) * W)
        chunks = lambda a: a.rearrange("p (c t) -> p c t", c=NC)
        half = lambda g: slice(g * 512, (g + 1) * 512)
        by_head = lambda a, k: a.rearrange("p (k n h) -> p k h n", h=2, n=QU // 2)[:, k, :, :]
        now_of = lambda i: ("last", 0) if is_last(i) else ("head", i)
        prev_of = lambda i: ("pro", 0) if is_first(i) else ("head", i - 1)
        is_first = lambda i: isinstance(i, int) and i == 0
        is_last = lambda i: isinstance(i, int) and i == HEADS - 1
        turn_banks = lambda t: (((ps_a, ps_c)[t % 2], "a"), ((ps_b, ps_d)[t % 2], "b"))
        tile_rows = lambda t: P if t < NC else NS
        head_blocks = lambda i: Blocks(3, 4, i)

        block = ctx.enter_context(nc.Block())

        @block.sync
        def _(sp):
            def load(B, src, col):
                n, p, _ = B
                if not (isinstance(n, int) and n < 2):
                    sp.wait_ge(w_lo_ready, n - 1)
                for r in range(2):
                    sp.dma_start(w_raw[p][:, 4 * r:4 * r + 4, :], src[:, 4 * r:4 * r + 4, bass.ds(col, P)]).then_inc(w_loaded[p], 16)

            def token_rows(prompt, sample, t):
                return prompt[0, t * P:(t + 1) * P, :] if t < NC else sample.rearrange("b t d -> (b t) d")

            def load_tokens(t):
                sp.dma_start(x_t[t][0:tile_rows(t), :], token_rows(x_prompt, x_sample, t)).then_inc(x_loaded[t], 16)

            pro = Blocks(0, 1, 0)
            load_tokens(0)
            sp.dma_start(ident[:], c_ident).then_inc(consts_loaded, 16)
            sp.dma_start(rows[0:16, :], lb_logits.rearrange("l (h p) -> (l h) p", p=P)).then_inc(consts_loaded, 16)
            sp.dma_start(rows[16:17, :], a_gnorm).then_inc(consts_loaded, 16)
            sp.dma_start(g_row[:], norm_in.to_broadcast([P, D])).then_inc(g_loaded, 16)
            load_tokens(1)
            load(pro(0), w_in_v, OFF["f"])
            for t in range(2, NC + 1):
                load_tokens(t)
            load(pro(1), w_in_v, OFF["q"])
            load(pro(2), w_in_v, OFF["z"])
            sp.wait_ge(pe_done, pe.at(("pro", 0), f"xb{NC}"))
            sp.dma_start(causal[:], c_causal).then_inc(masks_loaded, 16)
            sp.dma_start(causal_s[:], c_causal_s).then_inc(masks_loaded, 16)
            sp.dma_start(batch_m[:], c_batch).then_inc(masks_loaded, 16)

            def head(i):
                B = head_blocks(i)
                now = now_of(i)
                if is_first(i):
                    sp.dma_start(s0[:], st_in[:, :, 0, :]).then_inc(s0_loaded, 16)
                load(B(0), w_in_v, i * P + OFF["i"])
                if is_last(i):
                    load(B(1), w_in_v, OFF["kb"])
                    load(B(2), w_in_v, OFF["ga"])
                    load(B(3), w_pa_v, 0)
                    load(B(4), w_in_v, OFF["ga"] + P)
                else:
                    load(B(1), w_in_v, i * P + (OFF["f"] + P))
                    load(B(2), w_in_v, i * P + (OFF["q"] + P))
                    load(B(3), w_in_v, i * P + (OFF["z"] + P))
                sp.wait_ge(dve_done, dve.at(now, "s8"))
                sp.dma_start(sp_out[:, bass.ds(i, 1), :], S[:, NC - 1:NC, :]).then_inc(sp_stored, 16)
                sp.wait_ge(dve_done, dve.at(now, "so1"))
                sp.dma_start(st_out[:, :, bass.ds(i, 1), :], s0[:].rearrange("p b (o v) -> p b o v", o=1)).then_inc(s0_stored, 16)
                if not is_last(i):
                    sp.wait_ge(s0_stored, i * 16 + 16)
                    sp.dma_start(s0[:].rearrange("p b (o v) -> p b o v", o=1), st_in[:, :, bass.ds(i + 1, 1), :]).then_inc(s0_loaded, 16)

            head(0)
            with nc.sync.Fori(1, HEADS - 1) as i:
                head(i)
            head(HEADS - 1)

            with nc.sync.Fori(1, HEADS - 1) as j:
                B = Blocks(GA, 2, j)
                load(B(1), w_pa_v, j * P)
                load(B(2), w_in_v, j * P + (OFF["ga"] + P))
            load(Blocks(GA, 2, HEADS - 1)(1), w_pa_v, (HEADS - 1) * P)
            load(Blocks(KV, 1, 0)(0), w_in_v, OFF["vb"])
            def load_pair(B, off, m):
                n, p, _ = B
                sp.wait_ge(w_lo_ready, n - 1)
                for r in range(2):
                    sp.dma_start(w_raw[p][:, :, r * HD:(r + 1) * HD],
                                 w_in_v[:, :, bass.ds(m * HD + (off + r * QH // 2 * HD), HD)]).then_inc(w_loaded[p], 16)

            qz = Blocks(QZ, 2, 0)
            load_pair(qz(0), OFF["qb"], 0)
            load_pair(qz(1), OFF["zb"], 0)
            sp.wait_ge(slot_done, SLOTS * KV)
            sp.dma_start(dist[:], c_dist).then_inc(slopes_loaded, 16)
            sp.dma_start(slopes[:], c_slopes[:, 0:QH]).then_inc(slopes_loaded, 16)
            sp.dma_start(pick[:], c_slopes[:, QH:QH + 8]).then_inc(slopes_loaded, 16)
            sp.dma_start(sinks[:], b_sinks.to_broadcast([P, QH])).then_inc(slopes_loaded, 16)

            for new, old in ((ck_sample, cache_k), (cv_sample, cache_v)):
                sp.dma_start(new[0, :, 0:P - DEC].rearrange("b t h d -> b (t h d)"),
                             old[0, :, DEC:P].rearrange("b t h d -> b (t h d)")).then_inc(caches_stored, 16)
            sp.wait_ge(act_done, act.at(("kv", 0), "ks"))
            sp.wait_ge(dve_done, dve.at(("kv", 0), "vt1"))
            sp.dma_start(ck_prompt[0, 0].rearrange("t h d -> t (h d)"), k_out[:, 0, :]).then_inc(caches_stored, 16)
            sp.dma_start(cv_prompt[0, 0].rearrange("t h d -> t (h d)"), v_tk[:, NC - 1, :]).then_inc(caches_stored, 16)
            for m in range(NB):
                rows_m = slice(DEC * m, DEC * (m + 1))
                sp.dma_start(ck_sample[0, m, P - DEC:P].rearrange("t h d -> t (h d)"), k_out[rows_m, 1, :]).then_inc(caches_stored, 16)
                sp.dma_start(cv_sample[0, m, P - DEC:P].rearrange("t h d -> t (h d)"), v_tk[rows_m, NC, :]).then_inc(caches_stored, 16)
            with nc.sync.Fori(0, HEADS - 1) as m:
                B = Blocks(QZ, 2, m)
                load_pair(B(2), OFF["qb"], m + 1)
                load_pair(B(3), OFF["zb"], m + 1)
            gb = Blocks(GB, 2, 0)
            load(gb(0), w_in_v, OFF["gb"])
            load(gb(1), w_in_v, OFF["gb"] + P)
            sp.wait_ge(pe_done, pe.at(("swa_l", 0), "t7"))
            sp.wait_ge(dve_done, dve.at(("swa_l", 0), "n15"))
            sp.dma_start(ck[:], cache_k[0].rearrange("b t h d -> t b (h d)")).then_inc(caches_loaded, 16)
            sp.dma_start(cv[:], cache_v[0].rearrange("b t h d -> t b (h d)")).then_inc(caches_loaded, 16)
            sp.dma_start(bias_s, c_bias_s).then_inc(bias_s_loaded, 16)
            def load_pb(B, col):
                n, p, _ = B
                sp.wait_ge(w_lo_ready, n - 1)
                for r in range(2):
                    sp.dma_start(w_raw[p][r * HD:(r + 1) * HD, :, :], w_pb_v[r, :, :, bass.ds(col, P)]).then_inc(w_loaded[p], 16)

            with nc.sync.Fori(0, 3) as j:
                B = Blocks(GB, 2, j)
                load(B(2), w_in_v, j * (2 * P) + (OFF["gb"] + 2 * P))
                load(B(3), w_in_v, j * (2 * P) + (OFF["gb"] + 3 * P))
            pb = Blocks(PB, 2, 0)
            load_pb(pb(0), 0)
            load_pb(pb(1), P)

            wo_chunks = [0, 1, 4, 2, 5, 3, 6, 7]

            def load_wo(n):
                if n == 0:
                    sp.wait_ge(dve_done, dve.at(("swa_s", 0), "h"))
                else:
                    sp.wait_ge(wo_lo_ready, n)
                sp.dma_start(wo_raw[:], w_out_v[:, :, bass.ds(wo_chunks[n] * P, P)]).then_inc(wo_loaded, 16)

            load_wo(0)
            for j in range(3):
                load_pb(Blocks(PB, 2, j)(2), (2 * j + 2) * P)
                load_pb(Blocks(PB, 2, j)(3), (2 * j + 3) * P)
                load_wo(2 * j + 1)
                load_wo(2 * j + 2)
            load_wo(7)

            sp.wait_ge(dve_done, dve.at(("split_m", 0), "l7"))
            sp.dma_start(g_fin[:], norm_final.rearrange("(o d) -> o d", o=1).to_broadcast([P, D])).then_inc(g_fin_loaded, 16)

            def load_x(t):
                r = P if t < NC else NS
                sp.dma_start(x_o[t % 3][0:r, :], token_rows(x_prompt, x_sample, t)).then_inc(xo_loaded[t % 3], 16)

            for t in range(3):
                load_x(t)
            for t in range(NC + 1):
                r = P if t < NC else NS
                sp.wait_ge(dve_done, dve.at(("out", 0), f"yn{t}"))
                sp.dma_start(token_rows(y_prompt, y_sample, t), y_o[t % 3][0:r, :]).then_inc(y_stored[t % 3], 16)
                if t + 3 < NC + 1:
                    load_x(t + 3)
            for n in range(3):
                sp.wait_ge(y_stored[n], 16 * 3)
            sp.wait_ge(sp_stored, 16 * HEADS)
            sp.wait_ge(s0_stored, 16 * HEADS)
            sp.wait_ge(caches_stored, 16 * (4 + 2 * NB))

        @block.gpsimd
        def _(g):
            def split_lo(B):
                n, p, _ = B
                g.wait_ge(w_hi_ready, n + 1)
                g.tensor_tensor(w_l[p][:], w_raw[p][:], w_h[p][:].bitcast(F32), ALU.subtract).then_inc(w_lo_ready, 1)

            pro = Blocks(0, 1, 0)
            g.memset(eps[:], EPS).then_inc(pool_done, pool.tick(("pro", 0), "eps"))
            for n in range(3):
                split_lo(pro(n))

            def head(i):
                B, now = head_blocks(i), now_of(i)
                split_lo(B(0))
                split_lo(B(1))
                if is_first(i):
                    g.wait_ge(masks_loaded, 48)
                g.wait_ge(act_done, act.at(now, "vts"))
                g.tensor_tensor(v_exp[0:NS], v_tok[0:NS, NC:NC + 1, :].to_broadcast([NS, NB, P]),
                                batch_m[:].rearrange("p (b o) -> p b o", o=1).to_broadcast([NS, NB, P]),
                                ALU.mult).then_inc(pool_done, pool.tick(now, "vexp"))
                split_lo(B(2))
                g.wait_ge(pe_done, pe.at(now, "os"))
                g.tensor_tensor(s0[:], s0[:], E[:, NC:NC + NB].rearrange("p (b o) -> p b o", o=1).to_broadcast([P, NB, P]),
                                ALU.mult).then_inc(pool_done, pool.tick(now, "s0e"))
                split_lo(B(3))
                if is_last(i):
                    split_lo(B(4))

            head(0)
            with nc.gpsimd.Fori(1, HEADS - 1) as i:
                head(i)
            head(HEADS - 1)
            with nc.gpsimd.Fori(1, HEADS) as j:
                B = Blocks(GA, 2, j)
                split_lo(B(1))
                split_lo(B(2))
            for n in range(4):
                split_lo(Blocks(QZ, 2, 0)(n))
            with nc.gpsimd.Fori(0, HEADS - 1) as m:
                B = Blocks(QZ, 2, m)
                split_lo(B(4))
                split_lo(B(5))
            with nc.gpsimd.Fori(0, 4) as j:
                B = Blocks(GB, 2, j)
                split_lo(B(2))
                split_lo(B(3))

            wo_chunks = [0, 1, 4, 2, 5, 3, 6, 7]

            def wo_split_lo(n):
                c = wo_chunks[n]
                g.wait_ge(wo_hi_ready, n + 1)
                g.tensor_tensor(wo_at(c, 1), wo_raw[:], wo_at(c, 0).bitcast(F32), ALU.subtract).then_inc(wo_lo_ready, 1)

            wo_split_lo(0)
            for j in range(3):
                split_lo(Blocks(PB, 2, j)(2))
                split_lo(Blocks(PB, 2, j)(3))
                wo_split_lo(2 * j + 1)
                wo_split_lo(2 * j + 2)
            wo_split_lo(7)

        @block.scalar
        def _(a):
            pr = ("pro", 0)
            nc.scalar.preload_act_table_set("natural_log_exp_and_others")

            def split_hi(B):
                n, p, h = B
                a.wait_ge(w_loaded[p], h * 32 + 32)
                if not (isinstance(n, int) and n < 2):
                    a.wait_ge(slot_done, n * 3 - 3)
                a.activation(w_h[p][:], w_raw[p][:], ACT.Copy).then_inc(w_hi_ready, 1)

            a.wait_ge(dve_done, dve.at(pr, "lbd1"))
            a.activation(lbt[:, 0, :], lbt[:, 0, :], ACT.Exp).then_inc(act_done, act.tick(pr, "lb0"))
            a.activation(lbt[:, 1, :], lbt[:, 1, :], ACT.Exp).then_inc(act_done, act.tick(pr, "lb1"))
            a.wait_ge(pool_done, pool.at(pr, "eps"))
            pro = Blocks(0, 1, 0)
            for t in range(NC + 2):
                if t <= NC:
                    r = tile_rows(t)
                    a.wait_ge(x_loaded[t], 16)
                    if t:
                        a.wait_ge(act_done, act.at(pr, f"ss{t - 1}"))
                    a.activation(x_sq[0:r], x_t[t][0:r, :], ACT.Square, accum_out=rstd[0:r, 0, t:t + 1]).then_inc(act_done, act.tick(pr, f"ss{t}"))
                    a.wait_ge(act_done, act.at(pr, f"ss{t}"))
                    a.activation(rstd[0:r, 0, t:t + 1], rstd[0:r, 0, t:t + 1], ACT.Ln, scale=1.0 / D, bias=eps[0:r]).then_inc(act_done, act.tick(pr, f"ln{t}"))
                    a.wait_ge(act_done, act.at(pr, f"ln{t}"))
                    a.activation(rstd[0:r, 1, t:t + 1], rstd[0:r, 0, t:t + 1], ACT.Exp, scale=-0.5).then_inc(act_done, act.tick(pr, f"rstd{t}"))
                if t >= 1:
                    u = t - 1
                    for n, (bank, s) in enumerate(turn_banks(u)):
                        a.wait_ge(pe_done, pe.at(pr, f"x{s}{u}"))
                        a.activation(xn_h[:, 4 * n:4 * n + 4, u * P:u * P + tile_rows(u)], bank[:].rearrange("p (k t) -> p k t", k=4)[:, :, 0:tile_rows(u)],
                                     ACT.Copy).then_inc(act_done, act.tick(pr, f"hi_{s}{u}"))
                if t in (1, NC):
                    split_hi(pro(t // NC))

            def sig(where, name, n_slot, g, out):
                a.wait_ge(slot_done, n_slot)
                a.activation(out[:, span(g)], pj[g][:, 0:W], ACT.Sigmoid).then_inc(act_done, act.tick(where, f"{name}{g}"))

            def copy(where, name, n_slot, g, out, scale=1.0):
                a.wait_ge(slot_done, n_slot)
                a.activation(out[:, span(g)], pj[g][:, 0:W], ACT.Copy, scale=scale).then_inc(act_done, act.tick(where, f"{name}{g}"))

            def log_f(where, i):
                nc.scalar.preload_act_table_set("natural_log_exp_and_others")
                a.wait_ge(act_done, act.at(where, "sf2"))
                a.activation(b[:], k[:], ACT.Ln, scale=oml[:, bass.ds(i, 1)], bias=lb[:, bass.ds(i, 1)]).then_inc(act_done, act.tick(where, "lnf"))
                nc.scalar.preload_act_table(ACT.Sigmoid)

            for n, (name, out) in enumerate((("sf", k), ("sigq", q), ("sigz", zs))):
                for g in range(SLOTS):
                    sig(pr, name, 3 * n + g + 1, g, out)
                if n == 0:
                    log_f(pr, 0)
                if n + 2 < 4:
                    split_hi(pro(n + 2) if n == 0 else head_blocks(0)(0))

            def head(i):
                B, now = head_blocks(i), now_of(i)
                prev = prev_of(i)
                last = is_last(i)
                if not is_first(i):
                    nc.scalar.preload_act_table_set("natural_log_exp_and_others")
                    a.wait_ge(pe_done, pe.at(prev, "mss"))
                    a.activation(rs[:, half(0)], ps_a[:], ACT.Ln, bias=eps[:]).then_inc(act_done, act.tick(now, "rl0"))
                    a.activation(rs[:, half(1)], ps_b[:], ACT.Ln, bias=eps[:]).then_inc(act_done, act.tick(now, "rl1"))
                    a.activation(rs[:, SEQ:T], ps_d[:, 64:64 + NS], ACT.Ln, bias=eps[:]).then_inc(act_done, act.tick(now, "rls"))
                    a.wait_ge(act_done, act.at(now, "rls"))
                    a.activation(rs[:], rs[:], ACT.Exp, scale=-0.5).then_inc(act_done, act.tick(now, "rx"))
                if is_first(i):
                    nc.scalar.preload_act_table_set("natural_log_exp_and_others")
                split_hi(B(1))

                def v_copy(g):
                    a.wait_ge(slot_done, B(0)[0] * 3 + (g + 1))
                    a.activation(vT[:, span(g)], pj[g][:, 0:W], ACT.Copy).then_inc(act_done, act.tick(now, f"v{g}"))

                def exp(name, need, out, src, scale=1.0):
                    a.wait_ge(dve_done, dve.at(prev, need))
                    a.activation(out, src, ACT.Exp, scale=scale).then_inc(act_done, act.tick(now, name))

                v_copy(0)
                if not is_first(i):
                    a.wait_ge(pool_done, pool.at(prev, "s0e"))
                exp("ebl", "scan", E[:, 0:NC], chunks(b[:, 0:SEQ])[:, :, P - 1])
                exp("ebs", "scan", E[:, NC:NC + NB], b[:, SEQ:T].rearrange("p (b t) -> p b t", b=NB)[:, :, DEC - 1])
                exp("xkD", "kDs", kD[:], kD[:])
                v_copy(1)
                exp("x64", "a64k", d64[:], d64[:])
                exp("x32", "a32k", d32[:], d32[:])
                v_copy(2)
                split_hi(B(2))
                exp("xdq", "xc", dq[:], dk[:], -1.0)
                exp("xdk", "xc", dk[:], dk[:])
                if not is_first(i):
                    a.wait_ge(dve_done, dve.at(now, "ha"))
                exp("xqI", "scan", qI[:], b[:])
                for n, (bank, cols) in enumerate(((ps_a, slice(0, 4)), (ps_b, slice(4, 8)))):
                    a.wait_ge(pe_done, pe.at(now, f"vt{n}"))
                    a.activation(v_tok[:, cols, :], bank[:].rearrange("p (c v) -> p c v", c=4), ACT.Copy).then_inc(act_done, act.tick(now, f"vt{n}"))
                a.wait_ge(pe_done, pe.at(now, "vts"))
                a.activation(v_tok[0:NS, NC, :], ps_e[0:NS, 0:P], ACT.Copy).then_inc(act_done, act.tick(now, "vts"))

                def squares():
                    a.wait_ge(pe_done, pe.at(now, "o0"))
                    a.activation(vT[:, half(0)], ps_e[:], ACT.Square).then_inc(act_done, act.tick(now, "sq0"))
                    a.wait_ge(pe_done, pe.at(now, "o1"))
                    a.activation(vT[:, half(1)], ps_c[:], ACT.Square).then_inc(act_done, act.tick(now, "sq1"))
                    a.wait_ge(pe_done, pe.at(now, "os"))
                    a.activation(vT[:, SEQ:T], ps_d[:, 0:NS], ACT.Square).then_inc(act_done, act.tick(now, "sqs"))

                if last:
                    for g in range(SLOTS):
                        a.wait_ge(slot_done, B(1)[0] * 3 + (g + 1))
                        for h in range(2):
                            rows_h = slice(h * HD, (h + 1) * HD)
                            a.activation(kT[rows_h, h, span(g)], pj[g][rows_h, 0:W], ACT.Copy).then_inc(act_done, act.tick(now, f"k{g}{'ab'[h]}"))
                    split_hi(B(3))
                    squares()
                    a.wait_ge(pe_done, pe.at(now, "mss"))
                    a.activation(rs[:, half(0)], ps_a[:], ACT.Ln, bias=eps[:]).then_inc(act_done, act.tick(now, "fl0"))
                    a.activation(rs[:, half(1)], ps_b[:], ACT.Ln, bias=eps[:]).then_inc(act_done, act.tick(now, "fl1"))
                    a.activation(rs[:, SEQ:T], ps_d[:, 64:64 + NS], ACT.Ln, bias=eps[:]).then_inc(act_done, act.tick(now, "fls"))
                    a.wait_ge(act_done, act.at(now, "fls"))
                    a.activation(rs[:], rs[:], ACT.Exp, scale=-0.5).then_inc(act_done, act.tick(now, "fx"))
                    nc.scalar.preload_act_table(ACT.Sigmoid)
                    a.wait_ge(dve_done, dve.at(now, "qIm"))
                    for g in range(SLOTS):
                        sig(now, "sg", B(2)[0] * 3 + (g + 1), g, sg)
                    split_hi(B(4))
                    return
                nc.scalar.preload_act_table(ACT.Sigmoid)
                a.wait_ge(dve_done, dve.at(now, "qIm"))
                for g in range(SLOTS):
                    sig(now, "sf", B(1)[0] * 3 + (g + 1), g, k)
                log_f(now, i + 1)
                split_hi(B(3))
                sig(now, "sigq", B(2)[0] * 3 + 1, 0, q)
                squares()
                for g in (1, 2):
                    sig(now, "sigq", B(2)[0] * 3 + (g + 1), g, q)
                split_hi(B(4))
                a.wait_ge(dve_done, dve.at(now, "gates"))
                for g in range(SLOTS):
                    sig(now, "sigz", B(3)[0] * 3 + (g + 1), g, zs)

            head(0)
            with nc.scalar.Fori(1, HEADS - 1) as i:
                head(i)
            head(HEADS - 1)

            def split_rows(phase, src, hi):
                for n in range(KT):
                    a.activation(hi[:, n, :], src[:, n, :], ACT.Copy).then_inc(act_done, act.tick((phase, 0), f"h{n}"))

            a.wait_ge(dve_done, dve.at(("last", 0), "hal"))
            a.wait_ge(sp_stored, 16 * HEADS)
            a.wait_ge(s0_stored, 16 * HEADS)
            split_rows("split_a", ha, hl_h)
            with nc.scalar.Fori(1, HEADS) as j:
                B = Blocks(GA, 2, j)
                split_hi(B(1))
                for g in range(SLOTS):
                    a.wait_ge(dve_done, dve.at(("pa", j - 1), f"m{g}"))
                    sig(("pa", j - 1), "sg", B(0)[0] * 3 + (g + 1), g, sg)
                split_hi(B(2))

            qz, here = Blocks(QZ, 2, 0), ("kv", 0)
            split_hi(qz(0))
            a.wait_ge(dve_done, dve.at(("pa", HEADS - 1), "m2"))
            for g in range(SLOTS):
                copy(here, "v", 3 * KV + g + 1, g, zb)
            split_hi(qz(1))
            for g in range(SLOTS):
                copy(here, "q", 3 * QZ + g + 1, g, qT, HD ** -0.5)
            a.wait_ge(pe_done, pe.at(here, "vt0"))
            a.activation(v_tk[:, 0:4, :], ps_a[:].rearrange("p (c v) -> p c v", c=4), ACT.Copy).then_inc(act_done, act.tick(here, "vt0"))
            a.wait_ge(pe_done, pe.at(here, "vts"))
            a.activation(v_tk[0:NS, NC, :], ps_c[0:NS, 0:P], ACT.Copy).then_inc(act_done, act.tick(here, "vts"))
            a.wait_ge(pe_done, pe.at(here, "kt"))
            two_heads = lambda a: a.rearrange("p (h x) -> p h x", h=2)[:, :, 0:HD]
            a.activation(k_out[:, 0, :].rearrange("p (h d) -> p h d", h=2), two_heads(ps_d[:, 0:6 * HD]), ACT.Copy).then_inc(act_done, act.tick(here, "kt"))
            a.activation(k_out[0:NS, 1, :].rearrange("p (h d) -> p h d", h=2), two_heads(ps_e[0:NS, 0:6 * HD]), ACT.Copy).then_inc(act_done, act.tick(here, "ks"))
            split_hi(qz(2))
            for g in range(SLOTS):
                sig(here, "sigz", 3 * (QZ + 1) + g + 1, g, zb)
            split_hi(qz(3))

            def pair(m):
                B, now = Blocks(QZ, 2, m), pair_of(m)
                last = is_last(m)
                nc.scalar.preload_act_table_set("natural_log_exp_and_others")
                for k in quarters:
                    for h in range(2):
                        a.wait_ge(dve_done, dve.at(now, f"nm{h}_{k}"))
                        a.activation(by_head(stat[:, 2, :], k)[:, h, :], by_head(stat[:, 1, :], k)[:, h, :], ACT.Exp,
                                     bias=sink_m[:, h:h + 1]).then_inc(act_done, act.tick(now, f"es{h}_{k}"))
                    for u in range(QU * k, QU * (k + 1)):
                        keys = slice(P if u < 2 else 0, 2 * P)
                        a.activation(scores[:, u, keys], scores[:, u, keys], ACT.Exp, bias=stat[:, 1, u:u + 1],
                                     accum_out=stat[:, 3, u:u + 1]).then_inc(act_done, act.tick(now, f"p{u}"))

                def queries(g):
                    if not last:
                        copy(now, "q", B(2)[0] * 3 + (g + 1), g, qT, HD ** -0.5)

                if not last:
                    a.wait_ge(pe_done, pe.at(now, "s7"))
                    a.wait_ge(dve_done, dve.at(now, "qs"))
                for g in range(2):
                    queries(g)
                for n in range(0, NC, 2):
                    if n == 2:
                        queries(2)
                        if not last:
                            split_hi(B(4))
                    a.wait_ge(pe_done, pe.at(now, f"t{n}"))
                    if n >= 3:
                        a.wait_ge(pe_done, pe.at(now, f"o{n - 3}"))
                    fill = slice(P if n == 0 else 0, 4 * P)
                    src = (ps_a, ps_b, ps_c)[n % 3]
                    a.activation(PT[:, n % 3, :, :].rearrange("p a q -> p (a q)")[:, fill], src[:, fill], ACT.Copy).then_inc(act_done, act.tick(now, f"pt{n}"))
                if not last:
                    nc.scalar.preload_act_table(ACT.Sigmoid)
                    a.wait_ge(dve_done, dve.at(now, "h1"))
                    for g in range(SLOTS):
                        sig(now, "sigz", B(3)[0] * 3 + (g + 1), g, zb)
                    split_hi(B(5))

            with nc.scalar.Fori(0, HEADS - 1) as m:
                pair(m)
            pair(HEADS - 1)

            here = ("swa_s", 0)

            def gate_b(where, step, B, at, g):
                a.wait_ge(slot_done, B[0] * 3 + (g + 1))
                a.activation(sgb[:, at, span(g)], pj[g][:, 0:W].rearrange("p (o t) -> p o t", o=1), ACT.Sigmoid)\
                 .then_inc(act_done, act.tick(where, step))

            gb = Blocks(GB, 2, 0)
            nc.scalar.preload_act_table(ACT.Sigmoid)
            a.wait_ge(dve_done, dve.at(("swa_l", 0), "h1"))
            a.wait_ge(caches_stored, 16 * (4 + 2 * NB))
            for g in range(SLOTS):
                gate_b(here, f"g{g}", gb(0), slice(0, 1), g)
            nc.scalar.preload_act_table_set("natural_log_exp_and_others")
            a.wait_ge(pe_done, pe.at(here, "ct0"))
            a.activation(ckT[:, 0:4, :], ps_a[:].rearrange("p (c v) -> p c v", c=4), ACT.Copy).then_inc(act_done, act.tick(here, "ct0"))
            split_hi(gb(2))
            for h in range(2):
                a.wait_ge(dve_done, dve.at(here, f"nm{h}_0"))
                a.activation(stat_s[:, 2, 2 * h:2 * h + 2], stat_s[:, 1, 2 * h:2 * h + 2], ACT.Exp, bias=sinks_s[:, h:h + 1]).then_inc(act_done, act.tick(here, f"es{h}_0"))
            for u in range(4):
                a.activation(sc_s[:, u, :], sc_s[:, u, :], ACT.Exp, bias=stat_s[:, 1, u:u + 1], accum_out=stat_s[:, 3, u:u + 1]).then_inc(act_done, act.tick(here, f"p{u}"))
            a.wait_ge(pe_done, pe.at(here, "pt"))
            a.activation(PT_s.rearrange("p a q -> p (a q)"), ps_a[:], ACT.Copy).then_inc(act_done, act.tick(here, "pt"))
            nc.scalar.preload_act_table(ACT.Sigmoid)
            for g in range(SLOTS):
                gate_b(here, f"g{3 + g}", gb(1), slice(1, 2), g)
            split_hi(gb(3))
            a.wait_ge(dve_done, dve.at(here, "h"))
            with nc.scalar.Fori(1, 4) as j:
                B = Blocks(GB, 2, j)
                for m in range(2):
                    for g in range(SLOTS):
                        gate_b(("gb", j - 1), f"g{3 * m + g}", B(m), bass.ds(j * 2 + m, 1), g)
                    split_hi(B(2 + m))
            a.wait_ge(slot_done, 3 * PB)
            split_rows("split_b", hb, xn_h)

            wo_chunks = [0, 1, 4, 2, 5, 3, 6, 7]

            def wo_split_hi(n):
                a.wait_ge(wo_loaded, 16 * (n + 1))
                a.activation(wo_at(wo_chunks[n], 0), wo_raw[:], ACT.Copy).then_inc(wo_hi_ready, 1)

            a.wait_ge(dve_done, dve.at(("split_b", 0), "l7"))
            wo_split_hi(0)
            for j in range(3):
                split_hi(Blocks(PB, 2, j)(2))
                split_hi(Blocks(PB, 2, j)(3))
                wo_split_hi(2 * j + 1)
                a.wait_ge(dve_done, dve.at(("pb", j), "m5"))
                wo_split_hi(2 * j + 2)
            a.wait_ge(dve_done, dve.at(("pb", 3), "m5"))
            split_rows("split_m", mg, xn_h)
            wo_split_hi(7)
            nc.scalar.preload_act_table_set("natural_log_exp_and_others")
            here = ("out", 0)
            for t in range(NC + 1):
                r = P if t < NC else NS
                a.wait_ge(dve_done, dve.at(here, f"yb{t}"))
                if t:
                    a.wait_ge(act_done, act.at(here, f"rs{t - 1}"))
                else:
                    a.wait_ge(dve_done, dve.at(("split_m", 0), "l7"))
                a.activation(y_sq[0:r], y_o[t % 3][0:r, :], ACT.Square, accum_out=rstd[0:r, 0, t:t + 1]).then_inc(act_done, act.tick(here, f"ss{t}"))
                a.wait_ge(act_done, act.at(here, f"ss{t}"))
                a.activation(rstd[0:r, 0, t:t + 1], rstd[0:r, 0, t:t + 1], ACT.Ln, scale=1.0 / D, bias=eps[0:r]).then_inc(act_done, act.tick(here, f"ln{t}"))
                a.wait_ge(act_done, act.at(here, f"ln{t}"))
                a.activation(rstd[0:r, 1, t:t + 1], rstd[0:r, 0, t:t + 1], ACT.Exp, scale=-0.5).then_inc(act_done, act.tick(here, f"rs{t}"))

        @block.tensor
        def _(t):
            pr = ("pro", 0)

            def slot(B, g, xh=xn_h, xl=xn_l):
                n, p, _ = B
                if g == 0:
                    t.wait_ge(w_hi_ready, n + 1)
                    t.wait_ge(w_lo_ready, n + 1)
                passes = ((w_h[p], xh), (w_h[p], xl), (w_l[p], xh))
                for kt in range(KT):
                    for m, (w, x) in enumerate(passes):
                        mm = nc.tensor.matmul(pj[g][:, 0:W], w[:, kt, :], x[:, kt, span(g)],
                                              start=(kt == 0 and m == 0), stop=(kt == KT - 1 and m == 2))
                mm.then_inc(slot_done, 1)

            def slots(B, xh, xl, phase):
                n, p, _ = B
                t.wait_ge(w_hi_ready, n + 1)
                t.wait_ge(w_lo_ready, n + 1)
                passes = ((w_h[p], xh), (w_h[p], xl), (w_l[p], xh))
                for kt in range(KT):
                    t.wait_ge(dve_done, dve.at((phase, 0), f"l{kt}"))
                    for g in range(SLOTS):
                        for m, (w, x) in enumerate(passes):
                            mm = nc.tensor.matmul(pj[g][:, 0:W], w[:, kt, :], x[:, kt, span(g)],
                                                  start=(kt == 0 and m == 0), stop=(kt == KT - 1 and m == 2))
                        if kt == KT - 1:
                            mm.then_inc(slot_done, 1)

            t.wait_ge(consts_loaded, 48)
            nc.tensor.transpose(ps_e[:, 0:17], rows[0:17, :], ident[0:17, 0:17]).then_inc(pe_done, pe.tick(pr, "par"))
            pro = Blocks(0, 1, 0)
            for n in range(NC + 1):
                r = tile_rows(n)
                t.wait_ge(dve_done, dve.at(pr, f"xn{n}"))
                for m, (bank, s) in enumerate(turn_banks(n)):
                    if n >= 2:
                        t.wait_ge(act_done, act.at(pr, f"hi_{s}{n - 2}"))
                        t.wait_ge(dve_done, dve.at(pr, f"lo_{s}{n - 2}"))
                    for j in range(4):
                        kt = 4 * m + j
                        mm = nc.tensor.transpose(bank[:, j * P:j * P + r], x_n[n % 2][0:r, kt * P:(kt + 1) * P], ident[0:r, 0:r])
                    mm.then_inc(pe_done, pe.tick(pr, f"x{s}{n}"))
                for g in range(SLOTS):
                    done = -(-(g + 1) * W // P) - 1
                    if n == min(done + 1, NC):
                        t.wait_ge(act_done, act.at(pr, f"hi_b{done}"))
                        t.wait_ge(dve_done, dve.at(pr, f"lo_b{done}"))
                        slot(pro(0), g)
            for g in range(SLOTS):
                t.wait_ge(act_done, act.at(pr, f"sf{g}"))
                slot(pro(1), g)
            for g in range(SLOTS):
                t.wait_ge(dve_done, dve.at(pr, f"q{g}"))
                slot(pro(2), g)

            def head(i):
                B, now = head_blocks(i), now_of(i)
                prev = prev_of(i)
                last = is_last(i)

                def turn(bank, at, src, cols, name):
                    for j, c in enumerate(cols):
                        r = P if c < NC else NS
                        mm = nc.tensor.transpose(bank[0:r, at + j * P:at + (j + 1) * P], src[:, c * P:c * P + r], ident[:, :])
                    mm.then_inc(pe_done, pe.tick(now, name))

                for g in range(SLOTS):
                    t.wait_ge(dve_done, dve.at(prev, f"z{g}"))
                    slot(B(0), g)
                t.wait_ge(act_done, act.at(now, "v2"))
                turn(ps_a, 0, vT, range(0, 4), "vt0")
                turn(ps_b, 0, vT, range(4, 8), "vt1")
                turn(ps_e, 0, vT, [NC], "vts")

                def gate_slot(k_block, name, by, g):
                    if last and k_block == 3:
                        return
                    step = f"k{g}b" if last and k_block == 2 else f"{name}{g}"
                    t.wait_ge(by[0], by[1].at(now, step))
                    slot(B(k_block), g)

                gate_slot(1, "v", (act_done, act), 0)
                t.wait_ge(dve_done, dve.at(now, "kD"))
                turn(ps_c, 0, kD, range(0, 4), "kt0")
                turn(ps_d, 0, kD, range(4, 8), "kt1")
                t.wait_ge(act_done, act.at(now, "vts"))
                turn(ps_e, P, kD, [NC], "kts")
                gate_slot(1, "v", (act_done, act), 1)
                t.wait_ge(dve_done, dve.at(now, "dkm"))
                for n, bank in enumerate((ps_a, ps_b)):
                    for j in range(4):
                        c, o = 4 * n + j, j * P
                        nc.tensor.matmul(bank[0:64, o + 64:o + 128], d64[:, c, 0, :], d64[:, c, 1, :], start=True, stop=True)
                        for m in range(2):
                            nc.tensor.matmul(bank[64 * m:64 * m + 32, o + 64 * m + 32:o + 64 * m + 64],
                                             d32[:, 2 * c + m, 0, :], d32[:, 2 * c + m, 1, :], start=True, stop=True)
                        for m in range(4):
                            e = c * P + 32 * m
                            mm = nc.tensor.matmul(bank[32 * m:32 * m + 32, o + 32 * m:o + 32 * m + 32],
                                                  dk[:, e:e + 32], dq[:, e:e + 32], start=True, stop=True)
                    mm.then_inc(pe_done, pe.tick(now, f"p{n}"))
                gate_slot(1, "v", (act_done, act), 2)
                t.wait_ge(act_done, act.at(now, "vts"))
                t.wait_ge(dve_done, dve.at(now, "kts"))
                nc.tensor.matmul(ps_e[0:NS, 256:256 + NS], dk[:, SEQ:T], dq[:, SEQ:T], start=True, stop=True).then_inc(pe_done, pe.tick(now, "ps"))
                for n, bank in enumerate((ps_c, ps_d)):
                    for j in range(4):
                        c = 4 * n + j
                        mm = nc.tensor.matmul(bank[:, j * P:(j + 1) * P], k_tok[:, c, :], v_tok[:, c, :], start=True, stop=True)
                    mm.then_inc(pe_done, pe.tick(now, f"u{n}"))
                gate_slot(2, "sf", (act_done, act), 0)
                gate_slot(2, "sf", (act_done, act), 1)
                t.wait_ge(dve_done, dve.at(now, "atts"))
                t.wait_ge(dve_done, dve.at(now, "qIm"))
                for n, bank in enumerate((ps_e, ps_c)):
                    for j in range(4):
                        c = 4 * n + j
                        mm = nc.tensor.matmul(bank[:, j * P:(j + 1) * P], v_tok[:, c, :], att[:, c, :], start=True, stop=(c == 0))
                        if c:
                            mm = nc.tensor.matmul(bank[:, j * P:(j + 1) * P], S[:, c - 1, :], qI[:, c * P:(c + 1) * P], start=False, stop=True)
                    mm.then_inc(pe_done, pe.tick(now, f"o{n}"))
                t.wait_ge(s0_loaded, i * 16 + 16)
                nc.tensor.matmul(ps_d[:, 0:NS], v_tok[0:NS, NC, :], att_s[:, :], start=True, stop=True)
                for m in range(NB):
                    e = SEQ + DEC * m
                    mm = nc.tensor.matmul(ps_d[:, DEC * m:DEC * (m + 1)], s0[:, m, :], qI[:, e:e + DEC], start=False, stop=True, skip_group_check=True)
                mm.then_inc(pe_done, pe.tick(now, "os"))
                gate_slot(2, "sf", (act_done, act), 2)
                t.wait_ge(pool_done, pool.at(now, "vexp"))
                for n, bank in enumerate((ps_a, ps_b)):
                    nc.tensor.matmul(bank[:, :], k_tok[:, NC, :], v_exp[:, 4 * n:4 * n + 4, :].rearrange("p b v -> p (b v)"),
                                     start=True, stop=True).then_inc(pe_done, pe.tick(now, f"us{n}"))
                gate_slot(3, "q", (dve_done, dve), 0)
                t.wait_ge(act_done, act.at(now, "sqs"))
                t.wait_ge(dve_done, dve.at(now, "so1"))
                t.wait_ge(dve_done, dve.at(now, "gates"))
                nc.tensor.matmul(ps_a[:, :], mean_m[:, :], vT[:, half(0)], start=True, stop=True).then_inc(pe_done, pe.tick(now, "ms0"))
                nc.tensor.matmul(ps_b[:, :], mean_m[:, :], vT[:, half(1)], start=True, stop=True).then_inc(pe_done, pe.tick(now, "ms1"))
                nc.tensor.matmul(ps_d[:, 64:64 + NS], mean_m[:, :], vT[:, SEQ:T], start=True, stop=True).then_inc(pe_done, pe.tick(now, "mss"))
                gate_slot(3, "q", (dve_done, dve), 1)
                gate_slot(3, "q", (dve_done, dve), 2)

            head(0)
            with nc.tensor.Fori(1, HEADS - 1) as i:
                head(i)
            head(HEADS - 1)

            t.wait_ge(act_done, act.at(("last", 0), "sg2"))
            slots(Blocks(GA, 2, 0)(1), hl_h, hl_l, "split_a")
            with nc.tensor.Fori(1, HEADS) as j:
                B = Blocks(GA, 2, j)
                for g in range(SLOTS):
                    t.wait_ge(dve_done, dve.at(("pa", j - 1), f"m{g}"))
                    slot(B(0), g)
                for g in range(SLOTS):
                    t.wait_ge(act_done, act.at(("pa", j - 1), f"sg{g}"))
                    slot(B(1), g, hl_h, hl_l)

            qz, here = Blocks(QZ, 2, 0), ("kv", 0)
            for g in range(SLOTS):
                t.wait_ge(dve_done, dve.at(("pa", HEADS - 1), f"m{g}"))
                slot(Blocks(KV, 1, 0)(0), g)
            for g in range(SLOTS):
                t.wait_ge(act_done, act.at(here, f"v{g}"))
                slot(qz(0), g)
            for n, bank in enumerate((ps_a, ps_b)):
                for j in range(4):
                    c = 4 * n + j
                    mm = nc.tensor.transpose(bank[:, j * P:(j + 1) * P], zb[:, c * P:(c + 1) * P], ident[:, :])
                mm.then_inc(pe_done, pe.tick(here, f"vt{n}"))
            nc.tensor.transpose(ps_c[0:NS, 0:P], zb[:, SEQ:T], ident[:, :]).then_inc(pe_done, pe.tick(here, "vts"))
            for h in range(2):
                nc.tensor.transpose(ps_d[:, h * P:(h + 1) * P], kT[:, h, SEQ - P:SEQ], ident[:, :])
                mm = nc.tensor.transpose(ps_e[0:NS, h * P:(h + 1) * P], kT[:, h, SEQ:T], ident[:, :])
            mm.then_inc(pe_done, pe.tick(here, "kt"))
            for g in range(SLOTS):
                t.wait_ge(act_done, act.at(here, f"q{g}"))
                slot(qz(1), g)

            def pair(m):
                B, now = Blocks(QZ, 2, m), pair_of(m)
                prev = ("swa", m - 1)
                last = is_last(m)
                z_prev = lambda g: dve.at(prev, f"z{g}")
                t.wait_ge(dve_done, dve.at(prev, "h1"))
                for n in range(NC):
                    if n >= 4:
                        t.wait_ge(dve_done, dve.at(now, f"t{2 * (n - 4) + 1}"))
                    for h in range(2):
                        bank, o = score_bank(n, h)
                        lo = P if n == 0 else 0
                        mm = nc.tensor.matmul(bank[:, o + lo:o + 2 * P], qT[:, n * P:(n + 1) * P],
                                              kT[:, h, (n - 1) * P + lo:(n + 1) * P], start=True, stop=True)
                    mm.then_inc(pe_done, pe.tick(now, f"s{n}"))
                nxt = Blocks(GB, 2, 0)(0) if last else B(2)

                def next_slot(g):
                    t.wait_ge(dve_done, z_prev(g))
                    slot(nxt, g)

                for g in range(2):
                    next_slot(g)

                def turn(n):
                    bank = (ps_a, ps_b, ps_c)[n % 3]
                    t.wait_ge(dve_done, dve.at(now, f"n{2 * n + 1}"))
                    if n >= 3:
                        if n % 2:
                            t.wait_ge(act_done, act.at(now, f"pt{n - 3}"))
                        else:
                            t.wait_ge(dve_done, dve.at(now, f"pt{n - 3}"))
                    for h in range(2):
                        for w in range(1 if n == 0 else 0, 2):
                            o = (2 * h + w) * P
                            mm = nc.tensor.transpose(bank[:, o:o + P], scores[:, 2 * n + h, w * P:(w + 1) * P], ident[:, :])
                    mm.then_inc(pe_done, pe.tick(now, f"t{n}"))

                def out(n):
                    bank, o = (ps_d, ps_e)[n // 4], (n % 4) * P
                    if n % 2:
                        t.wait_ge(dve_done, dve.at(now, f"pt{n}"))
                    else:
                        t.wait_ge(act_done, act.at(now, f"pt{n}"))
                    for h in range(2):
                        rows_h = slice(h * HD, (h + 1) * HD)
                        for w in range(1 if n == 0 else 0, 2):
                            mm = nc.tensor.matmul(bank[rows_h, o:o + P], v_tk[:, n - 1 + w, rows_h], PT[:, n % 3, 2 * h + w, :],
                                                  start=(w == 0 or n == 0), stop=(w == 1))
                    mm.then_inc(pe_done, pe.tick(now, f"o{n}"))

                for n in range(3):
                    turn(n)
                next_slot(2)
                for n in range(NC):
                    out(n)
                    if n + 3 < NC:
                        turn(n + 3)
                if not last:
                    for g in range(SLOTS):
                        t.wait_ge(act_done, act.at(now, f"q{g}"))
                        slot(B(3), g)

            t.wait_ge(act_done, act.at(("kv", 0), "ks"))
            t.wait_ge(dve_done, dve.at(("kv", 0), "vt1"))
            with nc.tensor.Fori(0, HEADS - 1) as m:
                pair(m)
            pair(HEADS - 1)

            here, gb = ("swa_s", 0), Blocks(GB, 2, 0)
            t.wait_ge(caches_loaded, 32)
            t.wait_ge(dve_done, dve.at(("swa_l", 0), "h1"))
            for n, bank in enumerate((ps_a, ps_b)):
                for j in range(4):
                    mm = nc.tensor.transpose(bank[:, j * P:(j + 1) * P], ck[:, 4 * n + j, :], ident[:, :])
                mm.then_inc(pe_done, pe.tick(here, f"ct{n}"))
            t.wait_ge(act_done, act.at(here, "g0"))
            slot(gb(1), 0)
            t.wait_ge(act_done, act.at(here, "ct0"))
            t.wait_ge(dve_done, dve.at(here, "ct1"))
            for u in range(4):
                h, grp = u // 2, u % 2
                rows_h = slice(h * HD, (h + 1) * HD)
                bank, o = (ps_c, ps_d)[h], grp * 2 * P
                for j in range(4):
                    m = 4 * grp + j
                    q_m = q_s[rows_h, m, :, :].rearrange("p g t -> p (g t)")
                    nc.tensor.matmul(bank[32 * j:32 * j + 32, o:o + P], q_m, ckT[rows_h, m, :], start=True, stop=True)
                    mm = nc.tensor.matmul(bank[32 * j:32 * j + 32, o + P:o + P + NS], q_m, kT[rows_h, h, SEQ:T], start=True, stop=True)
                mm.then_inc(pe_done, pe.tick(here, f"s{u}"))
            for g in (1, 2):
                t.wait_ge(act_done, act.at(here, f"g{g}"))
                slot(gb(1), g)
            t.wait_ge(dve_done, dve.at(here, "n3"))
            for u in range(4):
                mm = nc.tensor.transpose(ps_a[:, u * P:(u + 1) * P], sc_s[:, u, 0:P], ident[:, :])
            mm.then_inc(pe_done, pe.tick(here, "pt"))
            for u in range(4):
                mm = nc.tensor.transpose(ps_b[0:NS, u * P:(u + 1) * P], sc_s[:, u, P:P + NS], ident[:, :])
            mm.then_inc(pe_done, pe.tick(here, "pn"))
            t.wait_ge(act_done, act.at(here, "pt"))
            t.wait_ge(dve_done, dve.at(here, "pn"))
            for u in range(4):
                h, grp = u // 2, u % 2
                rows_h = slice(h * HD, (h + 1) * HD)
                nc.tensor.matmul(ps_e[rows_h, grp * P:(grp + 1) * P], v_tk[0:NS, NC, rows_h], PT_n[:, u, :], start=True, stop=True)
                for j in range(4):
                    o = grp * P + 32 * j
                    mm = nc.tensor.matmul(ps_e[rows_h, o:o + 32], cv[:, 4 * grp + j, rows_h], PT_s[:, u, 32 * j:32 * j + 32],
                                          start=False, stop=True, skip_group_check=True)
            mm.then_inc(pe_done, pe.tick(here, "o"))

            with nc.tensor.Fori(1, 4) as j:
                B = Blocks(GB, 2, j)
                for m in range(2):
                    for g in range(SLOTS):
                        t.wait_ge(act_done, act.at(("gb", j - 1), f"g{3 * m + g}") - SLOTS)
                        slot(B(m), g)
            t.wait_ge(act_done, act.at(("gb", 2), "g5"))
            slots(Blocks(PB, 2, 0)(0), xn_h, xn_l, "split_b")
            for g in range(SLOTS):
                t.wait_ge(dve_done, dve.at(("pb", 0), f"g{g}"))
                slot(Blocks(PB, 2, 0)(1), g)
            with nc.tensor.Fori(1, 4) as j:
                B = Blocks(PB, 2, j)
                for m in range(2):
                    for g in range(SLOTS):
                        t.wait_ge(dve_done, dve.at(("pb", j), f"g{3 * m + g}") - 2 * SLOTS)
                        slot(B(m), g)
            here = ("out", 0)

            def token_tile(n, m, kt):
                r = tile_rows(n)
                cols = slice(n * P, n * P + r)
                passes = ((xn_h, 0), (xn_h, 1), (xn_l, 0))
                for i, (x, lo) in enumerate(passes):
                    mm = nc.tensor.matmul(bank_of(n, m)[0:r, :], x[:, kt, cols], wo_rhs(m, lo, kt),
                                          start=(kt == 0 and i == 0), stop=(kt == KT - 1 and i == 2))
                if kt == KT - 1:
                    mm.then_inc(pe_done, pe.tick(here, f"{'ab'[m]}{n}"))

            t.wait_ge(wo_lo_ready, 6)
            for kt in range(KT):
                t.wait_ge(dve_done, dve.at(("split_m", 0), f"l{kt}"))
                for n in range(4):
                    token_tile(n, 0, kt)
            t.wait_ge(wo_lo_ready, 8)
            for n in range(4):
                for kt in range(KT):
                    token_tile(n, 1, kt)
            for n in range(4, NC + 1):
                for m in range(2):
                    t.wait_ge(dve_done, dve.at(here, f"y{'ab'[m]}{n - 4}"))
                    for kt in range(KT):
                        token_tile(n, m, kt)

        @block.vector
        def _(v):
            pr = ("pro", 0)
            tt = nc.vector.tensor_tensor
            v.wait_ge(pe_done, pe.at(pr, "par"))
            v.tensor_copy(par[:, 0:17], ps_e[:, 0:17]).then_inc(dve_done, dve.tick(pr, "par"))
            v.wait_ge(dve_done, dve.at(pr, "par"))
            tt(lbt[:, 2, :], par[:, 0:8], par[:, 8:16], ALU.max).then_inc(dve_done, dve.tick(pr, "lbm"))
            v.wait_ge(dve_done, dve.at(pr, "lbm"))
            tt(lbt[:, 0, :], par[:, 0:8], lbt[:, 2, :], ALU.subtract).then_inc(dve_done, dve.tick(pr, "lbd0"))
            tt(lbt[:, 1, :], par[:, 8:16], lbt[:, 2, :], ALU.subtract).then_inc(dve_done, dve.tick(pr, "lbd1"))
            v.wait_ge(act_done, act.at(pr, "lb1"))
            tt(lbt[:, 2, :], lbt[:, 0, :], lbt[:, 1, :], ALU.add).then_inc(dve_done, dve.tick(pr, "lbs"))
            v.wait_ge(dve_done, dve.at(pr, "lbs"))
            v.reciprocal(lbt[:, 2, :], lbt[:, 2, :]).then_inc(dve_done, dve.tick(pr, "lbr"))
            v.wait_ge(dve_done, dve.at(pr, "lbr"))
            tt(lb[:], lbt[:, 0, :], lbt[:, 2, :], ALU.mult).then_inc(dve_done, dve.tick(pr, "lb"))
            v.wait_ge(dve_done, dve.at(pr, "lb"))
            v.tensor_scalar(oml[:], lb[:], -1.0, 1.0, ALU.mult, ALU.add).then_inc(dve_done, dve.tick(pr, "oml"))
            v.tensor_scalar(noml[:], lb[:], 1.0, -1.0, ALU.mult, ALU.add).then_inc(dve_done, dve.tick(pr, "noml"))
            v.memset(mean_m[:], 1.0 / P).then_inc(dve_done, dve.tick(pr, "ones"))
            v.wait_ge(g_loaded, 16)
            for t in range(NC + 2):
                if t <= NC:
                    r = tile_rows(t)
                    v.wait_ge(act_done, act.at(pr, f"rstd{t}"))
                    if t >= 2:
                        v.wait_ge(pe_done, pe.at(pr, f"xb{t - 2}"))
                    v.scalar_tensor_tensor(out=x_n[t % 2][0:r, :], in0=x_t[t][0:r, :], scalar=rstd[0:r, 1, t:t + 1], in1=g_row[0:r, :],
                                           op0=ALU.mult, op1=ALU.mult).then_inc(dve_done, dve.tick(pr, f"xn{t}"))
                if t >= 1:
                    u = t - 1
                    for n, (bank, s) in enumerate(turn_banks(u)):
                        v.wait_ge(act_done, act.at(pr, f"hi_{s}{u}"))
                        at = (slice(None), slice(4 * n, 4 * n + 4), slice(u * P, u * P + tile_rows(u)))
                        tt(xn_l[at], bank[:].rearrange("p (k t) -> p k t", k=4)[:, :, 0:tile_rows(u)], xn_h[at].bitcast(F32),
                           ALU.subtract).then_inc(dve_done, dve.tick(pr, f"lo_{s}{u}"))
            v.wait_ge(pe_done, pe.at(pr, f"xb{NC}"))
            v.memset(att[:], 0.0).then_inc(dve_done, dve.tick(pr, "att0"))
            v.memset(att_s[:], 0.0).then_inc(dve_done, dve.tick(pr, "atts0"))
            for h in range(2):
                v.memset(kT[(1 - h) * HD:(2 - h) * HD, h, :], 0.0).then_inc(dve_done, dve.tick(pr, f"zkT{h}"))
            for name, a in (("zk", k_tok[:, NC, :]), ("zv", v_exp[:].rearrange("p b v -> p (b v)"))):
                v.memset(a[NS:2 * NS], 0.0).then_inc(dve_done, dve.tick(pr, name + "_a"))
                v.memset(a[2 * NS:P], 0.0).then_inc(dve_done, dve.tick(pr, name + "_b"))
            v.memset(reset[:], 1.0).then_inc(dve_done, dve.tick(pr, "reset"))
            v.wait_ge(dve_done, dve.at(pr, "reset"))
            v.memset(reset[:, 0:SEQ:P], 0.0).then_inc(dve_done, dve.tick(pr, "reset_p"))
            v.memset(reset[:, SEQ:T:DEC], 0.0).then_inc(dve_done, dve.tick(pr, "reset_s"))

            def gated(where, name, g, out):
                v.wait_ge(act_done, act.at(where, f"{'sigq' if name == 'q' else 'sigz'}{g}"))
                tt(out[:, span(g)], out[:, span(g)], pj[g][:, 0:W], ALU.mult).then_inc(dve_done, dve.tick(where, f"{name}{g}"))

            def exponents_of(now, i):
                def need(steps, sem_, name):
                    v.wait_ge(sem_, steps.at(now, name))

                def done(name):
                    return dve.tick(now, name)

                need(act, act_done, "lnf")
                v.tensor_scalar(k[:], k[:], noml[:, bass.ds(i, 1)], oml[:, bass.ds(i, 1)], ALU.mult, ALU.add).then_inc(dve_done, done("kf"))
                if now[0] == "pro":
                    v.wait_ge(dve_done, dve.at(pr, "reset_s"))
                v.tensor_tensor_scan(b[:], reset[:], b[:], 0.0, ALU.mult, ALU.add).then_inc(dve_done, done("scan"))
                need(dve, dve_done, "scan")
                bc = chunks(b[:, 0:SEQ])
                bs = b[:, SEQ:T].rearrange("p (b t) -> p b t", b=NB)
                tt(chunks(kD[:, 0:SEQ]), bc[:, :, P - 1:P].to_broadcast([P, NC, P]), bc, ALU.subtract).then_inc(dve_done, done("kDa"))
                tt(kD[:, SEQ:T].rearrange("p (b t) -> p b t", b=NB), bs[:, :, DEC - 1:DEC].to_broadcast([P, NB, DEC]), bs, ALU.subtract).then_inc(dve_done, done("kDs"))
                for h, d in ((64, d64), (32, d32)):
                    n = SEQ // (2 * h)
                    bh = b[:, 0:SEQ].rearrange("p (c s t) -> p c s t", s=2, t=h)
                    mid = bh[:, :, 0, h - 1:h].to_broadcast([P, n, h])
                    tt(d[:, :, 1, :], bh[:, :, 1, :], mid, ALU.subtract).then_inc(dve_done, done(f"a{h}q"))
                    tt(d[:, :, 0, :], mid, bh[:, :, 0, :], ALU.subtract).then_inc(dve_done, done(f"a{h}k"))
                bd = b[:, 0:SEQ].rearrange("p (c t) -> p c t", t=32)
                tt(cs[:, 0:32].rearrange("p (c o) -> p c o", o=1), bd[:, :, 0:1], bd[:, :, 31:32], ALU.add).then_inc(dve_done, done("cs"))
                tt(cs[:, 32:40].rearrange("p (c o) -> p c o", o=1), bs[:, :, 0:1], bs[:, :, DEC - 1:DEC], ALU.add).then_inc(dve_done, done("css"))
                need(dve, dve_done, "css")
                v.scalar_tensor_tensor(out=dk[:, 0:SEQ].rearrange("p (c t) -> p c t", t=32), in0=cs[:, 0:32].rearrange("p (c o) -> p c o", o=1).to_broadcast([P, 32, 32]),
                                       scalar=0.5, in1=bd, op0=ALU.mult, op1=ALU.subtract).then_inc(dve_done, done("xa"))
                v.scalar_tensor_tensor(out=dk[:, SEQ:T].rearrange("p (c t) -> p c t", t=DEC), in0=cs[:, 32:40].rearrange("p (c o) -> p c o", o=1).to_broadcast([P, NB, DEC]),
                                       scalar=0.5, in1=bs, op0=ALU.mult, op1=ALU.subtract).then_inc(dve_done, done("xas"))
                need(dve, dve_done, "xas")
                v.tensor_scalar(dk[:], dk[:], CLAMP, -CLAMP, ALU.min, ALU.max).then_inc(dve_done, done("xc"))

            exponents_of(pr, 0)
            for g in range(SLOTS):
                gated(pr, "q", g, q)
            for g in range(SLOTS):
                gated(pr, "z", g, zs)

            def head(i):
                now = now_of(i)
                prev = prev_of(i)
                last = is_last(i)

                def need(steps, sem_, name):
                    v.wait_ge(sem_, steps.at(now, name))

                def done(name):
                    return dve.tick(now, name)

                if not is_first(i):
                    need(act, act_done, "rx")
                    tt(ha[:, bass.ds(i - 1, 1), :], ha[:, bass.ds(i - 1, 1), :], rs[:].rearrange("p (o t) -> p o t", o=1), ALU.mult).then_inc(dve_done, done("ha"))
                v.wait_ge(dve_done, dve.at(prev, "q2"))
                need(act, act_done, "xkD")
                tt(kD[:], kD[:], k[:], ALU.mult).then_inc(dve_done, done("kD"))
                for h, d in ((64, d64), (32, d32)):
                    need(act, act_done, f"x{h}")
                    tt(d[:, :, 1, :], d[:, :, 1, :], q[:, 0:SEQ].rearrange("p (c s t) -> p c s t", s=2, t=h)[:, :, 1, :], ALU.mult).then_inc(dve_done, done(f"m{h}q"))
                    tt(d[:, :, 0, :], d[:, :, 0, :], k[:, 0:SEQ].rearrange("p (c s t) -> p c s t", s=2, t=h)[:, :, 0, :], ALU.mult).then_inc(dve_done, done(f"m{h}k"))
                need(act, act_done, "xdk")
                tt(dq[:], dq[:], q[:], ALU.mult).then_inc(dve_done, done("dqm"))
                tt(dk[:], dk[:], k[:], ALU.mult).then_inc(dve_done, done("dkm"))
                need(act, act_done, "xqI")
                tt(qI[:], qI[:], q[:], ALU.mult).then_inc(dve_done, done("qIm"))
                for n, bank in enumerate((ps_c, ps_d)):
                    need(pe, pe_done, f"kt{n}")
                    v.tensor_copy(k_tok[:, 4 * n:4 * n + 4, :], bank[:].rearrange("p (c v) -> p c v", c=4)).then_inc(dve_done, done(f"kt{n}"))
                need(pe, pe_done, "kts")
                v.tensor_copy(k_tok[0:NS, NC, :], ps_e[0:NS, P:2 * P]).then_inc(dve_done, done("kts"))
                for c in range(NC):
                    u = (ps_c, ps_d)[c // 4][:, (c % 4) * P:(c % 4 + 1) * P]
                    if c % 4 == 0:
                        need(pe, pe_done, f"u{c // 4}")
                    if c == 0:
                        v.tensor_copy(S[:, 0, :], u).then_inc(dve_done, done("s1"))
                        continue
                    need(dve, dve_done, f"s{c}")
                    if c == NC - 1:
                        need(pe, pe_done, "ps")
                    if c == NC - 1 and not is_first(i):
                        v.wait_ge(sp_stored, i * 16)
                    v.scalar_tensor_tensor(out=S[:, c, :], in0=S[:, c - 1, :], scalar=E[:, c:c + 1], in1=u,
                                           op0=ALU.mult, op1=ALU.add).then_inc(dve_done, done(f"s{c + 1}"))
                if is_first(i):
                    v.wait_ge(masks_loaded, 48)
                for n, bank in enumerate((ps_a, ps_b)):
                    v.copy_predicated(att[:, 4 * n:4 * n + 4, :], causal[:].rearrange("p (o t) -> p o t", o=1).to_broadcast([P, 4, P]),
                                      bank[:].rearrange("p (c t) -> p c t", c=4)).then_inc(dve_done, done(f"att{n}"))
                v.copy_predicated(att_s[:], causal_s[:], ps_e[0:NS, 256:256 + NS]).then_inc(dve_done, done("atts"))

                def gate(name, squared, bank, cols, src):
                    need(act, act_done, squared)
                    v.scalar_tensor_tensor(out=ha[:, bass.ds(i, 1), cols], in0=bank[:, src].rearrange("p (o t) -> p o t", o=1), scalar=par[:, 16:17],
                                           in1=zs[:, cols].rearrange("p (o t) -> p o t", o=1), op0=ALU.mult, op1=ALU.mult).then_inc(dve_done, done(name))

                if not last:
                    exponents_of(now, i + 1)
                    gated(now, "q", 0, q)
                gate("gate0", "sq0", ps_e, half(0), slice(0, 512))
                gate("gate1", "sq1", ps_c, half(1), slice(0, 512))
                gate("gates", "sqs", ps_d, slice(SEQ, T), slice(0, NS))
                if not last:
                    gated(now, "q", 1, q)
                need(pool, pool_done, "s0e")
                for n, bank in enumerate((ps_a, ps_b)):
                    need(pe, pe_done, f"us{n}")
                    tt(s0[:, 4 * n:4 * n + 4, :], s0[:, 4 * n:4 * n + 4, :], bank[:].rearrange("p (b v) -> p b v", b=4), ALU.add).then_inc(dve_done, done(f"so{n}"))
                if last:
                    need(act, act_done, "fx")
                    tt(ha[:, i, :], ha[:, i, :], rs[:], ALU.mult).then_inc(dve_done, done("hal"))
                    return
                gated(now, "q", 2, q)
                for g in range(SLOTS):
                    gated(now, "z", g, zs)

            head(0)
            with nc.vector.Fori(1, HEADS - 1) as i:
                head(i)
            head(HEADS - 1)

            def split_rows(phase, src, hi, lo):
                for n in range(KT):
                    v.wait_ge(act_done, act.at((phase, 0), f"h{n}"))
                    tt(lo[:, n, :], src[:, n, :], hi[:, n, :].bitcast(F32), ALU.subtract).then_inc(dve_done, dve.tick((phase, 0), f"l{n}"))

            split_rows("split_a", ha, hl_h, hl_l)
            one = lambda a: a.rearrange("p (o t) -> p o t", o=1)

            def merge_a(B, j):
                gate = ("last", 0) if isinstance(j, int) else ("pa", j - 1)
                for g in range(SLOTS):
                    v.wait_ge(act_done, act.at(gate, f"sg{g}"))
                    v.wait_ge(slot_done, B(1)[0] * 3 + (g + 1))
                    tt(mg[:, bass.ds(j, 1), span(g)], one(sg[:, span(g)]), one(pj[g][:, 0:W]), ALU.mult).then_inc(dve_done, dve.tick(("pa", j), f"m{g}"))

            merge_a(Blocks(GA, 2, 0), 0)
            with nc.vector.Fori(1, HEADS) as j:
                merge_a(Blocks(GA, 2, j), j)

            here = ("kv", 0)
            v.wait_ge(slopes_loaded, 64)
            for h in range(2):
                v.tensor_tensor_reduce(out=bias[:, h, 0:8], in0=sinks[:, 8 * h:8 * h + 8], in1=pick[:], scale=1.0, scalar=0.0,
                                       op0=ALU.mult, op1=ALU.add, accum_out=sinks_s[:, h:h + 1]).then_inc(dve_done, dve.tick(here, f"sel{h}"))
            v.wait_ge(pe_done, pe.at(here, "vt1"))
            v.tensor_copy(v_tk[:, 4:8, :], ps_b[:].rearrange("p (c v) -> p c v", c=4)).then_inc(dve_done, dve.tick(here, "vt1"))
            for g in range(SLOTS):
                gated(here, "z", g, zb)

            def negate(now, k, new, old, sink, scores_next=len(quarters)):
                v.tensor_scalar(new(0), old(0), sink(0), -1.0, ALU.max, ALU.mult).then_inc(dve_done, dve.tick(now, f"nm0_{k}"))
                if scores_next < len(quarters):
                    v.wait_ge(pe_done, pe.at(now, f"s{2 * scores_next + 1}"))
                v.tensor_scalar(new(1), old(1), sink(1), -1.0, ALU.max, ALU.mult).then_inc(dve_done, dve.tick(now, f"nm1_{k}"))

            def normalise(now, k, st, first, last, target, keys):
                v.wait_ge(act_done, act.at(now, f"p{last - 1}"))
                tt(st[:, 3, first:last], st[:, 3, first:last], st[:, 2, first:last], ALU.add).then_inc(dve_done, dve.tick(now, f"dn{k}"))
                v.wait_ge(dve_done, dve.at(now, f"dn{k}"))
                v.reciprocal(st[:, 4, first:last], st[:, 3, first:last]).then_inc(dve_done, dve.tick(now, f"rd{k}"))
                v.wait_ge(dve_done, dve.at(now, f"rd{k}"))
                for u in range(first, last):
                    v.tensor_scalar(target[:, u, keys(u)], target[:, u, keys(u)], st[:, 4, u:u + 1], None, ALU.mult).then_inc(dve_done, dve.tick(now, f"n{u}"))

            def pair(m):
                now = pair_of(m)
                last = is_last(m)
                keys = lambda u: slice(P if u < 2 else 0, 2 * P)
                for h in range(2):
                    v.tensor_scalar(bias[:, h, :], dist[:], slopes[:, bass.ds(m + 8 * h, 1)], None, ALU.mult).then_inc(dve_done, dve.tick(now, f"b{h}"))
                def biased(u):
                    n, h = u // 2, u % 2
                    (bank, o), lo = score_bank(n, h), P if n == 0 else 0
                    v.tensor_tensor_reduce(out=scores[:, u, lo:2 * P], in0=bank[:, o + lo:o + 2 * P], in1=bias[:, h, lo:2 * P],
                                           scale=1.0, scalar=-3e38, op0=ALU.add, op1=ALU.max,
                                           accum_out=stat[:, 0, u:u + 1]).then_inc(dve_done, dve.tick(now, f"t{u}"))

                v.wait_ge(pe_done, pe.at(now, "s1"))
                v.tensor_copy(sink_m[:].rearrange("p (h m) -> p h m", h=2), sinks[:].rearrange("p (h m) -> p h m", h=2)[:, :, bass.ds(m, 1)])\
                 .then_inc(dve_done, dve.tick(now, "sk"))
                v.wait_ge(dve_done, dve.at(now, "b1"))
                v.tensor_copy(q_s[:, :, bass.ds(m, 1), :], qT[:, SEQ:T].rearrange("p (b o t) -> p b o t", b=NB, o=1)).then_inc(dve_done, dve.tick(now, "qs"))
                for k in quarters:
                    for u in range(QU * k, QU * (k + 1)):
                        biased(u)
                    v.wait_ge(dve_done, dve.at(now, f"t{QU * k + QU - 1}"))
                    negate(now, k, lambda h: by_head(stat[:, 1, :], k)[:, h, :], lambda h: by_head(stat[:, 0, :], k)[:, h, :],
                           lambda h: sink_m[:, h:h + 1], scores_next=k + 1)
                v.tensor_copy(z_s[:, bass.ds(m, 1), :], one(zb[:, SEQ:T])).then_inc(dve_done, dve.tick(now, "zs"))
                for k in quarters:
                    normalise(now, k, stat, QU * k, QU * (k + 1), scores, keys)
                for n in range(1, NC, 2):
                    v.wait_ge(pe_done, pe.at(now, f"t{n}"))
                    if n >= 3:
                        v.wait_ge(pe_done, pe.at(now, f"o{n - 3}"))
                    src = (ps_a, ps_b, ps_c)[n % 3]
                    v.tensor_copy(PT[:, n % 3, :, :].rearrange("p a q -> p (a q)"), src[:]).then_inc(dve_done, dve.tick(now, f"pt{n}"))
                for n, bank in enumerate((ps_d, ps_e)):
                    v.wait_ge(pe_done, pe.at(now, f"o{4 * n + 3}"))
                    tt(hb[:, bass.ds(m, 1), half(n)], one(bank[:]), one(zb[:, half(n)]), ALU.mult).then_inc(dve_done, dve.tick(now, f"h{n}"))
                if not last:
                    for g in range(SLOTS):
                        gated(now, "z", g, zb)

            with nc.vector.Fori(0, HEADS - 1) as m:
                pair(m)
            pair(HEADS - 1)

            here = ("swa_s", 0)
            v.wait_ge(pe_done, pe.at(here, "ct1"))
            v.tensor_copy(ckT[:, 4:8, :], ps_b[:].rearrange("p (c v) -> p c v", c=4)).then_inc(dve_done, dve.tick(here, "ct1"))
            v.wait_ge(bias_s_loaded, 16)
            for u in range(4):
                bank, o = (ps_c, ps_d)[u // 2], (u % 2) * 2 * P
                v.wait_ge(pe_done, pe.at(here, f"s{u | 1}"))
                v.tensor_tensor_reduce(out=sc_s[:, u, :], in0=bank[:, o:o + P + NS], in1=bias_s[:, u, :], scale=1.0, scalar=-3e38,
                                       op0=ALU.add, op1=ALU.max, accum_out=stat_s[:, 0, u:u + 1]).then_inc(dve_done, dve.tick(here, f"t{u}"))
            v.wait_ge(dve_done, dve.at(here, "t3"))
            negate(here, 0, lambda h: stat_s[:, 1, 2 * h:2 * h + 2], lambda h: stat_s[:, 0, 2 * h:2 * h + 2], lambda h: sinks_s[:, h:h + 1])
            normalise(here, 0, stat_s, 0, 4, sc_s, lambda u: slice(0, P + NS))
            v.wait_ge(pe_done, pe.at(here, "pn"))
            v.tensor_copy(PT_n.rearrange("p a q -> p (a q)"), ps_b[0:NS, :]).then_inc(dve_done, dve.tick(here, "pn"))
            v.wait_ge(pe_done, pe.at(here, "o"))
            for_g = lambda a: a.rearrange("p g (b t) -> p g b t", t=DEC)
            tt(for_g(hb[:, :, SEQ:T]), ps_e[:, 0:2 * P].rearrange("p (b g t) -> p g b t", b=NB, g=HEADS), for_g(z_s[:]), ALU.mult).then_inc(dve_done, dve.tick(here, "h"))

            split_rows("split_b", hb, xn_h, xn_l)
            with nc.vector.Fori(0, 4) as j:
                B, now = Blocks(PB, 2, j), ("pb", j)
                for m in range(2):
                    for g in range(SLOTS):
                        s_, at = 3 * m + g, bass.ds(j * 2 + m, 1)
                        v.wait_ge(slot_done, B(m)[0] * 3 + (g + 1))
                        tt(sgb[:, at, span(g)], sgb[:, at, span(g)], one(pj[g][:, 0:W]), ALU.mult).then_inc(dve_done, dve.tick(now, f"g{s_}"))
                        v.wait_ge(dve_done, dve.at(now, f"g{s_}"))
                        tt(mg[:, at, span(g)], mg[:, at, span(g)], sgb[:, at, span(g)], ALU.add).then_inc(dve_done, dve.tick(now, f"m{s_}"))
            split_rows("split_m", mg, xn_h, xn_l)
            here = ("out", 0)
            v.wait_ge(g_fin_loaded, 16)
            for t in range(NC + 1):
                r = P if t < NC else NS
                v.wait_ge(xo_loaded[t % 3], 16 * (t // 3 + 1))
                if t >= 3:
                    v.wait_ge(y_stored[t % 3], 16 * (t // 3))
                for m in range(2):
                    v.wait_ge(pe_done, pe.at(here, f"{'ab'[m]}{t}"))
                    tt(y_o[t % 3][0:r, half(m)], bank_of(t, m)[0:r, :], x_o[t % 3][0:r, half(m)], ALU.add).then_inc(dve_done, dve.tick(here, f"y{'ab'[m]}{t}"))
                v.wait_ge(act_done, act.at(here, f"rs{t}"))
                v.scalar_tensor_tensor(out=y_o[t % 3][0:r, :], in0=y_o[t % 3][0:r, :], scalar=rstd[0:r, 1, t:t + 1], in1=g_fin[0:r, :],
                                       op0=ALU.mult, op1=ALU.mult).then_inc(dve_done, dve.tick(here, f"yn{t}"))


_INS = ["x_prompt", "x_sample", "state_hgrn", "cache_k", "cache_v", "norm_in", "w_in", "lb_logits", "a_gnorm",
        "b_sinks", "w_pa", "w_pb", "w_out", "norm_final"]
_CONSTS = ["c_ident", "c_causal", "c_causal_s", "c_batch", "c_dist", "c_slopes", "c_bias_s"]
_OUTS = [(1, 1024, 1024), (8, 4, 1024), (1, 1, 8, 128, 128), (1, 1, 128, 2, 64), (1, 1, 128, 2, 64),
         (1, 8, 8, 128, 128), (1, 8, 128, 2, 64), (1, 8, 128, 2, 64)]


def shape_constants():
    import numpy as np

    s, t = np.arange(P)[:, None], np.arange(P)[None, :]
    ss, st = np.arange(NS)[:, None], np.arange(NS)[None, :]
    dist = np.arange(P)[:, None] - (np.arange(2 * P)[None, :] - P)
    slopes = np.float32(2.0) ** (np.float32(-8.0) * np.arange(1, QH + 1, dtype=np.float32) / np.float32(QH))
    row = np.arange(P)
    bias_s = np.zeros((P, 4, P + NS), np.float32)
    for u in range(4):
        slope = slopes[8 * (u // 2) + row // DEC % 8][:, None]
        batch, query = (4 * (u % 2) + row // 32)[:, None], (row % DEC)[:, None]
        old, new = query + P - np.arange(P)[None, :], query - np.arange(NS)[None, :] % DEC
        bias_s[:, u, 0:P] = np.where(old < P, -slope * old, -1e30)
        bias_s[:, u, P:] = np.where((new >= 0) & (np.arange(NS)[None, :] // DEC == batch), -slope * new, -1e30)
    return {
        "c_ident": np.eye(P, dtype=np.float32),
        "c_causal": (s <= t).astype(np.int32),
        "c_causal_s": ((ss <= st) & (ss // DEC == st // DEC)).astype(np.int32),
        "c_dist": np.where((dist >= 0) & (dist < P), -dist, OFFSET).astype(np.float32),
        "c_slopes": np.concatenate([np.broadcast_to(slopes, (P, QH)), (row // DEC % 8)[:, None] == np.arange(8)], 1).astype(np.float32),
        "c_bias_s": bias_s,
        "c_batch": (ss // DEC == np.arange(NB)[None, :]).astype(np.float32),
    }


def kernel(**inputs):
    import numpy as _np
    import concourse.bacc as _bacc
    from concourse import mybir as _mybir
    from concourse.bass_utils import run_bass_kernel_spmd as _run

    nc = _bacc.Bacc("TRN2", target_bir_lowering=False, num_devices=1)
    constants = shape_constants()
    arrays, args = {}, []
    for name, a in [(n, inputs[n]) for n in _INS] + [(n, constants[n]) for n in _CONSTS]:
        a = _np.ascontiguousarray(a)
        arrays[f"in_{name}_dram"] = a
        args.append(nc.dram_tensor(f"in_{name}_dram", a.shape, _mybir.dt.from_np(a.dtype), kind="ExternalInput").ap())
    for i, shape in enumerate(_OUTS):
        args.append(nc.dram_tensor(f"out_{i}_dram", shape, _mybir.dt.float32, kind="ExternalOutput").ap())
    hybrid_step(nc, *args)
    r = _run(nc, [arrays], core_ids=[0])
    return tuple(r.results[0][f"out_{i}_dram"] for i in range(len(_OUTS)))
```

```python
from contextlib import ExitStack

import concourse.bass as bass
from concourse import mybir

F32 = mybir.dt.float32
F32R = mybir.dt.float32r
I32 = mybir.dt.int32
ALU = mybir.AluOpType
ACT = mybir.ActivationFunctionType

P = 128
D = 1024
KT = D // P
SEQ = 1024
NB, DEC = 8, 4
NS = NB * DEC
T = SEQ + NS
NC = SEQ // P
SLOTS = 3
W = T // SLOTS
HEADS = 8
QH, HD = 16, 64
EPS = 1e-6
QU = 4
OFFSET = -1e33
CLAMP = 85.0
WO_ORDER = [0, 1, 4, 2, 5, 3, 6, 7]
OFF = dict(q=0, f=1024, i=2048, z=3072, qb=4096, kb=5120, vb=5248, zb=5376, ga=6400, gb=7424)


class Steps:

    def __init__(self, order):
        self.base, self.names, self.now, total = {}, {}, {}, 0
        for phase, names, rounds, skip in order:
            assert len(set(names)) == len(names), phase
            self.base[phase], self.names[phase], self.now[phase] = total - skip, names, skip
            total += len(names) * rounds - skip

    def at(self, where, step):
        phase, i = where
        return i * len(self.names[phase]) + (self.base[phase] + self.names[phase].index(step) + 1)

    def tick(self, where, step):
        phase = where[0]
        want = self.names[phase][self.now[phase] % len(self.names[phase])]
        assert want == step, f"{phase}: {step} stands where {want} is due"
        self.now[phase] += 1
        return 1


class Blocks:

    def __init__(self, first, per, i):
        self.first, self.per, self.i = first, per, i

    def __call__(self, k):
        return (self.i * self.per + (self.first + k), (self.first + k) % 2,
                self.i * (self.per // 2) + (self.first + k) // 2)


def hybrid_step(nc, x_prompt, x_sample, state_hgrn, cache_k, cache_v, norm_in, w_in, lb_logits, a_gnorm,
                b_sinks, w_pa, w_pb, w_out, norm_final, c_ident, c_causal, c_causal_s, c_batch,
                c_dist, c_slopes, c_bias_s,
                y_prompt, y_sample, st_prompt, ck_prompt, cv_prompt, st_sample, ck_sample, cv_sample):
    each_slot = lambda s: [f"{s}{g}" for g in range(SLOTS)]
    each_tile = lambda s, first=0, last=KT: [f"{s}{n}" for n in range(first, last)]
    per_tile = lambda first, second: [f"{s}{t - d}" for t in range(NC + 2) for d, names in ((0, first), (1, second))
                                      for s in names if 0 <= t - d <= NC]
    quarters = range(2 * NC // QU)
    units = lambda s, k: [f"{s}{u}" for u in range(QU * k, QU * (k + 1))]
    exps = [x for k in quarters for x in [f"es0_{k}", f"es1_{k}"] + units("p", k)]
    softmax = (["b0", "b1", "sk", "qs"] + [x for k in quarters for x in units("t", k) + [f"nm0_{k}", f"nm1_{k}"]] + ["zs"]
               + [x for k in quarters for x in [f"dn{k}", f"rd{k}"] + units("n", k)])
    turn_order = ["t0", "t1", "t2"] + [x for n in range(NC) for x in [f"o{n}"] + ([f"t{n + 3}"] if n + 3 < NC else [])]
    norms = ["rl0", "rl1", "rls", "rx"]
    exponentials = ["v0", "ebl", "ebs", "xkD", "v1", "x64", "x32", "v2", "xdq", "xdk", "xqI"]
    turned = ["vt0", "vt1", "vts", "v3_hi", "v3_hi2"]
    squares_of_head = ["sq0", "sh0", "sq1", "sh1", "sqs", "shs"]
    act = Steps([
        ("pro", ["lb0", "lb1"] + per_tile(["ss", "ln", "rstd"], ["hi_a", "hi_b"]) + each_slot("sf") + ["lnf"]
         + each_slot("sigq") + each_slot("sigz"), 1, 0),
        ("head", norms + exponentials + turned + each_slot("sf") + ["lnf", "sigq0"] + squares_of_head
         + ["sigq1", "sigq2"] + each_slot("sigz"), HEADS - 1, len(norms)),
        ("last", norms + exponentials + turned + [f"k{g}{h}" for g in range(SLOTS) for h in "ab"] + squares_of_head
         + each_tile("h", 0, 3) + each_slot("sg") + each_tile("h", 3, 5) + ["fl0", "fl1", "fls", "fx"] + each_tile("h", 5), 1, 0),
        ("pa", each_slot("sg"), HEADS - 1, 0),
        ("kv", each_slot("v") + each_slot("q") + ["vt0", "vts", "kt", "ks"] + each_slot("sigz"), 1, 0),
        ("swa", exps + ["q0", "q1", "pt0", "q2", "pt2", "pt4", "pt6"] + each_slot("sigz"), HEADS - 1, 0),
        ("swa_l", exps + ["pt0", "pt2", "pt4", "pt6"], 1, 0),
        ("swa_s", ["g0", "g1", "g2", "ct0", "es0_0", "es1_0"] + units("p", 0) + ["pt", "g3", "g4", "g5"], 1, 0),
        ("gb", [f"g{n}" for n in range(2 * SLOTS)], HEADS // 2 - 2, 0),
        ("gb_l", ["g0", "g1", "g2"] + each_tile("h", 0, KT - 1) + ["g3", "g4", "g5", "h7"], 1, 0),
        ("pb_l", each_tile("h"), 1, 0),
        ("out", [f"{s}{t}" for t in range(NC + 1) for s in ("ss", "ln", "rs")], 1, 0),
    ])
    exponents = ["kf", "scan", "kDa", "kDs", "a64q", "a64k", "a32q", "a32k", "cs", "css", "xa", "xas", "xc"]
    products = ["kD", "m64q", "m64k", "m32q", "m32k", "dqm", "dkm", "qIm", "kt0", "kt1", "kts", "k3_hi", "k3_hi2", "k3_lo"]
    chain = [f"s{c}" for c in range(1, NC + 1)]
    masked = ["att0", "att1", "atts"]
    gated_head = ["gate0", "gate1", "gates", "sl0", "sl1", "sls"]
    merged = [f"{s}{n}" for n in range(2 * SLOTS) for s in "gm"]
    dve = Steps([
        ("pro", ["par", "lbm", "lbd0", "lbd1", "lbs", "lbr", "lb", "oml", "noml", "mean"] + per_tile(["xn"], ["lo_a", "lo_b"])
         + ["att0", "atts0", "zkT0", "zkT1", "reset", "reset_p", "reset_s"] + exponents + each_slot("q") + each_slot("z"), 1, 0),
        ("head", ["ha"] + products + chain + masked + exponents + ["q0"] + gated_head
         + ["q1", "so0", "so1", "q2"] + each_slot("z"), HEADS - 1, 1),
        ("last", ["ha"] + products + chain + masked + gated_head + ["so0", "so1"]
         + each_tile("l", 0, 5) + ["hal"] + each_tile("l", 5), 1, 0),
        ("pa", each_slot("m"), HEADS, 0),
        ("kv", ["sel0", "sel1", "vt1"] + each_slot("z"), 1, 0),
        ("swa", softmax + ["pt1", "pt3", "pt5", "pt7", "h0", "h1"] + each_slot("z"), HEADS - 1, 0),
        ("swa_l", softmax + ["pt1", "pt3", "pt5", "pt7", "h0", "h1"], 1, 0),
        ("swa_s", ["ct1"] + units("t", 0) + ["nm0_0", "nm1_0", "dn0", "rd0"] + units("n", 0) + ["pn", "h"], 1, 0),
        ("gb_l", each_tile("l"), 1, 0),
        ("pb", merged, HEADS // 2 - 1, 0),
        ("pb_l", merged[:2 * SLOTS] + each_tile("l", 0, KT - 1) + merged[2 * SLOTS:] + ["l7"], 1, 0),
        ("out", [f"{s}{t}" for t in range(NC + 1) for s in ("ya", "yb", "yn")], 1, 0),
    ])
    head_products = ["vt0", "vt1", "vts", "kt0", "kt1", "kts", "p0", "p1", "ps", "u0", "u1",
                     "o0", "o1", "os", "us0", "us1", "ms0", "ms1", "mss"]
    pe = Steps([
        ("pro", ["par"] + [f"{s}{t}" for t in range(NC + 1) for s in ("xa", "xb")], 1, 0),
        ("head", head_products, HEADS - 1, 0),
        ("last", head_products, 1, 0),
        ("kv", ["vt0", "vt1", "vts", "kt"], 1, 0),
        ("swa", [f"s{n}" for n in range(NC)] + turn_order, HEADS - 1, 0),
        ("swa_l", [f"s{n}" for n in range(NC)] + turn_order, 1, 0),
        ("swa_s", ["ct0", "ct1", "s0", "s1", "s2", "s3", "pt", "pn", "o"], 1, 0),
        ("out", [f"{s}{t}" for s in "ab" for t in range(4)] + [f"{s}{t}" for t in range(4, NC + 1) for s in "ab"], 1, 0),
    ])
    pool = Steps([
        ("pro", ["eps"], 1, 0),
        ("head", ["v3_lo", "vexp", "s0e"], HEADS - 1, 0),
        ("last", ["v3_lo", "vexp", "s0e"], 1, 0),
    ])

    ctx = ExitStack()
    with ctx:
        def sb(name, shape, dt=F32, where=ctx):
            return where.enter_context(nc.sbuf_tensor(name, shape, dt))

        def sem(name):
            return ctx.enter_context(nc.semaphore(name))

        pj = [ctx.enter_context(nc.psum_tensor(f"pj{g}", [P, 512], F32)) for g in range(SLOTS)]
        ps_a, ps_b, ps_c, ps_d, ps_e = [ctx.enter_context(nc.psum_tensor(f"ps_{n}", [P, 512], F32)) for n in "abcde"]

        xn_h = sb("xn_h", [P, KT, T], F32R)
        xn_l = sb("xn_l", [P, KT, T], F32R)
        w_raw = [sb(f"w_raw{p}", [P, KT, P]) for p in range(2)]
        w_h = [sb(f"w_h{p}", [P, KT, P], F32R) for p in range(2)]
        w_l = [sb(f"w_l{p}", [P, KT, P], F32R) for p in range(2)]
        kT = sb("kT", [P, 2, T])
        ident = sb("ident", [P, P])
        mean_m = sb("mean_m", [P, P], F32R)
        par = sb("par", [P, 32])
        lb = sb("lb", [P, HEADS])
        oml = sb("oml", [P, HEADS])
        noml = sb("noml", [P, HEADS])
        lbt = sb("lbt", [P, 3, HEADS])
        rstd = sb("rstd", [P, 2, NC + 1])
        eps = sb("eps", [P, 1])
        mg_area = ExitStack()
        ha = sb("ha", [P, HEADS, T], where=mg_area)
        mg_area.close()
        mg = sb("mg", [P, HEADS, T], where=mg_area)
        mg_area.close()
        x_o = [sb(f"x_o{n}", [P, D], where=mg_area) for n in range(3)]
        y_o = [sb(f"y_o{n}", [P, D], where=mg_area) for n in range(3)]
        y_sq = sb("y_sq", [P, D], where=mg_area)
        g_fin = sb("g_fin", [P, D], where=mg_area)
        sb("mg_pad", [P, HEADS * (T - D)], where=mg_area)
        ctx.enter_context(mg_area)

        area = ExitStack()
        q = sb("q", [P, T], where=area)
        k = sb("k", [P, T], where=area)
        b = sb("b", [P, T], where=area)
        d64 = sb("d64", [P, NC, 2, 64], where=area)
        d32 = sb("d32", [P, 2 * NC, 2, 32], where=area)
        dq = sb("dq", [P, T], where=area)
        dk = sb("dk", [P, T], where=area)
        kD = sb("kD", [P, T], where=area)
        E = sb("E", [P, NC + NB], where=area)
        cs = sb("cs", [P, 32 + NB], where=area)
        sb("area_pad", [P, 8], where=area)
        vT = sb("vT", [P, T], where=area)
        v_tok = sb("v_tok", [P, NC + 1, P], where=area)
        k_tok = sb("k_tok", [P, NC + 1, P], where=area)
        att = sb("att", [P, NC, P], where=area)
        v_exp = sb("v_exp", [3 * NS, NB, P], F32R, where=area)
        zs = sb("zs", [P, T], where=area)
        s0 = sb("s0", [P, NB, P], where=area)
        S = sb("S", [P, NC, P], where=area)
        qI = sb("qI", [P, T], where=area)
        rs = qI
        att_s = sb("att_s", [NS, NS], where=area)
        reset = sb("reset", [P, T], mybir.dt.bfloat16, where=area)
        causal = sb("causal", [P, P], I32, where=area)
        causal_s = sb("causal_s", [NS, NS], I32, where=area)
        batch_m = sb("batch_m", [3 * NS, NB], where=area)
        k3 = sb("k3", [3 * NS, P], F32R, where=area)
        v3 = sb("v3", [3 * NS, P], F32R, where=area)
        area.close()

        area = ExitStack()
        sb("sq_pad0", [P, 6 * T + 2 * D + 64], where=area)
        sq_l = sb("sq_l", [P, T], F32R, where=area)
        sb("sq_pad1", [P, 2 * (NC + 1) * P + 4 * D + T], where=area)
        sq_h = sb("sq_h", [P, T], F32R, where=area)
        area.close()

        area = ExitStack()
        sg = sb("sg", [P, T], where=area)
        hl_h = sb("hl_h", [P, KT, T], F32R, where=area)
        hl_l = sb("hl_l", [P, KT, T], F32R, where=area)
        area.close()

        area = ExitStack()
        hb = sb("hb", [P, HEADS, T], where=area)
        swa = ExitStack()
        zb = sb("zb", [P, T], where=swa)
        k_out = sb("k_out", [P, 2, P], where=swa)
        dist = sb("dist", [P, 2 * P], where=swa)
        bias = sb("bias", [P, 2, 2 * P], where=swa)
        sb("gate_pad", [P, T - 8 * P], where=swa)
        v_tk = sb("v_tk", [P, NC + 1, P], where=swa)
        qT = sb("qT", [P, T], where=swa)
        PT = sb("PT", [P, 3, 4, P], where=swa)
        q_s = sb("q_s", [P, NB, HEADS, DEC], where=swa)
        z_s = sb("z_s", [P, HEADS, NS], where=swa)
        stat = sb("stat", [P, 5, 2 * NC], where=swa)
        sinks = sb("sinks", [P, QH], where=swa)
        pick = sb("pick", [P, HEADS], where=swa)
        sink_m = sb("sink_m", [P, 2], where=swa)
        sinks_s = sb("sinks_s", [P, 2], where=swa)
        slopes = sb("slopes", [P, QH], where=swa)
        stat_s = sb("stat_s", [P, 5, 4], where=swa)
        sc = ExitStack()
        scores = sb("scores", [P, 2 * NC, 2 * P], where=sc)
        sc.close()
        ck = sb("ck", [P, NB, P], where=sc)
        cv = sb("cv", [P, NB, P], where=sc)
        ckT = sb("ckT", [P, NB, P], where=sc)
        sc_s = sb("sc_s", [P, 4, P + NS], where=sc)
        sc.close()
        swa.close()
        sgb = sb("sgb", [P, HEADS, T], where=area)
        wo_raw = sb("wo_raw", [P, KT, P], where=area)
        area.close()
        bias_s = qT[:, 0:4 * (P + NS)].rearrange("p (u k) -> p u k", u=4)
        PT_s = PT[:, 0, :, :]
        PT_n = PT[0:NS, 1, :, :]

        area = ExitStack()
        wo_h0 = sb("wo_h0", [P, KT, 512], F32R, where=area)
        wo_l0 = sb("wo_l0", [P, KT, 512], F32R, where=area)
        sb("wo_pad", [P, HEADS * T - 2 * KT * 512], where=area)
        wo_1 = sb("wo_1", [P, HEADS, T], F32R, where=area)
        area.close()
        wo_at = lambda c, lo: ((wo_h0, wo_l0)[lo][:, :, c * P:(c + 1) * P] if c < 4 else
                               wo_1[:, 2 * (c - 4) + lo, 0:D].rearrange("p (k c) -> p k c", k=KT))
        wo_rhs = lambda m, lo, kt: (wo_h0, wo_l0)[lo][:, kt, :] if m == 0 else wo_1[:, lo:HEADS:2, kt * P:(kt + 1) * P]

        area = ExitStack()
        x_t = [sb(f"x_t{n}", [P, D], where=area) for n in range(NC + 1)]
        x_sq = sb("x_sq", [P, D], where=area)
        x_n = [sb(f"x_n{n}", [P, D], where=area) for n in range(3)]
        g_row = sb("g_row", [P, D], where=area)
        rows = sb("rows", [32, P], where=area)
        area.close()

        act_done, dve_done, pe_done, pool_done = sem("act_done"), sem("dve_done"), sem("pe_done"), sem("pool_done")
        w_loaded = [sem("w_loaded0"), sem("w_loaded1")]
        w_hi_ready, w_lo_ready, slot_done = sem("w_hi_ready"), sem("w_lo_ready"), sem("slot_done")
        gb_tile_read, pb_tile_read = sem("gb_tile_read"), sem("pb_tile_read")
        wo_loaded, wo_hi_ready, wo_lo_ready = sem("wo_loaded"), sem("wo_hi_ready"), sem("wo_lo_ready")
        x_loaded = [sem(f"x_loaded{t}") for t in range(NC + 1)]
        consts_loaded, g_loaded, masks_loaded, g_fin_loaded = sem("consts_loaded"), sem("g_loaded"), sem("masks_loaded"), sem("g_fin_loaded")
        s0_loaded, slopes_loaded, caches_loaded, bias_s_loaded = sem("s0_loaded"), sem("slopes_loaded"), sem("caches_loaded"), sem("bias_s_loaded")
        xo_loaded = [sem(f"xo_loaded{n}") for n in range(3)]
        s0_stored, sp_stored, caches_stored = sem("s0_stored"), sem("sp_stored"), sem("caches_stored")
        y_stored = [sem(f"y_stored{n}") for n in range(3)]

        w_pa_v = w_pa[0].rearrange("(k p) c -> p k c", p=P)
        w_pb_v = w_pb[0].rearrange("(s k d) c -> s d k c", s=2, d=HD)
        w_out_v = w_out[0].rearrange("(k p) c -> p k c", p=P)
        GA = 3 + 4 * HEADS - 2
        KV = GA + 2 * HEADS
        QZ = KV + 1
        GB = QZ + 2 * HEADS
        PB = GB + HEADS
        bank_of = lambda t, n: ([ps_a, ps_b, ps_c, ps_d, ps_e] + pj)[t % 4 + 4 * n]
        score_bank = lambda n, h: ((ps_a, ps_b, ps_c, ps_d)[n % 4], h * 2 * P)
        pair_of = lambda m: ("swa_l", 0) if is_last(m) else ("swa", m)
        w_in_v = w_in[0].rearrange("(k p) c -> p k c", p=P)
        st_in = state_hgrn[0].rearrange("b h k v -> k b h v")
        st_out = st_sample[0].rearrange("b h k v -> k b h v")
        sp_out = st_prompt[0, 0].rearrange("h k v -> k h v")
        span = lambda g: slice(g * W, (g + 1) * W)
        chunks = lambda a: a.rearrange("p (c t) -> p c t", c=NC)
        part = {"0": slice(0, 512), "1": slice(512, SEQ), "s": slice(SEQ, T)}
        half = lambda g: slice(g * 512, (g + 1) * 512)
        by_head = lambda a, k: a.rearrange("p (k n h) -> p k h n", h=2, n=QU // 2)[:, k, :, :]
        now_of = lambda i: ("last", 0) if is_last(i) else ("head", i)
        prev_of = lambda i: ("pro", 0) if is_first(i) else ("head", i - 1)
        is_first = lambda i: isinstance(i, int) and i == 0
        is_last = lambda i: isinstance(i, int) and i == HEADS - 1
        turn_banks = lambda t: (((ps_a, ps_c, ps_e)[t % 3], "a"), ((ps_b, ps_d, pj[2])[t % 3], "b"))
        tile_rows = lambda t: P if t < NC else NS
        head_blocks = lambda i: Blocks(3, 4, i)

        block = ctx.enter_context(nc.Block())

        @block.sync
        def _(sp):
            def load(B, src, col):
                n, p, _ = B
                if not (isinstance(n, int) and n < 2):
                    sp.wait_ge(w_lo_ready, n - 1)
                for r in range(2):
                    sp.dma_start(w_raw[p][:, 4 * r:4 * r + 4, :], src[:, 4 * r:4 * r + 4, bass.ds(col, P)]).then_inc(w_loaded[p], 16)

            def token_rows(prompt, sample, t):
                return prompt[0, t * P:(t + 1) * P, :] if t < NC else sample.rearrange("b t d -> (b t) d")

            def load_tokens(t):
                sp.dma_start(x_t[t][0:tile_rows(t), :], token_rows(x_prompt, x_sample, t)).then_inc(x_loaded[t], 16)

            pro = Blocks(0, 1, 0)
            load_tokens(0)
            sp.dma_start(ident[:], c_ident).then_inc(consts_loaded, 16)
            sp.dma_start(rows[0:16, :], lb_logits.rearrange("l (h p) -> (l h) p", p=P)).then_inc(consts_loaded, 16)
            sp.dma_start(rows[16:17, :], a_gnorm).then_inc(consts_loaded, 16)
            sp.dma_start(g_row[:], norm_in.to_broadcast([P, D])).then_inc(g_loaded, 16)
            load_tokens(1)
            load(pro(0), w_in_v, OFF["f"])
            for t in range(2, NC + 1):
                load_tokens(t)
            load(pro(1), w_in_v, OFF["q"])
            load(pro(2), w_in_v, OFF["z"])
            sp.wait_ge(pe_done, pe.at(("pro", 0), f"xb{NC}"))
            sp.dma_start(causal[:], c_causal).then_inc(masks_loaded, 16)
            sp.dma_start(causal_s[:], c_causal_s).then_inc(masks_loaded, 16)
            sp.dma_start(batch_m[:], c_batch).then_inc(masks_loaded, 16)

            def head(i):
                B = head_blocks(i)
                now = now_of(i)
                if is_first(i):
                    sp.dma_start(s0[:], st_in[:, :, 0, :]).then_inc(s0_loaded, 16)
                if is_last(i):
                    load(B(1), w_in_v, OFF["kb"])
                    load(B(2), w_in_v, OFF["ga"])
                    load(B(3), w_pa_v, 0)
                    load(B(4), w_in_v, OFF["ga"] + P)
                else:
                    load(B(1), w_in_v, i * P + (OFF["f"] + P))
                    load(B(2), w_in_v, i * P + (OFF["q"] + P))
                    load(B(3), w_in_v, i * P + (OFF["z"] + P))
                    load(B(4), w_in_v, i * P + (OFF["i"] + P))
                sp.wait_ge(dve_done, dve.at(now, "s8"))
                sp.dma_start(sp_out[:, bass.ds(i, 1), :], S[:, NC - 1:NC, :]).then_inc(sp_stored, 16)
                sp.wait_ge(dve_done, dve.at(now, "so1"))
                sp.dma_start(st_out[:, :, bass.ds(i, 1), :], s0[:].rearrange("p b (o v) -> p b o v", o=1)).then_inc(s0_stored, 16)
                if not is_last(i):
                    sp.wait_ge(s0_stored, i * 16 + 16)
                    sp.dma_start(s0[:].rearrange("p b (o v) -> p b o v", o=1), st_in[:, :, bass.ds(i + 1, 1), :]).then_inc(s0_loaded, 16)

            load(head_blocks(0)(0), w_in_v, OFF["i"])
            head(0)
            with nc.sync.Fori(1, HEADS - 1) as i:
                head(i)
            head(HEADS - 1)

            with nc.sync.Fori(1, HEADS - 1) as j:
                B = Blocks(GA, 2, j)
                load(B(1), w_pa_v, j * P)
                load(B(2), w_in_v, j * P + (OFF["ga"] + P))
            load(Blocks(GA, 2, HEADS - 1)(1), w_pa_v, (HEADS - 1) * P)
            load(Blocks(KV, 1, 0)(0), w_in_v, OFF["vb"])
            def load_pair(B, off, m):
                n, p, _ = B
                sp.wait_ge(w_lo_ready, n - 1)
                for r in range(2):
                    sp.dma_start(w_raw[p][:, :, r * HD:(r + 1) * HD],
                                 w_in_v[:, :, bass.ds(m * HD + (off + r * QH // 2 * HD), HD)]).then_inc(w_loaded[p], 16)

            qz = Blocks(QZ, 2, 0)
            load_pair(qz(0), OFF["qb"], 0)
            load_pair(qz(1), OFF["zb"], 0)
            sp.wait_ge(slot_done, SLOTS * KV)
            sp.dma_start(dist[:], c_dist).then_inc(slopes_loaded, 16)
            sp.dma_start(slopes[:], c_slopes[:, 0:QH]).then_inc(slopes_loaded, 16)
            sp.dma_start(pick[:], c_slopes[:, QH:QH + 8]).then_inc(slopes_loaded, 16)
            sp.dma_start(sinks[:], b_sinks.to_broadcast([P, QH])).then_inc(slopes_loaded, 16)

            load_pair(qz(2), OFF["qb"], 1)
            load_pair(qz(3), OFF["zb"], 1)
            for new, old in ((ck_sample, cache_k), (cv_sample, cache_v)):
                sp.dma_start(new[0, :, 0:P - DEC].rearrange("b t h d -> b (t h d)"),
                             old[0, :, DEC:P].rearrange("b t h d -> b (t h d)")).then_inc(caches_stored, 16)
            sp.wait_ge(act_done, act.at(("kv", 0), "ks"))
            sp.wait_ge(dve_done, dve.at(("kv", 0), "vt1"))
            sp.dma_start(ck_prompt[0, 0].rearrange("t h d -> t (h d)"), k_out[:, 0, :]).then_inc(caches_stored, 16)
            sp.dma_start(cv_prompt[0, 0].rearrange("t h d -> t (h d)"), v_tk[:, NC - 1, :]).then_inc(caches_stored, 16)
            for m in range(NB):
                rows_m = slice(DEC * m, DEC * (m + 1))
                sp.dma_start(ck_sample[0, m, P - DEC:P].rearrange("t h d -> t (h d)"), k_out[rows_m, 1, :]).then_inc(caches_stored, 16)
                sp.dma_start(cv_sample[0, m, P - DEC:P].rearrange("t h d -> t (h d)"), v_tk[rows_m, NC, :]).then_inc(caches_stored, 16)
            with nc.sync.Fori(1, HEADS - 1) as m:
                B = Blocks(QZ, 2, m)
                load_pair(B(2), OFF["qb"], m + 1)
                load_pair(B(3), OFF["zb"], m + 1)
            gb = Blocks(GB, 2, 0)
            load(gb(0), w_in_v, OFF["gb"])
            load(gb(1), w_in_v, OFF["gb"] + P)
            sp.wait_ge(pe_done, pe.at(("swa_l", 0), "t7"))
            sp.wait_ge(dve_done, dve.at(("swa_l", 0), "n15"))
            sp.dma_start(ck[:], cache_k[0].rearrange("b t h d -> t b (h d)")).then_inc(caches_loaded, 16)
            sp.dma_start(cv[:], cache_v[0].rearrange("b t h d -> t b (h d)")).then_inc(caches_loaded, 16)
            sp.dma_start(bias_s, c_bias_s).then_inc(bias_s_loaded, 16)

            def load_pb(B, col):
                n, p, _ = B
                sp.wait_ge(w_lo_ready, n - 1)
                for r in range(2):
                    sp.dma_start(w_raw[p][r * HD:(r + 1) * HD, :, :], w_pb_v[r, :, :, bass.ds(col, P)]).then_inc(w_loaded[p], 16)

            with nc.sync.Fori(0, 3) as j:
                B = Blocks(GB, 2, j)
                load(B(2), w_in_v, j * (2 * P) + (OFF["gb"] + 2 * P))
                load(B(3), w_in_v, j * (2 * P) + (OFF["gb"] + 3 * P))
            pb = Blocks(PB, 2, 0)
            load_pb(pb(0), 0)
            load_pb(pb(1), P)

            def load_wo(n):
                if n == 0:
                    sp.wait_ge(dve_done, dve.at(("swa_s", 0), "h"))
                else:
                    sp.wait_ge(wo_lo_ready, n)
                sp.dma_start(wo_raw[:], w_out_v[:, :, bass.ds(WO_ORDER[n] * P, P)]).then_inc(wo_loaded, 16)

            load_wo(0)
            for j in range(3):
                load_pb(Blocks(PB, 2, j)(2), (2 * j + 2) * P)
                load_pb(Blocks(PB, 2, j)(3), (2 * j + 3) * P)
                load_wo(2 * j + 1)
                load_wo(2 * j + 2)
            load_wo(7)

            sp.wait_ge(dve_done, dve.at(("pb_l", 0), "l7"))
            sp.dma_start(g_fin[:], norm_final.rearrange("(o d) -> o d", o=1).to_broadcast([P, D])).then_inc(g_fin_loaded, 16)

            def load_x(t):
                r = P if t < NC else NS
                sp.dma_start(x_o[t % 3][0:r, :], token_rows(x_prompt, x_sample, t)).then_inc(xo_loaded[t % 3], 16)

            for t in range(3):
                load_x(t)
            for t in range(NC + 1):
                r = P if t < NC else NS
                sp.wait_ge(dve_done, dve.at(("out", 0), f"yn{t}"))
                sp.dma_start(token_rows(y_prompt, y_sample, t), y_o[t % 3][0:r, :]).then_inc(y_stored[t % 3], 16)
                if t + 3 < NC + 1:
                    load_x(t + 3)
            for n in range(3):
                sp.wait_ge(y_stored[n], 16 * 3)
            sp.wait_ge(sp_stored, 16 * HEADS)
            sp.wait_ge(s0_stored, 16 * HEADS)
            sp.wait_ge(caches_stored, 16 * (4 + 2 * NB))

        @block.gpsimd
        def _(g):
            def split_lo(B):
                n, p, _ = B
                g.wait_ge(w_hi_ready, n + 1)
                g.tensor_tensor(w_l[p][:], w_raw[p][:], w_h[p][:].bitcast(F32), ALU.subtract).then_inc(w_lo_ready, 1)

            pro = Blocks(0, 1, 0)
            g.memset(eps[:], EPS).then_inc(pool_done, pool.tick(("pro", 0), "eps"))
            for n in range(3):
                split_lo(pro(n))

            def head(i):
                B, now = head_blocks(i), now_of(i)
                split_lo(B(0))
                split_lo(B(1))
                if is_first(i):
                    g.wait_ge(masks_loaded, 48)
                g.wait_ge(act_done, act.at(now, "v3_hi2"))
                g.tensor_tensor(v3[NS:2 * NS, :], v_tok[0:NS, NC, :], v3[0:NS, :].bitcast(F32), ALU.subtract).then_inc(pool_done, pool.tick(now, "v3_lo"))
                g.wait_ge(pool_done, pool.at(now, "v3_lo"))
                g.tensor_tensor(v_exp[:], v3[:].bitcast(F32).rearrange("p (o v) -> p o v", o=1).to_broadcast([3 * NS, NB, P]),
                                batch_m[:].rearrange("p (b o) -> p b o", o=1).to_broadcast([3 * NS, NB, P]),
                                ALU.mult).then_inc(pool_done, pool.tick(now, "vexp"))
                split_lo(B(2))
                g.wait_ge(pe_done, pe.at(now, "os"))
                g.tensor_tensor(s0[:], s0[:], E[:, NC:NC + NB].rearrange("p (b o) -> p b o", o=1).to_broadcast([P, NB, P]),
                                ALU.mult).then_inc(pool_done, pool.tick(now, "s0e"))
                split_lo(B(3))
                if is_last(i):
                    split_lo(B(4))

            head(0)
            with nc.gpsimd.Fori(1, HEADS - 1) as i:
                head(i)
            head(HEADS - 1)
            with nc.gpsimd.Fori(1, HEADS) as j:
                B = Blocks(GA, 2, j)
                split_lo(B(1))
                split_lo(B(2))
            for n in range(4):
                split_lo(Blocks(QZ, 2, 0)(n))
            with nc.gpsimd.Fori(0, HEADS - 1) as m:
                B = Blocks(QZ, 2, m)
                split_lo(B(4))
                split_lo(B(5))
            with nc.gpsimd.Fori(0, 4) as j:
                B = Blocks(GB, 2, j)
                split_lo(B(2))
                split_lo(B(3))

            def wo_split_lo(n):
                c = WO_ORDER[n]
                g.wait_ge(wo_hi_ready, n + 1)
                g.tensor_tensor(wo_at(c, 1), wo_raw[:], wo_at(c, 0).bitcast(F32), ALU.subtract).then_inc(wo_lo_ready, 1)

            wo_split_lo(0)
            for j in range(3):
                split_lo(Blocks(PB, 2, j)(2))
                split_lo(Blocks(PB, 2, j)(3))
                wo_split_lo(2 * j + 1)
                wo_split_lo(2 * j + 2)
            wo_split_lo(7)

        @block.scalar
        def _(a):
            pr = ("pro", 0)
            nc.scalar.preload_act_table_set("natural_log_exp_and_others")

            def split_hi(B):
                n, p, h = B
                a.wait_ge(w_loaded[p], h * 32 + 32)
                if not (isinstance(n, int) and n < 2):
                    a.wait_ge(slot_done, n * 3 - 3)
                a.activation(w_h[p][:], w_raw[p][:], ACT.Copy).then_inc(w_hi_ready, 1)

            a.wait_ge(dve_done, dve.at(pr, "lbd1"))
            a.activation(lbt[:, 0, :], lbt[:, 0, :], ACT.Exp).then_inc(act_done, act.tick(pr, "lb0"))
            a.activation(lbt[:, 1, :], lbt[:, 1, :], ACT.Exp).then_inc(act_done, act.tick(pr, "lb1"))
            a.wait_ge(pool_done, pool.at(pr, "eps"))
            pro = Blocks(0, 1, 0)
            for t in range(NC + 2):
                if t <= NC:
                    r = tile_rows(t)
                    a.wait_ge(x_loaded[t], 16)
                    if t:
                        a.wait_ge(act_done, act.at(pr, f"ss{t - 1}"))
                    a.activation(x_sq[0:r], x_t[t][0:r, :], ACT.Square, accum_out=rstd[0:r, 0, t:t + 1]).then_inc(act_done, act.tick(pr, f"ss{t}"))
                    a.wait_ge(act_done, act.at(pr, f"ss{t}"))
                    a.activation(rstd[0:r, 0, t:t + 1], rstd[0:r, 0, t:t + 1], ACT.Ln, scale=1.0 / D, bias=eps[0:r]).then_inc(act_done, act.tick(pr, f"ln{t}"))
                    a.wait_ge(act_done, act.at(pr, f"ln{t}"))
                    a.activation(rstd[0:r, 1, t:t + 1], rstd[0:r, 0, t:t + 1], ACT.Exp, scale=-0.5).then_inc(act_done, act.tick(pr, f"rstd{t}"))
                if t >= 1:
                    u = t - 1
                    for n, (bank, s) in enumerate(turn_banks(u)):
                        a.wait_ge(pe_done, pe.at(pr, f"x{s}{u}"))
                        a.activation(xn_h[:, 4 * n:4 * n + 4, u * P:u * P + tile_rows(u)], bank[:].rearrange("p (k t) -> p k t", k=4)[:, :, 0:tile_rows(u)],
                                     ACT.Copy).then_inc(act_done, act.tick(pr, f"hi_{s}{u}"))
                if t in (1, NC):
                    split_hi(pro(t // NC))

            def sig(where, name, n_slot, g, out):
                a.wait_ge(slot_done, n_slot)
                a.activation(out[:, span(g)], pj[g][:, 0:W], ACT.Sigmoid).then_inc(act_done, act.tick(where, f"{name}{g}"))

            def copy(where, name, n_slot, g, out, scale=1.0):
                a.wait_ge(slot_done, n_slot)
                a.activation(out[:, span(g)], pj[g][:, 0:W], ACT.Copy, scale=scale).then_inc(act_done, act.tick(where, f"{name}{g}"))

            def round_tile(where, n, src, hi):
                a.activation(hi[:, n, :], src[:, n, :], ACT.Copy).then_inc(act_done, act.tick(where, f"h{n}"))

            def log_f(where, i):
                nc.scalar.preload_act_table_set("natural_log_exp_and_others")
                a.wait_ge(act_done, act.at(where, "sf2"))
                a.activation(b[:], k[:], ACT.Ln, scale=oml[:, bass.ds(i, 1)], bias=lb[:, bass.ds(i, 1)]).then_inc(act_done, act.tick(where, "lnf"))
                nc.scalar.preload_act_table(ACT.Sigmoid)

            for n, (name, out) in enumerate((("sf", k), ("sigq", q), ("sigz", zs))):
                for g in range(SLOTS):
                    sig(pr, name, 3 * n + g + 1, g, out)
                if n == 0:
                    log_f(pr, 0)
                if n + 2 < 4:
                    split_hi(pro(n + 2) if n == 0 else head_blocks(0)(0))

            def head(i):
                B, now = head_blocks(i), now_of(i)
                prev = prev_of(i)
                last = is_last(i)
                if not is_first(i):
                    nc.scalar.preload_act_table_set("natural_log_exp_and_others")
                    a.wait_ge(pe_done, pe.at(prev, "mss"))
                    a.activation(rs[:, half(0)], ps_a[:], ACT.Ln, bias=eps[:]).then_inc(act_done, act.tick(now, "rl0"))
                    a.activation(rs[:, half(1)], ps_b[:], ACT.Ln, bias=eps[:]).then_inc(act_done, act.tick(now, "rl1"))
                    a.activation(rs[:, SEQ:T], ps_d[:, 64:64 + NS], ACT.Ln, bias=eps[:]).then_inc(act_done, act.tick(now, "rls"))
                    a.wait_ge(act_done, act.at(now, "rls"))
                    a.activation(rs[:], rs[:], ACT.Exp, scale=-0.5).then_inc(act_done, act.tick(now, "rx"))
                if is_first(i):
                    nc.scalar.preload_act_table_set("natural_log_exp_and_others")
                split_hi(B(1))

                def v_copy(g):
                    a.wait_ge(slot_done, B(0)[0] * 3 + (g + 1))
                    a.activation(vT[:, span(g)], pj[g][:, 0:W], ACT.Copy).then_inc(act_done, act.tick(now, f"v{g}"))

                def exp(name, need, out, src, scale=1.0):
                    a.wait_ge(dve_done, dve.at(prev, need))
                    a.activation(out, src, ACT.Exp, scale=scale).then_inc(act_done, act.tick(now, name))

                v_copy(0)
                if not is_first(i):
                    a.wait_ge(pool_done, pool.at(prev, "s0e"))
                exp("ebl", "scan", E[:, 0:NC], chunks(b[:, 0:SEQ])[:, :, P - 1])
                exp("ebs", "scan", E[:, NC:NC + NB], b[:, SEQ:T].rearrange("p (b t) -> p b t", b=NB)[:, :, DEC - 1])
                exp("xkD", "kDs", kD[:], kD[:])
                v_copy(1)
                exp("x64", "a64k", d64[:], d64[:])
                exp("x32", "a32k", d32[:], d32[:])
                v_copy(2)
                split_hi(B(2))
                exp("xdq", "xc", dq[:], dk[:], -1.0)
                exp("xdk", "xc", dk[:], dk[:])
                if not is_first(i):
                    a.wait_ge(dve_done, dve.at(now, "ha"))
                exp("xqI", "scan", qI[:], b[:])
                for n, (bank, cols) in enumerate(((ps_a, slice(0, 4)), (ps_b, slice(4, 8)))):
                    a.wait_ge(pe_done, pe.at(now, f"vt{n}"))
                    a.activation(v_tok[:, cols, :], bank[:].rearrange("p (c v) -> p c v", c=4), ACT.Copy).then_inc(act_done, act.tick(now, f"vt{n}"))
                a.wait_ge(pe_done, pe.at(now, "vts"))
                a.activation(v_tok[0:NS, NC, :], ps_e[0:NS, 0:P], ACT.Copy).then_inc(act_done, act.tick(now, "vts"))
                a.wait_ge(act_done, act.at(now, "vts"))
                a.activation(v3[0:NS, :], v_tok[0:NS, NC, :], ACT.Copy).then_inc(act_done, act.tick(now, "v3_hi"))
                a.activation(v3[2 * NS:3 * NS, :], v_tok[0:NS, NC, :], ACT.Copy).then_inc(act_done, act.tick(now, "v3_hi2"))

                def squares():
                    for n, src in (("0", ps_e[:]), ("1", ps_c[:]), ("s", ps_d[:, 0:NS])):
                        a.wait_ge(pe_done, pe.at(now, f"o{n}"))
                        a.activation(vT[:, part[n]], src, ACT.Square).then_inc(act_done, act.tick(now, f"sq{n}"))
                        a.activation(sq_h[:, part[n]], src, ACT.Square).then_inc(act_done, act.tick(now, f"sh{n}"))

                if last:
                    for g in range(SLOTS):
                        a.wait_ge(slot_done, B(1)[0] * 3 + (g + 1))
                        for h in range(2):
                            rows_h = slice(h * HD, (h + 1) * HD)
                            a.activation(kT[rows_h, h, span(g)], pj[g][rows_h, 0:W], ACT.Copy).then_inc(act_done, act.tick(now, f"k{g}{'ab'[h]}"))
                    split_hi(B(3))
                    squares()
                    a.wait_ge(pool_done, pool.at(now, "s0e"))
                    a.wait_ge(dve_done, dve.at(now, "gates"))
                    for n in range(3):
                        round_tile(now, n, ha, hl_h)
                    nc.scalar.preload_act_table(ACT.Sigmoid)
                    for g in range(SLOTS):
                        sig(now, "sg", B(2)[0] * 3 + (g + 1), g, sg)
                    nc.scalar.preload_act_table_set("natural_log_exp_and_others")
                    for n in (3, 4):
                        round_tile(now, n, ha, hl_h)
                    a.wait_ge(pe_done, pe.at(now, "mss"))
                    for n, src in (("0", ps_a[:]), ("1", ps_b[:]), ("s", ps_d[:, 64:64 + NS])):
                        a.activation(rs[:, part[n]], src, ACT.Ln, bias=eps[:]).then_inc(act_done, act.tick(now, f"fl{n}"))
                    a.wait_ge(act_done, act.at(now, "fls"))
                    a.activation(rs[:], rs[:], ACT.Exp, scale=-0.5).then_inc(act_done, act.tick(now, "fx"))
                    for n in (5, 6):
                        round_tile(now, n, ha, hl_h)
                    a.wait_ge(dve_done, dve.at(now, "hal"))
                    round_tile(now, 7, ha, hl_h)
                    split_hi(B(4))
                    nc.scalar.preload_act_table(ACT.Sigmoid)
                    return
                nc.scalar.preload_act_table(ACT.Sigmoid)
                a.wait_ge(dve_done, dve.at(now, "qIm"))
                for g in range(SLOTS):
                    sig(now, "sf", B(1)[0] * 3 + (g + 1), g, k)
                log_f(now, i + 1)
                split_hi(B(3))
                sig(now, "sigq", B(2)[0] * 3 + 1, 0, q)
                squares()
                for g in (1, 2):
                    sig(now, "sigq", B(2)[0] * 3 + (g + 1), g, q)
                split_hi(B(4))
                a.wait_ge(dve_done, dve.at(now, "gates"))
                for g in range(SLOTS):
                    sig(now, "sigz", B(3)[0] * 3 + (g + 1), g, zs)

            head(0)
            with nc.scalar.Fori(1, HEADS - 1) as i:
                head(i)
            head(HEADS - 1)

            with nc.scalar.Fori(1, HEADS) as j:
                B = Blocks(GA, 2, j)
                split_hi(B(1))
                for g in range(SLOTS):
                    a.wait_ge(dve_done, dve.at(("pa", j - 1), f"m{g}"))
                    sig(("pa", j - 1), "sg", B(0)[0] * 3 + (g + 1), g, sg)
                split_hi(B(2))

            qz, here = Blocks(QZ, 2, 0), ("kv", 0)
            split_hi(qz(0))
            a.wait_ge(dve_done, dve.at(("pa", HEADS - 1), "m2"))
            for g in range(SLOTS):
                copy(here, "v", 3 * KV + g + 1, g, zb)
            split_hi(qz(1))
            for g in range(SLOTS):
                copy(here, "q", 3 * QZ + g + 1, g, qT, HD ** -0.5)
            a.wait_ge(pe_done, pe.at(here, "vt0"))
            a.activation(v_tk[:, 0:4, :], ps_a[:].rearrange("p (c v) -> p c v", c=4), ACT.Copy).then_inc(act_done, act.tick(here, "vt0"))
            a.wait_ge(pe_done, pe.at(here, "vts"))
            a.activation(v_tk[0:NS, NC, :], ps_c[0:NS, 0:P], ACT.Copy).then_inc(act_done, act.tick(here, "vts"))
            a.wait_ge(pe_done, pe.at(here, "kt"))
            two_heads = lambda a: a.rearrange("p (h x) -> p h x", h=2)[:, :, 0:HD]
            a.activation(k_out[:, 0, :].rearrange("p (h d) -> p h d", h=2), two_heads(ps_d[:, 0:6 * HD]), ACT.Copy).then_inc(act_done, act.tick(here, "kt"))
            a.activation(k_out[0:NS, 1, :].rearrange("p (h d) -> p h d", h=2), two_heads(ps_e[0:NS, 0:6 * HD]), ACT.Copy).then_inc(act_done, act.tick(here, "ks"))
            split_hi(qz(2))
            for g in range(SLOTS):
                sig(here, "sigz", 3 * (QZ + 1) + g + 1, g, zb)
            split_hi(qz(3))

            def pair(m):
                B, now = Blocks(QZ, 2, m), pair_of(m)
                last = is_last(m)
                nc.scalar.preload_act_table_set("natural_log_exp_and_others")
                for k in quarters:
                    for h in range(2):
                        a.wait_ge(dve_done, dve.at(now, f"nm{h}_{k}"))
                        a.activation(by_head(stat[:, 2, :], k)[:, h, :], by_head(stat[:, 1, :], k)[:, h, :], ACT.Exp,
                                     bias=sink_m[:, h:h + 1]).then_inc(act_done, act.tick(now, f"es{h}_{k}"))
                    for u in range(QU * k, QU * (k + 1)):
                        keys = slice(P if u < 2 else 0, 2 * P)
                        a.activation(scores[:, u, keys], scores[:, u, keys], ACT.Exp, bias=stat[:, 1, u:u + 1],
                                     accum_out=stat[:, 3, u:u + 1]).then_inc(act_done, act.tick(now, f"p{u}"))

                def queries(g):
                    if not last:
                        copy(now, "q", B(2)[0] * 3 + (g + 1), g, qT, HD ** -0.5)

                if not last:
                    a.wait_ge(pe_done, pe.at(now, "s7"))
                    a.wait_ge(dve_done, dve.at(now, "qs"))
                for g in range(2):
                    queries(g)
                for n in range(0, NC, 2):
                    if n == 2:
                        queries(2)
                        if not last:
                            split_hi(B(4))
                    a.wait_ge(pe_done, pe.at(now, f"t{n}"))
                    if n >= 3:
                        a.wait_ge(pe_done, pe.at(now, f"o{n - 3}"))
                    fill = slice(P if n == 0 else 0, 4 * P)
                    src = (ps_a, ps_b, ps_c)[n % 3]
                    a.activation(PT[:, n % 3, :, :].rearrange("p a q -> p (a q)")[:, fill], src[:, fill], ACT.Copy).then_inc(act_done, act.tick(now, f"pt{n}"))
                if not last:
                    nc.scalar.preload_act_table(ACT.Sigmoid)
                    a.wait_ge(dve_done, dve.at(now, "h1"))
                    for g in range(SLOTS):
                        sig(now, "sigz", B(3)[0] * 3 + (g + 1), g, zb)
                    split_hi(B(5))

            with nc.scalar.Fori(0, HEADS - 1) as m:
                pair(m)
            pair(HEADS - 1)

            here = ("swa_s", 0)

            def gate_b(where, step, B, at, g):
                a.wait_ge(slot_done, B[0] * 3 + (g + 1))
                a.activation(sgb[:, at, span(g)], pj[g][:, 0:W].rearrange("p (o t) -> p o t", o=1), ACT.Sigmoid)\
                 .then_inc(act_done, act.tick(where, step))

            gb = Blocks(GB, 2, 0)
            nc.scalar.preload_act_table(ACT.Sigmoid)
            a.wait_ge(dve_done, dve.at(("swa_l", 0), "h1"))
            a.wait_ge(caches_stored, 16 * (4 + 2 * NB))
            for g in range(SLOTS):
                gate_b(here, f"g{g}", gb(0), slice(0, 1), g)
            nc.scalar.preload_act_table_set("natural_log_exp_and_others")
            a.wait_ge(pe_done, pe.at(here, "ct0"))
            a.activation(ckT[:, 0:4, :], ps_a[:].rearrange("p (c v) -> p c v", c=4), ACT.Copy).then_inc(act_done, act.tick(here, "ct0"))
            split_hi(gb(2))
            for h in range(2):
                a.wait_ge(dve_done, dve.at(here, f"nm{h}_0"))
                a.activation(stat_s[:, 2, 2 * h:2 * h + 2], stat_s[:, 1, 2 * h:2 * h + 2], ACT.Exp, bias=sinks_s[:, h:h + 1]).then_inc(act_done, act.tick(here, f"es{h}_0"))
            for u in range(4):
                a.activation(sc_s[:, u, :], sc_s[:, u, :], ACT.Exp, bias=stat_s[:, 1, u:u + 1], accum_out=stat_s[:, 3, u:u + 1]).then_inc(act_done, act.tick(here, f"p{u}"))
            a.wait_ge(pe_done, pe.at(here, "pt"))
            a.activation(PT_s.rearrange("p a q -> p (a q)"), ps_a[:], ACT.Copy).then_inc(act_done, act.tick(here, "pt"))
            nc.scalar.preload_act_table(ACT.Sigmoid)
            for g in range(SLOTS):
                gate_b(here, f"g{3 + g}", gb(1), slice(1, 2), g)
            split_hi(gb(3))
            a.wait_ge(dve_done, dve.at(here, "h"))
            with nc.scalar.Fori(1, 3) as j:
                B = Blocks(GB, 2, j)
                for m in range(2):
                    for g in range(SLOTS):
                        gate_b(("gb", j - 1), f"g{3 * m + g}", B(m), bass.ds(j * 2 + m, 1), g)
                    split_hi(B(2 + m))
            here, gb = ("gb_l", 0), Blocks(GB, 2, 3)
            for g in range(SLOTS):
                gate_b(here, f"g{g}", gb(0), slice(6, 7), g)
            split_hi(gb(2))
            for n in range(KT):
                if n < KT - 1:
                    a.wait_ge(gb_tile_read, n + 1)
                else:
                    for g in range(SLOTS):
                        gate_b(here, f"g{3 + g}", gb(1), slice(7, 8), g)
                round_tile(here, n, hb, xn_h)
            split_hi(gb(3))

            def wo_split_hi(n):
                a.wait_ge(wo_loaded, 16 * (n + 1))
                a.activation(wo_at(WO_ORDER[n], 0), wo_raw[:], ACT.Copy).then_inc(wo_hi_ready, 1)

            a.wait_ge(dve_done, dve.at(("gb_l", 0), "l7"))
            wo_split_hi(0)
            for j in range(3):
                split_hi(Blocks(PB, 2, j)(2))
                split_hi(Blocks(PB, 2, j)(3))
                wo_split_hi(2 * j + 1)
                a.wait_ge(dve_done, dve.at(("pb", j), "m5"))
                wo_split_hi(2 * j + 2)
            for n in range(KT):
                if n < KT - 1:
                    a.wait_ge(pb_tile_read, n + 1)
                if n >= KT - 2:
                    a.wait_ge(dve_done, dve.at(("pb_l", 0), "m2" if n == KT - 2 else "m5"))
                round_tile(("pb_l", 0), n, mg, xn_h)
            wo_split_hi(7)
            nc.scalar.preload_act_table_set("natural_log_exp_and_others")
            here = ("out", 0)
            for t in range(NC + 1):
                r = P if t < NC else NS
                a.wait_ge(dve_done, dve.at(here, f"yb{t}"))
                if t:
                    a.wait_ge(act_done, act.at(here, f"rs{t - 1}"))
                else:
                    a.wait_ge(dve_done, dve.at(("pb_l", 0), "l7"))
                a.activation(y_sq[0:r], y_o[t % 3][0:r, :], ACT.Square, accum_out=rstd[0:r, 0, t:t + 1]).then_inc(act_done, act.tick(here, f"ss{t}"))
                a.wait_ge(act_done, act.at(here, f"ss{t}"))
                a.activation(rstd[0:r, 0, t:t + 1], rstd[0:r, 0, t:t + 1], ACT.Ln, scale=1.0 / D, bias=eps[0:r]).then_inc(act_done, act.tick(here, f"ln{t}"))
                a.wait_ge(act_done, act.at(here, f"ln{t}"))
                a.activation(rstd[0:r, 1, t:t + 1], rstd[0:r, 0, t:t + 1], ACT.Exp, scale=-0.5).then_inc(act_done, act.tick(here, f"rs{t}"))

        @block.tensor
        def _(t):
            pr = ("pro", 0)

            def slot(B, g, xh=xn_h, xl=xn_l):
                n, p, _ = B
                if g == 0:
                    t.wait_ge(w_hi_ready, n + 1)
                    t.wait_ge(w_lo_ready, n + 1)
                passes = ((w_h[p], xh), (w_h[p], xl), (w_l[p], xh))
                for kt in range(KT):
                    for m, (w, x) in enumerate(passes):
                        mm = nc.tensor.matmul(pj[g][:, 0:W], w[:, kt, :], x[:, kt, span(g)],
                                              start=(kt == 0 and m == 0), stop=(kt == KT - 1 and m == 2))
                mm.then_inc(slot_done, 1)

            def slots(B, xh, xl, split=None, tile_read=None):
                n, p, _ = B
                t.wait_ge(w_hi_ready, n + 1)
                t.wait_ge(w_lo_ready, n + 1)
                passes = ((w_h[p], xh), (w_h[p], xl), (w_l[p], xh))
                for kt in range(KT):
                    if split:
                        t.wait_ge(dve_done, dve.at((split, 0), f"l{kt}"))
                    for g in range(SLOTS):
                        for m, (w, x) in enumerate(passes):
                            mm = nc.tensor.matmul(pj[g][:, 0:W], w[:, kt, :], x[:, kt, span(g)],
                                                  start=(kt == 0 and m == 0), stop=(kt == KT - 1 and m == 2))
                        if kt == KT - 1:
                            mm.then_inc(slot_done, 1)
                    if tile_read and kt < KT - 1:
                        mm.then_inc(tile_read, 1)

            t.wait_ge(consts_loaded, 48)
            nc.tensor.transpose(ps_e[:, 0:17], rows[0:17, :], ident[0:17, 0:17]).then_inc(pe_done, pe.tick(pr, "par"))
            pro = Blocks(0, 1, 0)
            for n in range(NC + 1):
                r = tile_rows(n)
                t.wait_ge(dve_done, dve.at(pr, f"xn{n}"))
                for m, (bank, s) in enumerate(turn_banks(n)):
                    if n >= 3:
                        t.wait_ge(act_done, act.at(pr, f"hi_{s}{n - 3}"))
                        t.wait_ge(dve_done, dve.at(pr, f"lo_{s}{n - 3}"))
                    for j in range(4):
                        kt = 4 * m + j
                        mm = nc.tensor.transpose(bank[:, j * P:j * P + r], x_n[n % 3][0:r, kt * P:(kt + 1) * P], ident[0:r, 0:r])
                    mm.then_inc(pe_done, pe.tick(pr, f"x{s}{n}"))
                for g in range(SLOTS):
                    done = -(-(g + 1) * W // P) - 1
                    if n == min(done + 1, NC):
                        t.wait_ge(act_done, act.at(pr, f"hi_b{done}"))
                        t.wait_ge(dve_done, dve.at(pr, f"lo_b{done}"))
                        slot(pro(0), g)
            for g in range(SLOTS):
                t.wait_ge(act_done, act.at(pr, f"sf{g}"))
                slot(pro(1), g)
            for g in range(SLOTS):
                t.wait_ge(dve_done, dve.at(pr, f"q{g}"))
                slot(pro(2), g)

            def head(i):
                B, now = head_blocks(i), now_of(i)
                prev = prev_of(i)
                last = is_last(i)

                def turn(bank, at, src, cols, name):
                    for j, c in enumerate(cols):
                        r = P if c < NC else NS
                        mm = nc.tensor.transpose(bank[0:r, at + j * P:at + (j + 1) * P], src[:, c * P:c * P + r], ident[:, :])
                    mm.then_inc(pe_done, pe.tick(now, name))

                def gate_slot(k_block, name, by, g):
                    if last and k_block == 3:
                        return
                    step = f"k{g}b" if last and k_block == 2 else f"{name}{g}"
                    t.wait_ge(by[0], by[1].at(now, step))
                    slot(B(k_block), g)

                for g in range(SLOTS):
                    t.wait_ge(dve_done, dve.at(prev, f"z{g}"))
                    slot(B(0), g)
                gate_slot(1, "v", (act_done, act), 0)
                t.wait_ge(act_done, act.at(now, "v2"))
                turn(ps_a, 0, vT, range(0, 4), "vt0")
                turn(ps_b, 0, vT, range(4, 8), "vt1")
                turn(ps_e, 0, vT, [NC], "vts")

                t.wait_ge(dve_done, dve.at(now, "kD"))
                turn(ps_c, 0, kD, range(0, 4), "kt0")
                turn(ps_d, 0, kD, range(4, 8), "kt1")
                t.wait_ge(act_done, act.at(now, "vts"))
                turn(ps_e, P, kD, [NC], "kts")
                gate_slot(1, "v", (act_done, act), 1)
                t.wait_ge(dve_done, dve.at(now, "dkm"))
                for n, bank in enumerate((ps_a, ps_b)):
                    for j in range(4):
                        c, o = 4 * n + j, j * P
                        nc.tensor.matmul(bank[0:64, o + 64:o + 128], d64[:, c, 0, :], d64[:, c, 1, :], start=True, stop=True)
                        for m in range(2):
                            nc.tensor.matmul(bank[64 * m:64 * m + 32, o + 64 * m + 32:o + 64 * m + 64],
                                             d32[:, 2 * c + m, 0, :], d32[:, 2 * c + m, 1, :], start=True, stop=True)
                        for m in range(4):
                            e = c * P + 32 * m
                            mm = nc.tensor.matmul(bank[32 * m:32 * m + 32, o + 32 * m:o + 32 * m + 32],
                                                  dk[:, e:e + 32], dq[:, e:e + 32], start=True, stop=True)
                    mm.then_inc(pe_done, pe.tick(now, f"p{n}"))
                gate_slot(1, "v", (act_done, act), 2)
                t.wait_ge(act_done, act.at(now, "vts"))
                t.wait_ge(dve_done, dve.at(now, "kts"))
                nc.tensor.matmul(ps_e[0:NS, 256:256 + NS], dk[:, SEQ:T], dq[:, SEQ:T], start=True, stop=True).then_inc(pe_done, pe.tick(now, "ps"))
                for n, bank in enumerate((ps_c, ps_d)):
                    for j in range(4):
                        c = 4 * n + j
                        mm = nc.tensor.matmul(bank[:, j * P:(j + 1) * P], k_tok[:, c, :], v_tok[:, c, :], start=True, stop=True)
                    mm.then_inc(pe_done, pe.tick(now, f"u{n}"))
                gate_slot(2, "sf", (act_done, act), 0)
                gate_slot(2, "sf", (act_done, act), 1)
                t.wait_ge(dve_done, dve.at(now, "atts"))
                t.wait_ge(dve_done, dve.at(now, "qIm"))
                for n, bank in enumerate((ps_e, ps_c)):
                    for j in range(4):
                        c = 4 * n + j
                        mm = nc.tensor.matmul(bank[:, j * P:(j + 1) * P], v_tok[:, c, :], att[:, c, :], start=True, stop=(c == 0))
                        if c:
                            mm = nc.tensor.matmul(bank[:, j * P:(j + 1) * P], S[:, c - 1, :], qI[:, c * P:(c + 1) * P], start=False, stop=True)
                    mm.then_inc(pe_done, pe.tick(now, f"o{n}"))
                t.wait_ge(s0_loaded, i * 16 + 16)
                nc.tensor.matmul(ps_d[:, 0:NS], v_tok[0:NS, NC, :], att_s[:, :], start=True, stop=True)
                for m in range(NB):
                    e = SEQ + DEC * m
                    mm = nc.tensor.matmul(ps_d[:, DEC * m:DEC * (m + 1)], s0[:, m, :], qI[:, e:e + DEC], start=False, stop=True, skip_group_check=True)
                mm.then_inc(pe_done, pe.tick(now, "os"))
                gate_slot(2, "sf", (act_done, act), 2)
                t.wait_ge(pool_done, pool.at(now, "vexp"))
                for n, bank in enumerate((ps_a, ps_b)):
                    nc.tensor.matmul(bank[:, :], k3[:, :], v_exp[:, 4 * n:4 * n + 4, :].rearrange("p b v -> p (b v)"),
                                     start=True, stop=True).then_inc(pe_done, pe.tick(now, f"us{n}"))
                gate_slot(3, "q", (dve_done, dve), 0)
                t.wait_ge(dve_done, dve.at(now, "so1"))
                for n, bank in (("0", ps_a[:, :]), ("1", ps_b[:, :]), ("s", ps_d[:, 64:64 + NS])):
                    nc.tensor.matmul(bank, mean_m[:, :], sq_h[:, part[n]], start=True, stop=False)
                    nc.tensor.matmul(bank, mean_m[:, :], sq_l[:, part[n]], start=False, stop=True).then_inc(pe_done, pe.tick(now, f"ms{n}"))
                gate_slot(3, "q", (dve_done, dve), 1)
                gate_slot(3, "q", (dve_done, dve), 2)

            head(0)
            with nc.tensor.Fori(1, HEADS - 1) as i:
                head(i)
            head(HEADS - 1)

            t.wait_ge(act_done, act.at(("last", 0), "sg2"))
            slots(Blocks(GA, 2, 0)(1), hl_h, hl_l, split="last")
            with nc.tensor.Fori(1, HEADS) as j:
                B = Blocks(GA, 2, j)
                for g in range(SLOTS):
                    t.wait_ge(dve_done, dve.at(("pa", j - 1), f"m{g}"))
                    slot(B(0), g)
                for g in range(SLOTS):
                    t.wait_ge(act_done, act.at(("pa", j - 1), f"sg{g}"))
                    slot(B(1), g, hl_h, hl_l)

            qz, here = Blocks(QZ, 2, 0), ("kv", 0)
            for g in range(SLOTS):
                t.wait_ge(dve_done, dve.at(("pa", HEADS - 1), f"m{g}"))
                slot(Blocks(KV, 1, 0)(0), g)
            for g in range(SLOTS):
                t.wait_ge(act_done, act.at(here, f"v{g}"))
                slot(qz(0), g)
            for n, bank in enumerate((ps_a, ps_b)):
                for j in range(4):
                    c = 4 * n + j
                    mm = nc.tensor.transpose(bank[:, j * P:(j + 1) * P], zb[:, c * P:(c + 1) * P], ident[:, :])
                mm.then_inc(pe_done, pe.tick(here, f"vt{n}"))
            nc.tensor.transpose(ps_c[0:NS, 0:P], zb[:, SEQ:T], ident[:, :]).then_inc(pe_done, pe.tick(here, "vts"))
            for h in range(2):
                nc.tensor.transpose(ps_d[:, h * P:(h + 1) * P], kT[:, h, SEQ - P:SEQ], ident[:, :])
                mm = nc.tensor.transpose(ps_e[0:NS, h * P:(h + 1) * P], kT[:, h, SEQ:T], ident[:, :])
            mm.then_inc(pe_done, pe.tick(here, "kt"))
            for g in range(SLOTS):
                t.wait_ge(act_done, act.at(here, f"q{g}"))
                slot(qz(1), g)

            def pair(m):
                B, now = Blocks(QZ, 2, m), pair_of(m)
                prev = ("swa", m - 1)
                last = is_last(m)
                z_prev = lambda g: dve.at(prev, f"z{g}")
                t.wait_ge(dve_done, dve.at(prev, "h1"))
                for n in range(NC):
                    if n >= 4:
                        t.wait_ge(dve_done, dve.at(now, f"t{2 * (n - 4) + 1}"))
                    for h in range(2):
                        bank, o = score_bank(n, h)
                        lo = P if n == 0 else 0
                        mm = nc.tensor.matmul(bank[:, o + lo:o + 2 * P], qT[:, n * P:(n + 1) * P],
                                              kT[:, h, (n - 1) * P + lo:(n + 1) * P], start=True, stop=True)
                    mm.then_inc(pe_done, pe.tick(now, f"s{n}"))
                nxt = Blocks(GB, 2, 0)(0) if last else B(2)

                def next_slot(g):
                    t.wait_ge(dve_done, z_prev(g))
                    slot(nxt, g)

                for g in range(2):
                    next_slot(g)

                def turn(n):
                    bank = (ps_a, ps_b, ps_c)[n % 3]
                    t.wait_ge(dve_done, dve.at(now, f"n{2 * n + 1}"))
                    if n >= 3:
                        if n % 2:
                            t.wait_ge(act_done, act.at(now, f"pt{n - 3}"))
                        else:
                            t.wait_ge(dve_done, dve.at(now, f"pt{n - 3}"))
                    for h in range(2):
                        for w in range(1 if n == 0 else 0, 2):
                            o = (2 * h + w) * P
                            mm = nc.tensor.transpose(bank[:, o:o + P], scores[:, 2 * n + h, w * P:(w + 1) * P], ident[:, :])
                    mm.then_inc(pe_done, pe.tick(now, f"t{n}"))

                def out(n):
                    bank, o = (ps_d, ps_e)[n // 4], (n % 4) * P
                    if n % 2:
                        t.wait_ge(dve_done, dve.at(now, f"pt{n}"))
                    else:
                        t.wait_ge(act_done, act.at(now, f"pt{n}"))
                    for w in range(1 if n == 0 else 0, 2):
                        for h in range(2):
                            rows_h = slice(h * HD, (h + 1) * HD)
                            mm = nc.tensor.matmul(bank[rows_h, o:o + P], v_tk[:, n - 1 + w, rows_h], PT[:, n % 3, 2 * h + w, :],
                                                  start=(w == 0 or n == 0), stop=(w == 1))
                    mm.then_inc(pe_done, pe.tick(now, f"o{n}"))

                for n in range(3):
                    turn(n)
                next_slot(2)
                for n in range(NC):
                    out(n)
                    if n + 3 < NC:
                        turn(n + 3)
                if not last:
                    for g in range(SLOTS):
                        t.wait_ge(act_done, act.at(now, f"q{g}"))
                        slot(B(3), g)

            t.wait_ge(act_done, act.at(("kv", 0), "ks"))
            t.wait_ge(dve_done, dve.at(("kv", 0), "vt1"))
            with nc.tensor.Fori(0, HEADS - 1) as m:
                pair(m)
            pair(HEADS - 1)

            here, gb = ("swa_s", 0), Blocks(GB, 2, 0)
            t.wait_ge(act_done, act.at(here, "g0"))
            slot(gb(1), 0)
            t.wait_ge(caches_loaded, 32)
            t.wait_ge(dve_done, dve.at(("swa_l", 0), "h1"))
            for n, bank in enumerate((ps_a, ps_b)):
                for j in range(4):
                    mm = nc.tensor.transpose(bank[:, j * P:(j + 1) * P], ck[:, 4 * n + j, :], ident[:, :])
                mm.then_inc(pe_done, pe.tick(here, f"ct{n}"))
            t.wait_ge(act_done, act.at(here, "ct0"))
            t.wait_ge(dve_done, dve.at(here, "ct1"))
            for u in range(4):
                h, grp = u // 2, u % 2
                rows_h = slice(h * HD, (h + 1) * HD)
                bank, o = (ps_c, ps_d)[h], grp * 2 * P
                for j in range(4):
                    m = 4 * grp + j
                    q_m = q_s[rows_h, m, :, :].rearrange("p g t -> p (g t)")
                    nc.tensor.matmul(bank[32 * j:32 * j + 32, o:o + P], q_m, ckT[rows_h, m, :], start=True, stop=True)
                    mm = nc.tensor.matmul(bank[32 * j:32 * j + 32, o + P:o + P + NS], q_m, kT[rows_h, h, SEQ:T], start=True, stop=True)
                mm.then_inc(pe_done, pe.tick(here, f"s{u}"))
            for g in (1, 2):
                t.wait_ge(act_done, act.at(here, f"g{g}"))
                slot(gb(1), g)
            t.wait_ge(dve_done, dve.at(here, "n3"))
            for u in range(4):
                mm = nc.tensor.transpose(ps_a[:, u * P:(u + 1) * P], sc_s[:, u, 0:P], ident[:, :])
            mm.then_inc(pe_done, pe.tick(here, "pt"))
            for u in range(4):
                mm = nc.tensor.transpose(ps_b[0:NS, u * P:(u + 1) * P], sc_s[:, u, P:P + NS], ident[:, :])
            mm.then_inc(pe_done, pe.tick(here, "pn"))
            t.wait_ge(act_done, act.at(here, "pt"))
            t.wait_ge(dve_done, dve.at(here, "pn"))
            for u in range(4):
                h, grp = u // 2, u % 2
                rows_h = slice(h * HD, (h + 1) * HD)
                nc.tensor.matmul(ps_e[rows_h, grp * P:(grp + 1) * P], v_tk[0:NS, NC, rows_h], PT_n[:, u, :], start=True, stop=True)
                for j in range(4):
                    o = grp * P + 32 * j
                    mm = nc.tensor.matmul(ps_e[rows_h, o:o + 32], cv[:, 4 * grp + j, rows_h], PT_s[:, u, 32 * j:32 * j + 32],
                                          start=False, stop=True, skip_group_check=True)
            mm.then_inc(pe_done, pe.tick(here, "o"))

            with nc.tensor.Fori(1, 3) as j:
                B = Blocks(GB, 2, j)
                for m in range(2):
                    for g in range(SLOTS):
                        t.wait_ge(act_done, act.at(("gb", j - 1), f"g{3 * m + g}") - SLOTS)
                        slot(B(m), g)
            gb = Blocks(GB, 2, 3)
            for g in range(SLOTS):
                t.wait_ge(act_done, act.at(("gb", 1), f"g{3 + g}"))
                slot(gb(0), g)
            t.wait_ge(act_done, act.at(("gb_l", 0), "g2"))
            slots(gb(1), xn_h, xn_l, tile_read=gb_tile_read)

            pb = Blocks(PB, 2, 0)
            t.wait_ge(act_done, act.at(("gb_l", 0), "g5"))
            slots(pb(0), xn_h, xn_l, split="gb_l")
            for g in range(SLOTS):
                t.wait_ge(dve_done, dve.at(("pb", 0), f"g{g}"))
                slot(pb(1), g)
            with nc.tensor.Fori(1, 3) as j:
                B = Blocks(PB, 2, j)
                for m in range(2):
                    for g in range(SLOTS):
                        t.wait_ge(dve_done, dve.at(("pb", j), f"g{3 * m + g}") - 2 * SLOTS)
                        slot(B(m), g)
            pb = Blocks(PB, 2, 3)
            for g in range(SLOTS):
                t.wait_ge(dve_done, dve.at(("pb", 2), f"g{3 + g}"))
                slot(pb(0), g)
            t.wait_ge(dve_done, dve.at(("pb_l", 0), "g2"))
            slots(pb(1), xn_h, xn_l, tile_read=pb_tile_read)
            here = ("out", 0)

            def token_tile(n, m, kt):
                r = tile_rows(n)
                cols = slice(n * P, n * P + r)
                passes = ((xn_h, 0), (xn_h, 1), (xn_l, 0))
                for i, (x, lo) in enumerate(passes):
                    mm = nc.tensor.matmul(bank_of(n, m)[0:r, :], x[:, kt, cols], wo_rhs(m, lo, kt),
                                          start=(kt == 0 and i == 0), stop=(kt == KT - 1 and i == 2))
                if kt == KT - 1:
                    mm.then_inc(pe_done, pe.tick(here, f"{'ab'[m]}{n}"))

            t.wait_ge(wo_lo_ready, 6)
            for kt in range(KT):
                t.wait_ge(dve_done, dve.at(("pb_l", 0), f"l{kt}"))
                for n in range(4):
                    token_tile(n, 0, kt)
            t.wait_ge(wo_lo_ready, 8)
            for n in range(4):
                for kt in range(KT):
                    token_tile(n, 1, kt)
            for n in range(4, NC + 1):
                for m in range(2):
                    t.wait_ge(dve_done, dve.at(here, f"y{'ab'[m]}{n - 4}"))
                    for kt in range(KT):
                        token_tile(n, m, kt)

        @block.vector
        def _(v):
            pr = ("pro", 0)
            tt = nc.vector.tensor_tensor
            v.wait_ge(pe_done, pe.at(pr, "par"))
            v.tensor_copy(par[:, 0:17], ps_e[:, 0:17]).then_inc(dve_done, dve.tick(pr, "par"))
            v.wait_ge(dve_done, dve.at(pr, "par"))
            tt(lbt[:, 2, :], par[:, 0:8], par[:, 8:16], ALU.max).then_inc(dve_done, dve.tick(pr, "lbm"))
            v.wait_ge(dve_done, dve.at(pr, "lbm"))
            tt(lbt[:, 0, :], par[:, 0:8], lbt[:, 2, :], ALU.subtract).then_inc(dve_done, dve.tick(pr, "lbd0"))
            tt(lbt[:, 1, :], par[:, 8:16], lbt[:, 2, :], ALU.subtract).then_inc(dve_done, dve.tick(pr, "lbd1"))
            v.wait_ge(act_done, act.at(pr, "lb1"))
            tt(lbt[:, 2, :], lbt[:, 0, :], lbt[:, 1, :], ALU.add).then_inc(dve_done, dve.tick(pr, "lbs"))
            v.wait_ge(dve_done, dve.at(pr, "lbs"))
            v.reciprocal(lbt[:, 2, :], lbt[:, 2, :]).then_inc(dve_done, dve.tick(pr, "lbr"))
            v.wait_ge(dve_done, dve.at(pr, "lbr"))
            tt(lb[:], lbt[:, 0, :], lbt[:, 2, :], ALU.mult).then_inc(dve_done, dve.tick(pr, "lb"))
            v.wait_ge(dve_done, dve.at(pr, "lb"))
            v.tensor_scalar(oml[:], lb[:], -1.0, 1.0, ALU.mult, ALU.add).then_inc(dve_done, dve.tick(pr, "oml"))
            v.tensor_scalar(noml[:], lb[:], 1.0, -1.0, ALU.mult, ALU.add).then_inc(dve_done, dve.tick(pr, "noml"))
            v.tensor_scalar(mean_m[:], ident[:], 0.0, 1.0 / P, ALU.mult, ALU.add).then_inc(dve_done, dve.tick(pr, "mean"))
            v.wait_ge(g_loaded, 16)
            for t in range(NC + 2):
                if t <= NC:
                    r = tile_rows(t)
                    v.wait_ge(act_done, act.at(pr, f"rstd{t}"))
                    if t >= 3:
                        v.wait_ge(pe_done, pe.at(pr, f"xb{t - 3}"))
                    v.scalar_tensor_tensor(out=x_n[t % 3][0:r, :], in0=x_t[t][0:r, :], scalar=rstd[0:r, 1, t:t + 1], in1=g_row[0:r, :],
                                           op0=ALU.mult, op1=ALU.mult).then_inc(dve_done, dve.tick(pr, f"xn{t}"))
                if t >= 1:
                    u = t - 1
                    for n, (bank, s) in enumerate(turn_banks(u)):
                        v.wait_ge(act_done, act.at(pr, f"hi_{s}{u}"))
                        at = (slice(None), slice(4 * n, 4 * n + 4), slice(u * P, u * P + tile_rows(u)))
                        tt(xn_l[at], bank[:].rearrange("p (k t) -> p k t", k=4)[:, :, 0:tile_rows(u)], xn_h[at].bitcast(F32),
                           ALU.subtract).then_inc(dve_done, dve.tick(pr, f"lo_{s}{u}"))
            v.wait_ge(pe_done, pe.at(pr, f"xb{NC}"))
            v.memset(att[:], 0.0).then_inc(dve_done, dve.tick(pr, "att0"))
            v.memset(att_s[:], 0.0).then_inc(dve_done, dve.tick(pr, "atts0"))
            for h in range(2):
                v.memset(kT[(1 - h) * HD:(2 - h) * HD, h, :], 0.0).then_inc(dve_done, dve.tick(pr, f"zkT{h}"))
            v.memset(reset[:], 1.0).then_inc(dve_done, dve.tick(pr, "reset"))
            v.wait_ge(dve_done, dve.at(pr, "reset"))
            v.memset(reset[:, 0:SEQ:P], 0.0).then_inc(dve_done, dve.tick(pr, "reset_p"))
            v.memset(reset[:, SEQ:T:DEC], 0.0).then_inc(dve_done, dve.tick(pr, "reset_s"))

            def gated(where, name, g, out):
                v.wait_ge(act_done, act.at(where, f"{'sigq' if name == 'q' else 'sigz'}{g}"))
                tt(out[:, span(g)], out[:, span(g)], pj[g][:, 0:W], ALU.mult).then_inc(dve_done, dve.tick(where, f"{name}{g}"))

            def rest_tile(where, n, src, hi, lo):
                v.wait_ge(act_done, act.at(where, f"h{n}"))
                tt(lo[:, n, :], src[:, n, :], hi[:, n, :].bitcast(F32), ALU.subtract).then_inc(dve_done, dve.tick(where, f"l{n}"))

            def exponents_of(now, i):
                def need(steps, sem_, name):
                    v.wait_ge(sem_, steps.at(now, name))

                def done(name):
                    return dve.tick(now, name)

                need(act, act_done, "lnf")
                v.tensor_scalar(k[:], k[:], noml[:, bass.ds(i, 1)], oml[:, bass.ds(i, 1)], ALU.mult, ALU.add).then_inc(dve_done, done("kf"))
                if now[0] == "pro":
                    v.wait_ge(dve_done, dve.at(pr, "reset_s"))
                v.tensor_tensor_scan(b[:], reset[:], b[:], 0.0, ALU.mult, ALU.add).then_inc(dve_done, done("scan"))
                need(dve, dve_done, "scan")
                bc = chunks(b[:, 0:SEQ])
                bs = b[:, SEQ:T].rearrange("p (b t) -> p b t", b=NB)
                tt(chunks(kD[:, 0:SEQ]), bc[:, :, P - 1:P].to_broadcast([P, NC, P]), bc, ALU.subtract).then_inc(dve_done, done("kDa"))
                tt(kD[:, SEQ:T].rearrange("p (b t) -> p b t", b=NB), bs[:, :, DEC - 1:DEC].to_broadcast([P, NB, DEC]), bs, ALU.subtract).then_inc(dve_done, done("kDs"))
                for h, d in ((64, d64), (32, d32)):
                    n = SEQ // (2 * h)
                    bh = b[:, 0:SEQ].rearrange("p (c s t) -> p c s t", s=2, t=h)
                    mid = bh[:, :, 0, h - 1:h].to_broadcast([P, n, h])
                    tt(d[:, :, 1, :], bh[:, :, 1, :], mid, ALU.subtract).then_inc(dve_done, done(f"a{h}q"))
                    tt(d[:, :, 0, :], mid, bh[:, :, 0, :], ALU.subtract).then_inc(dve_done, done(f"a{h}k"))
                bd = b[:, 0:SEQ].rearrange("p (c t) -> p c t", t=32)
                tt(cs[:, 0:32].rearrange("p (c o) -> p c o", o=1), bd[:, :, 0:1], bd[:, :, 31:32], ALU.add).then_inc(dve_done, done("cs"))
                tt(cs[:, 32:40].rearrange("p (c o) -> p c o", o=1), bs[:, :, 0:1], bs[:, :, DEC - 1:DEC], ALU.add).then_inc(dve_done, done("css"))
                need(dve, dve_done, "css")
                v.scalar_tensor_tensor(out=dk[:, 0:SEQ].rearrange("p (c t) -> p c t", t=32), in0=cs[:, 0:32].rearrange("p (c o) -> p c o", o=1).to_broadcast([P, 32, 32]),
                                       scalar=0.5, in1=bd, op0=ALU.mult, op1=ALU.subtract).then_inc(dve_done, done("xa"))
                v.scalar_tensor_tensor(out=dk[:, SEQ:T].rearrange("p (c t) -> p c t", t=DEC), in0=cs[:, 32:40].rearrange("p (c o) -> p c o", o=1).to_broadcast([P, NB, DEC]),
                                       scalar=0.5, in1=bs, op0=ALU.mult, op1=ALU.subtract).then_inc(dve_done, done("xas"))
                need(dve, dve_done, "xas")
                v.tensor_scalar(dk[:], dk[:], CLAMP, -CLAMP, ALU.min, ALU.max).then_inc(dve_done, done("xc"))

            exponents_of(pr, 0)
            for g in range(SLOTS):
                gated(pr, "q", g, q)
            for g in range(SLOTS):
                gated(pr, "z", g, zs)

            def head(i):
                now = now_of(i)
                prev = prev_of(i)
                last = is_last(i)

                def need(steps, sem_, name):
                    v.wait_ge(sem_, steps.at(now, name))

                def done(name):
                    return dve.tick(now, name)

                if not is_first(i):
                    need(act, act_done, "rx")
                    tt(ha[:, bass.ds(i - 1, 1), :], ha[:, bass.ds(i - 1, 1), :], rs[:].rearrange("p (o t) -> p o t", o=1), ALU.mult).then_inc(dve_done, done("ha"))
                v.wait_ge(dve_done, dve.at(prev, "q2"))
                need(act, act_done, "xkD")
                tt(kD[:], kD[:], k[:], ALU.mult).then_inc(dve_done, done("kD"))
                for h, d in ((64, d64), (32, d32)):
                    need(act, act_done, f"x{h}")
                    tt(d[:, :, 1, :], d[:, :, 1, :], q[:, 0:SEQ].rearrange("p (c s t) -> p c s t", s=2, t=h)[:, :, 1, :], ALU.mult).then_inc(dve_done, done(f"m{h}q"))
                    tt(d[:, :, 0, :], d[:, :, 0, :], k[:, 0:SEQ].rearrange("p (c s t) -> p c s t", s=2, t=h)[:, :, 0, :], ALU.mult).then_inc(dve_done, done(f"m{h}k"))
                need(act, act_done, "xdk")
                tt(dq[:], dq[:], q[:], ALU.mult).then_inc(dve_done, done("dqm"))
                tt(dk[:], dk[:], k[:], ALU.mult).then_inc(dve_done, done("dkm"))
                need(act, act_done, "xqI")
                tt(qI[:], qI[:], q[:], ALU.mult).then_inc(dve_done, done("qIm"))
                for n, bank in enumerate((ps_c, ps_d)):
                    need(pe, pe_done, f"kt{n}")
                    v.tensor_copy(k_tok[:, 4 * n:4 * n + 4, :], bank[:].rearrange("p (c v) -> p c v", c=4)).then_inc(dve_done, done(f"kt{n}"))
                need(pe, pe_done, "kts")
                v.tensor_copy(k_tok[0:NS, NC, :], ps_e[0:NS, P:2 * P]).then_inc(dve_done, done("kts"))
                need(dve, dve_done, "kts")
                v.tensor_copy(k3[0:NS, :], k_tok[0:NS, NC, :]).then_inc(dve_done, done("k3_hi"))
                v.tensor_copy(k3[NS:2 * NS, :], k_tok[0:NS, NC, :]).then_inc(dve_done, done("k3_hi2"))
                need(dve, dve_done, "k3_hi")
                tt(k3[2 * NS:3 * NS, :], k_tok[0:NS, NC, :], k3[0:NS, :].bitcast(F32), ALU.subtract).then_inc(dve_done, done("k3_lo"))
                for c in range(NC):
                    u = (ps_c, ps_d)[c // 4][:, (c % 4) * P:(c % 4 + 1) * P]
                    if c % 4 == 0:
                        need(pe, pe_done, f"u{c // 4}")
                    if c == 0:
                        v.tensor_copy(S[:, 0, :], u).then_inc(dve_done, done("s1"))
                        continue
                    need(dve, dve_done, f"s{c}")
                    if c == NC - 1:
                        need(pe, pe_done, "ps")
                    if c == NC - 1 and not is_first(i):
                        v.wait_ge(sp_stored, i * 16)
                    v.scalar_tensor_tensor(out=S[:, c, :], in0=S[:, c - 1, :], scalar=E[:, c:c + 1], in1=u,
                                           op0=ALU.mult, op1=ALU.add).then_inc(dve_done, done(f"s{c + 1}"))
                if is_first(i):
                    v.wait_ge(masks_loaded, 48)
                for n, bank in enumerate((ps_a, ps_b)):
                    v.copy_predicated(att[:, 4 * n:4 * n + 4, :], causal[:].rearrange("p (o t) -> p o t", o=1).to_broadcast([P, 4, P]),
                                      bank[:].rearrange("p (c t) -> p c t", c=4)).then_inc(dve_done, done(f"att{n}"))
                v.copy_predicated(att_s[:], causal_s[:], ps_e[0:NS, 256:256 + NS]).then_inc(dve_done, done("atts"))

                def gate(name, squared, bank, cols, src):
                    need(act, act_done, squared)
                    v.scalar_tensor_tensor(out=ha[:, bass.ds(i, 1), cols], in0=bank[:, src].rearrange("p (o t) -> p o t", o=1), scalar=par[:, 16:17],
                                           in1=zs[:, cols].rearrange("p (o t) -> p o t", o=1), op0=ALU.mult, op1=ALU.mult).then_inc(dve_done, done(name))

                if not last:
                    exponents_of(now, i + 1)
                    gated(now, "q", 0, q)
                gate("gate0", "sh0", ps_e, half(0), slice(0, 512))
                gate("gate1", "sh1", ps_c, half(1), slice(0, 512))
                gate("gates", "shs", ps_d, slice(SEQ, T), slice(0, NS))
                for n in "01s":
                    tt(sq_l[:, part[n]], vT[:, part[n]], sq_h[:, part[n]].bitcast(F32), ALU.subtract).then_inc(dve_done, done(f"sl{n}"))
                if not last:
                    gated(now, "q", 1, q)
                need(pool, pool_done, "s0e")
                for n, bank in enumerate((ps_a, ps_b)):
                    need(pe, pe_done, f"us{n}")
                    tt(s0[:, 4 * n:4 * n + 4, :], s0[:, 4 * n:4 * n + 4, :], bank[:].rearrange("p (b v) -> p b v", b=4), ALU.add).then_inc(dve_done, done(f"so{n}"))
                if last:
                    need(pe, pe_done, "us1")
                    need(dve, dve_done, "so1")
                    for n in range(KT - 1):
                        if n == 4:
                            v.wait_ge(sp_stored, 16 * HEADS)
                            v.wait_ge(s0_stored, 16 * HEADS)
                        if n == 5:
                            need(act, act_done, "fx")
                            tt(ha[:, i, :], ha[:, i, :], rs[:], ALU.mult).then_inc(dve_done, done("hal"))
                        rest_tile(now, n, ha, hl_h, hl_l)
                    rest_tile(now, KT - 1, ha, hl_h, hl_l)
                    return
                gated(now, "q", 2, q)
                for g in range(SLOTS):
                    gated(now, "z", g, zs)

            head(0)
            with nc.vector.Fori(1, HEADS - 1) as i:
                head(i)
            head(HEADS - 1)

            one = lambda a: a.rearrange("p (o t) -> p o t", o=1)

            def merge_a(B, j):
                gate = ("last", 0) if isinstance(j, int) else ("pa", j - 1)
                for g in range(SLOTS):
                    v.wait_ge(act_done, act.at(gate, f"sg{g}"))
                    v.wait_ge(slot_done, B(1)[0] * 3 + (g + 1))
                    tt(mg[:, bass.ds(j, 1), span(g)], one(sg[:, span(g)]), one(pj[g][:, 0:W]), ALU.mult).then_inc(dve_done, dve.tick(("pa", j), f"m{g}"))

            merge_a(Blocks(GA, 2, 0), 0)
            with nc.vector.Fori(1, HEADS) as j:
                merge_a(Blocks(GA, 2, j), j)

            here = ("kv", 0)
            v.wait_ge(slopes_loaded, 64)
            for h in range(2):
                v.tensor_tensor_reduce(out=bias[:, h, 0:8], in0=sinks[:, 8 * h:8 * h + 8], in1=pick[:], scale=1.0, scalar=0.0,
                                       op0=ALU.mult, op1=ALU.add, accum_out=sinks_s[:, h:h + 1]).then_inc(dve_done, dve.tick(here, f"sel{h}"))
            v.wait_ge(pe_done, pe.at(here, "vt1"))
            v.tensor_copy(v_tk[:, 4:8, :], ps_b[:].rearrange("p (c v) -> p c v", c=4)).then_inc(dve_done, dve.tick(here, "vt1"))
            v.wait_ge(dve_done, dve.at(here, "sel1"))
            for g in range(SLOTS):
                gated(here, "z", g, zb)

            def negate(now, k, new, old, sink, scores_next=len(quarters)):
                v.tensor_scalar(new(0), old(0), sink(0), -1.0, ALU.max, ALU.mult).then_inc(dve_done, dve.tick(now, f"nm0_{k}"))
                if scores_next < len(quarters):
                    v.wait_ge(pe_done, pe.at(now, f"s{2 * scores_next + 1}"))
                v.tensor_scalar(new(1), old(1), sink(1), -1.0, ALU.max, ALU.mult).then_inc(dve_done, dve.tick(now, f"nm1_{k}"))

            def normalise(now, k, st, first, last, target, keys):
                v.wait_ge(act_done, act.at(now, f"p{last - 1}"))
                tt(st[:, 3, first:last], st[:, 3, first:last], st[:, 2, first:last], ALU.add).then_inc(dve_done, dve.tick(now, f"dn{k}"))
                v.wait_ge(dve_done, dve.at(now, f"dn{k}"))
                v.reciprocal(st[:, 4, first:last], st[:, 3, first:last]).then_inc(dve_done, dve.tick(now, f"rd{k}"))
                v.wait_ge(dve_done, dve.at(now, f"rd{k}"))
                for u in range(first, last):
                    v.tensor_scalar(target[:, u, keys(u)], target[:, u, keys(u)], st[:, 4, u:u + 1], None, ALU.mult).then_inc(dve_done, dve.tick(now, f"n{u}"))

            def pair(m):
                now = pair_of(m)
                last = is_last(m)
                keys = lambda u: slice(P if u < 2 else 0, 2 * P)
                for h in range(2):
                    v.tensor_scalar(bias[:, h, :], dist[:], slopes[:, bass.ds(m + 8 * h, 1)], None, ALU.mult).then_inc(dve_done, dve.tick(now, f"b{h}"))
                def biased(u):
                    n, h = u // 2, u % 2
                    (bank, o), lo = score_bank(n, h), P if n == 0 else 0
                    v.tensor_tensor_reduce(out=scores[:, u, lo:2 * P], in0=bank[:, o + lo:o + 2 * P], in1=bias[:, h, lo:2 * P],
                                           scale=1.0, scalar=-3e38, op0=ALU.add, op1=ALU.max,
                                           accum_out=stat[:, 0, u:u + 1]).then_inc(dve_done, dve.tick(now, f"t{u}"))

                v.wait_ge(pe_done, pe.at(now, "s1"))
                v.tensor_copy(sink_m[:].rearrange("p (h m) -> p h m", h=2), sinks[:].rearrange("p (h m) -> p h m", h=2)[:, :, bass.ds(m, 1)])\
                 .then_inc(dve_done, dve.tick(now, "sk"))
                v.wait_ge(dve_done, dve.at(now, "b1"))
                v.tensor_copy(q_s[:, :, bass.ds(m, 1), :], qT[:, SEQ:T].rearrange("p (b o t) -> p b o t", b=NB, o=1)).then_inc(dve_done, dve.tick(now, "qs"))
                for k in quarters:
                    for u in range(QU * k, QU * (k + 1)):
                        biased(u)
                    v.wait_ge(dve_done, dve.at(now, f"t{QU * k + QU - 1}"))
                    negate(now, k, lambda h: by_head(stat[:, 1, :], k)[:, h, :], lambda h: by_head(stat[:, 0, :], k)[:, h, :],
                           lambda h: sink_m[:, h:h + 1], scores_next=k + 1)
                v.tensor_copy(z_s[:, bass.ds(m, 1), :], one(zb[:, SEQ:T])).then_inc(dve_done, dve.tick(now, "zs"))
                for k in quarters:
                    normalise(now, k, stat, QU * k, QU * (k + 1), scores, keys)
                for n in range(1, NC, 2):
                    v.wait_ge(pe_done, pe.at(now, f"t{n}"))
                    if n >= 3:
                        v.wait_ge(pe_done, pe.at(now, f"o{n - 3}"))
                    src = (ps_a, ps_b, ps_c)[n % 3]
                    v.tensor_copy(PT[:, n % 3, :, :].rearrange("p a q -> p (a q)"), src[:]).then_inc(dve_done, dve.tick(now, f"pt{n}"))
                for n, bank in enumerate((ps_d, ps_e)):
                    v.wait_ge(pe_done, pe.at(now, f"o{4 * n + 3}"))
                    tt(hb[:, bass.ds(m, 1), half(n)], one(bank[:]), one(zb[:, half(n)]), ALU.mult).then_inc(dve_done, dve.tick(now, f"h{n}"))
                if not last:
                    for g in range(SLOTS):
                        gated(now, "z", g, zb)

            with nc.vector.Fori(0, HEADS - 1) as m:
                pair(m)
            pair(HEADS - 1)

            here = ("swa_s", 0)
            v.wait_ge(pe_done, pe.at(here, "ct1"))
            v.tensor_copy(ckT[:, 4:8, :], ps_b[:].rearrange("p (c v) -> p c v", c=4)).then_inc(dve_done, dve.tick(here, "ct1"))
            v.wait_ge(bias_s_loaded, 16)
            for u in range(4):
                bank, o = (ps_c, ps_d)[u // 2], (u % 2) * 2 * P
                v.wait_ge(pe_done, pe.at(here, f"s{u | 1}"))
                v.tensor_tensor_reduce(out=sc_s[:, u, :], in0=bank[:, o:o + P + NS], in1=bias_s[:, u, :], scale=1.0, scalar=-3e38,
                                       op0=ALU.add, op1=ALU.max, accum_out=stat_s[:, 0, u:u + 1]).then_inc(dve_done, dve.tick(here, f"t{u}"))
            v.wait_ge(dve_done, dve.at(here, "t3"))
            negate(here, 0, lambda h: stat_s[:, 1, 2 * h:2 * h + 2], lambda h: stat_s[:, 0, 2 * h:2 * h + 2], lambda h: sinks_s[:, h:h + 1])
            normalise(here, 0, stat_s, 0, 4, sc_s, lambda u: slice(0, P + NS))
            v.wait_ge(pe_done, pe.at(here, "pn"))
            v.tensor_copy(PT_n.rearrange("p a q -> p (a q)"), ps_b[0:NS, :]).then_inc(dve_done, dve.tick(here, "pn"))
            v.wait_ge(pe_done, pe.at(here, "o"))
            for_g = lambda a: a.rearrange("p g (b t) -> p g b t", t=DEC)
            tt(for_g(hb[:, :, SEQ:T]), ps_e[:, 0:2 * P].rearrange("p (b g t) -> p g b t", b=NB, g=HEADS), for_g(z_s[:]), ALU.mult).then_inc(dve_done, dve.tick(here, "h"))

            for n in range(KT):
                rest_tile(("gb_l", 0), n, hb, xn_h, xn_l)

            def merge_b(B, now, j, m):
                for g in range(SLOTS):
                    s_, at = 3 * m + g, bass.ds(j * 2 + m, 1)
                    v.wait_ge(slot_done, B(m)[0] * 3 + (g + 1))
                    tt(sgb[:, at, span(g)], sgb[:, at, span(g)], one(pj[g][:, 0:W]), ALU.mult).then_inc(dve_done, dve.tick(now, f"g{s_}"))
                    v.wait_ge(dve_done, dve.at(now, f"g{s_}"))
                    tt(mg[:, at, span(g)], mg[:, at, span(g)], sgb[:, at, span(g)], ALU.add).then_inc(dve_done, dve.tick(now, f"m{s_}"))

            with nc.vector.Fori(0, 3) as j:
                for m in range(2):
                    merge_b(Blocks(PB, 2, j), ("pb", j), j, m)
            now = ("pb_l", 0)
            merge_b(Blocks(PB, 2, 3), now, 3, 0)
            for n in range(KT - 1):
                rest_tile(now, n, mg, xn_h, xn_l)
            merge_b(Blocks(PB, 2, 3), now, 3, 1)
            rest_tile(now, KT - 1, mg, xn_h, xn_l)
            here = ("out", 0)
            v.wait_ge(g_fin_loaded, 16)
            for t in range(NC + 1):
                r = P if t < NC else NS
                v.wait_ge(xo_loaded[t % 3], 16 * (t // 3 + 1))
                if t >= 3:
                    v.wait_ge(y_stored[t % 3], 16 * (t // 3))
                for m in range(2):
                    v.wait_ge(pe_done, pe.at(here, f"{'ab'[m]}{t}"))
                    tt(y_o[t % 3][0:r, half(m)], bank_of(t, m)[0:r, :], x_o[t % 3][0:r, half(m)], ALU.add).then_inc(dve_done, dve.tick(here, f"y{'ab'[m]}{t}"))
                v.wait_ge(act_done, act.at(here, f"rs{t}"))
                v.scalar_tensor_tensor(out=y_o[t % 3][0:r, :], in0=y_o[t % 3][0:r, :], scalar=rstd[0:r, 1, t:t + 1], in1=g_fin[0:r, :],
                                       op0=ALU.mult, op1=ALU.mult).then_inc(dve_done, dve.tick(here, f"yn{t}"))


_INS = ["x_prompt", "x_sample", "state_hgrn", "cache_k", "cache_v", "norm_in", "w_in", "lb_logits", "a_gnorm",
        "b_sinks", "w_pa", "w_pb", "w_out", "norm_final"]
_CONSTS = ["c_ident", "c_causal", "c_causal_s", "c_batch", "c_dist", "c_slopes", "c_bias_s"]
_OUTS = [(1, 1024, 1024), (8, 4, 1024), (1, 1, 8, 128, 128), (1, 1, 128, 2, 64), (1, 1, 128, 2, 64),
         (1, 8, 8, 128, 128), (1, 8, 128, 2, 64), (1, 8, 128, 2, 64)]


def shape_constants():
    import numpy as np

    s, t = np.arange(P)[:, None], np.arange(P)[None, :]
    ss, st = np.arange(NS)[:, None], np.arange(NS)[None, :]
    dist = np.arange(P)[:, None] - (np.arange(2 * P)[None, :] - P)
    slopes = np.float32(2.0) ** (np.float32(-8.0) * np.arange(1, QH + 1, dtype=np.float32) / np.float32(QH))
    row = np.arange(P)
    bias_s = np.zeros((P, 4, P + NS), np.float32)
    for u in range(4):
        slope = slopes[8 * (u // 2) + row // DEC % 8][:, None]
        batch, query = (4 * (u % 2) + row // 32)[:, None], (row % DEC)[:, None]
        old, new = query + P - np.arange(P)[None, :], query - np.arange(NS)[None, :] % DEC
        bias_s[:, u, 0:P] = np.where(old < P, -slope * old, -1e30)
        bias_s[:, u, P:] = np.where((new >= 0) & (np.arange(NS)[None, :] // DEC == batch), -slope * new, -1e30)
    return {
        "c_ident": np.eye(P, dtype=np.float32),
        "c_causal": (s <= t).astype(np.int32),
        "c_causal_s": ((ss <= st) & (ss // DEC == st // DEC)).astype(np.int32),
        "c_dist": np.where((dist >= 0) & (dist < P), -dist, OFFSET).astype(np.float32),
        "c_slopes": np.concatenate([np.broadcast_to(slopes, (P, QH)), (row // DEC % 8)[:, None] == np.arange(8)], 1).astype(np.float32),
        "c_bias_s": bias_s,
        "c_batch": np.tile(ss // DEC == np.arange(NB)[None, :], (3, 1)).astype(np.float32),
    }


def kernel(**inputs):
    import numpy as _np
    import concourse.bacc as _bacc
    from concourse import mybir as _mybir
    from concourse.bass_utils import run_bass_kernel_spmd as _run

    nc = _bacc.Bacc("TRN2", target_bir_lowering=False, num_devices=1)
    constants = shape_constants()
    arrays, args = {}, []
    for name, a in [(n, inputs[n]) for n in _INS] + [(n, constants[n]) for n in _CONSTS]:
        a = _np.ascontiguousarray(a)
        arrays[f"in_{name}_dram"] = a
        args.append(nc.dram_tensor(f"in_{name}_dram", a.shape, _mybir.dt.from_np(a.dtype), kind="ExternalInput").ap())
    for i, shape in enumerate(_OUTS):
        args.append(nc.dram_tensor(f"out_{i}_dram", shape, _mybir.dt.float32, kind="ExternalOutput").ap())
    hybrid_step(nc, *args)
    r = _run(nc, [arrays], core_ids=[0])
    return tuple(r.results[0][f"out_{i}_dram"] for i in range(len(_OUTS)))
```
